# Optimizing a Trainium2 kernel written in Bass

```python
import math
import jax, jax.numpy as jnp
from jax import lax
import numpy as np

D_MODEL = 1024
BATCH = 1
SEQ = 256
DEPTH = 1

GRID_W = 64
CTX_LEN = 256

N_MOD = 6
NORM_EPS = 1e-6

MIX_WIDTH = D_MODEL
RET_HEADS = 4
RET_WIDTH = MIX_WIDTH // 2
RET_DV = RET_WIDTH // RET_HEADS
RET_DK = RET_DV // 2
RET_CHUNK = 128
DIFF_HEADS = 4
DIFF_WIDTH = MIX_WIDTH - RET_WIDTH
DIFF_DV = DIFF_WIDTH // DIFF_HEADS
DIFF_D = DIFF_DV // 2
Q_BLOCK = 128
ROPE_DIM = RET_DK
ROPE_BASE = 10000.0

RET_QK_COLS = RET_HEADS * RET_DK
IN_SPLITS = (RET_QK_COLS, 2 * RET_QK_COLS, 2 * RET_QK_COLS + RET_WIDTH, 2 * RET_QK_COLS + 2 * RET_WIDTH, 2 * RET_QK_COLS + 2 * RET_WIDTH + DIFF_WIDTH, 2 * RET_QK_COLS + 2 * RET_WIDTH + 2 * DIFF_WIDTH)
IN_COLS = 2 * RET_QK_COLS + 2 * RET_WIDTH + 3 * DIFF_WIDTH

PEER_HEADS = 8
PEER_NKEYS = 128
PEER_N_EXPERTS = PEER_NKEYS * PEER_NKEYS
PEER_QDIM = 256
PEER_HALF = PEER_QDIM // 2
PEER_TOPK = 16
PEER_BLOCK = 128


def rms_norm(x, g, eps=NORM_EPS):
    xf = x.astype(jnp.float32)
    y = xf * lax.rsqrt(jnp.mean(xf * xf, axis=-1, keepdims=True) + eps)
    return (y * g.astype(jnp.float32)).astype(x.dtype)

def modulate(x, g, shift, scale):
    return rms_norm(x, g) * (1.0 + scale) + shift

def adaln_params(cond, w_mod, b_mod):
    mod = jax.nn.silu(cond) @ w_mod + b_mod
    return mod.reshape(cond.shape[0], N_MOD, 1, cond.shape[-1])

def heads(t, n_heads):
    b, l, _ = t.shape
    return t.reshape(b, l, n_heads, -1).transpose(0, 2, 1, 3)

def merge_heads(t):
    b, h, l, e = t.shape
    return t.transpose(0, 2, 1, 3).reshape(b, l, h * e)

def axial_rope_tables(rows, head_dim, dtype):
    quarter = head_dim // 4
    freqs = ROPE_BASE ** (-jnp.arange(quarter, dtype=jnp.float32) / quarter)
    row = jnp.repeat(jnp.arange(rows, dtype=jnp.float32), GRID_W)
    col = jnp.tile(jnp.arange(GRID_W, dtype=jnp.float32), rows)
    ar = row[:, None] * freqs
    ac = col[:, None] * freqs
    ang = jnp.concatenate([ar, ar, ac, ac], axis=-1)
    return jnp.cos(ang).astype(dtype), jnp.sin(ang).astype(dtype)

def apply_rope(x, cos, sin):
    quarter = x.shape[-1] // 4
    xr = x.reshape(x.shape[:-1] + (2, 2, quarter))
    rot = jnp.concatenate([-xr[..., 1:, :], xr[..., :1, :]], axis=-2).reshape(x.shape)
    return x * cos + rot * sin

def decayed_state(k, v, log_gamma):
    l = k.shape[2]
    dist = (l - 1 - jnp.arange(l)).astype(jnp.float32)
    w = jnp.exp(dist[None, :] * log_gamma[:, None]).astype(k.dtype)
    return jnp.einsum('bhjd,hj,bhje->bhde', k, w, v)

def retention_chunkwise(q, k, v, log_gamma, init_state, strict):
    b, h, l, dk = q.shape
    dv = v.shape[-1]
    n = l // RET_CHUNK
    C = RET_CHUNK
    qc = q.reshape(b, h, n, C, dk)
    kc = k.reshape(b, h, n, C, dk)
    vc = v.reshape(b, h, n, C, dv)
    idx = jnp.arange(C, dtype=jnp.float32)
    diff = idx[:, None] - idx[None, :]
    mask = (diff > 0) if strict else (diff >= 0)
    lg = log_gamma[:, None, None]
    intra_decay = jnp.where(mask, jnp.exp(jnp.where(mask, diff, 0.0) * lg), 0.0).astype(q.dtype)
    scores = jnp.einsum('bhnid,bhnjd->bhnij', qc, kc) * intra_decay[None, :, None]
    out = jnp.einsum('bhnij,bhnje->bhnie', scores, vc)
    k_w = jnp.exp((C - 1 - idx)[None, :] * log_gamma[:, None]).astype(q.dtype)
    local = jnp.einsum('bhnjd,hj,bhnje->bhnde', kc, k_w, vc)
    chunk_decay = jnp.exp(C * log_gamma).astype(q.dtype)[None, :, None, None]

    def step(r, s):
        return chunk_decay * r + s, r

    _, r_prev = lax.scan(step, init_state.astype(local.dtype), jnp.moveaxis(local, 2, 0))
    r_prev = jnp.moveaxis(r_prev, 0, 2)
    q_w = jnp.exp((idx + 1.0)[None, :] * log_gamma[:, None]).astype(q.dtype)
    out = out + jnp.einsum('bhnid,hi,bhnde->bhnie', qc, q_w, r_prev)
    return out.reshape(b, h, l, dv)

def bidirectional_retention(q, k, v, lg_f, lg_b, state_f, state_b):
    flip = lambda t: jnp.flip(t, axis=2)
    y_f = retention_chunkwise(q, k, v, lg_f, state_f, strict=False)
    y_b = flip(retention_chunkwise(flip(q), flip(k), flip(v), lg_b, state_b, strict=True))
    return y_f + y_b

def retention_group(rq, rk, rv, rg, crq, crk, crv, crg, decay_logit, norm_g, cos, sin, with_ctx_out):
    scale = RET_DK ** -0.5
    log_gamma = jax.nn.log_sigmoid(decay_logit.astype(jnp.float32))
    lg_f, lg_b = log_gamma[0], log_gamma[1]
    q = apply_rope(heads(rq, RET_HEADS), cos, sin)
    k = apply_rope(heads(rk, RET_HEADS), cos, sin) * scale
    v = heads(rv, RET_HEADS)
    kc = heads(crk, RET_HEADS) * scale
    vc = heads(crv, RET_HEADS)
    state_f = decayed_state(kc, vc, lg_f)
    state_b = decayed_state(jnp.flip(kc, axis=2), jnp.flip(vc, axis=2), lg_b)
    y = bidirectional_retention(q, k, v, lg_f, lg_b, state_f, state_b)
    g_norm = norm_g[:, None, :]
    out = merge_heads(rms_norm(y, g_norm)) * jax.nn.silu(rg)
    ctx_out = None
    if with_ctx_out:
        qc = heads(crq, RET_HEADS)
        zero = jnp.zeros(state_f.shape, state_f.dtype)
        yc = bidirectional_retention(qc, kc, vc, lg_f, lg_b, zero, zero)
        ctx_out = merge_heads(rms_norm(yc, g_norm)) * jax.nn.silu(crg)
    return out, ctx_out

def diff_softmax_attend(q, k, v, lam):
    s = jnp.einsum('bhpqd,bhpkd->bhpqk', q, k).astype(jnp.float32) * (DIFF_D ** -0.5)
    p = jax.nn.softmax(s, axis=-1)
    a = (p[:, :, 0] - lam * p[:, :, 1]).astype(v.dtype)
    return jnp.einsum('bhqk,bhke->bhqe', a, v)

def diff_attention_group(dq, dk, dv, cdq, cdk, cdv, qk_norm_g, lam_params, norm_g, lam_init, cos, sin, with_ctx_out):
    def qk_heads(t, g):
        b_, l_, _ = t.shape
        t = t.reshape(b_, l_, DIFF_HEADS, 2, DIFF_D).transpose(0, 2, 3, 1, 4)
        return rms_norm(t, g)

    q = apply_rope(qk_heads(dq, qk_norm_g[0]), cos, sin)
    k = apply_rope(qk_heads(dk, qk_norm_g[1]), cos, sin)
    v = heads(dv, DIFF_HEADS)
    kc = qk_heads(cdk, qk_norm_g[1])
    vc = heads(cdv, DIFF_HEADS)
    lp = lam_params.astype(jnp.float32)
    lam = jnp.exp(jnp.sum(lp[0] * lp[1])) - jnp.exp(jnp.sum(lp[2] * lp[3])) + lam_init
    keys = jnp.concatenate([kc, k], axis=3)
    vals = jnp.concatenate([vc, v], axis=2)
    b, h, _, l, d = q.shape
    nb = l // Q_BLOCK
    q_blocks = jnp.moveaxis(q.reshape(b, h, 2, nb, Q_BLOCK, d), 3, 0)
    y = lax.map(lambda qb: diff_softmax_attend(qb, keys, vals, lam), q_blocks)
    y = jnp.moveaxis(y, 0, 2).reshape(b, h, l, DIFF_DV)
    g_norm = norm_g[:, None, :]
    out = merge_heads(rms_norm(y, g_norm) * (1.0 - lam_init))
    ctx_out = None
    if with_ctx_out:
        qc = qk_heads(cdq, qk_norm_g[0])
        yc = diff_softmax_attend(qc, kc, vc, lam)
        ctx_out = merge_heads(rms_norm(yc, g_norm) * (1.0 - lam_init))
    return out, ctx_out

def peer_ffn(h, w_query, sub_keys, expert_u, expert_v):
    b, l, d = h.shape
    tokens = h.reshape(-1, PEER_BLOCK, d)

    def block_fn(hb):
        t = hb.shape[0]
        q = (hb @ w_query).reshape(t, PEER_HEADS, 2, PEER_HALF)
        s = jnp.einsum('thpc,hpnc->thpn', q, sub_keys).astype(jnp.float32)
        v1, i1 = lax.top_k(s[:, :, 0], PEER_TOPK)
        v2, i2 = lax.top_k(s[:, :, 1], PEER_TOPK)
        cand = (v1[..., :, None] + v2[..., None, :]).reshape(t, PEER_HEADS, PEER_TOPK * PEER_TOPK)
        cand_idx = (i1[..., :, None] * PEER_NKEYS + i2[..., None, :]).reshape(t, PEER_HEADS, PEER_TOPK * PEER_TOPK)
        best, pos = lax.top_k(cand, PEER_TOPK)
        experts = jnp.take_along_axis(cand_idx, pos, axis=-1)
        gate = jax.nn.softmax(best, axis=-1).astype(hb.dtype)
        u = expert_u[experts]
        vsel = expert_v[experts]
        act = jax.nn.gelu(jnp.einsum('thkd,td->thk', u, hb), approximate=False)
        return jnp.einsum('thk,thkd->td', gate * act, vsel)

    return lax.map(block_fn, tokens).reshape(b, l, d)

def first_inputs(seed: int = 0) -> dict:
    key = jax.random.key(seed)
    ks = jax.random.split(key, 20)
    nrm = lambda k, shape, s: jax.random.normal(k, shape, jnp.float32) * s
    L = DEPTH
    D = D_MODEL
    decay_init = jnp.asarray(np.log(2.0 ** (5 + np.arange(RET_HEADS)) - 1.0).astype(np.float32))
    return {
        "x": nrm(ks[0], (BATCH, SEQ, D), 1.0),
        "c": nrm(ks[1], (BATCH, D), 1.0),
        "ctx": nrm(ks[2], (BATCH, CTX_LEN, D), 1.0),
        "c_ctx": nrm(ks[3], (D,), 1.0),
        "w_mod": nrm(ks[4], (L, D, N_MOD * D), 0.5 * D ** -0.5),
        "b_mod": nrm(ks[5], (L, N_MOD * D), 0.02),
        "norm1_g": 1.0 + nrm(ks[6], (L, D), 0.02),
        "norm2_g": 1.0 + nrm(ks[7], (L, D), 0.02),
        "w_in": nrm(ks[8], (L, D, IN_COLS), D ** -0.5),
        "ret_decay_logit": decay_init[None, None, :] + nrm(ks[9], (L, 2, RET_HEADS), 0.1),
        "ret_norm_g": 1.0 + nrm(ks[10], (L, RET_HEADS, RET_DV), 0.02),
        "diff_qk_norm_g": 1.0 + nrm(ks[11], (L, 2, DIFF_D), 0.02),
        "diff_lambda": nrm(ks[12], (L, 4, DIFF_D), 0.1),
        "diff_norm_g": 1.0 + nrm(ks[13], (L, DIFF_HEADS, DIFF_DV), 0.02),
        "w_out": nrm(ks[14], (L, MIX_WIDTH, D), MIX_WIDTH ** -0.5),
        "peer_w_query": nrm(ks[15], (L, D, PEER_HEADS * PEER_QDIM), D ** -0.5),
        "peer_sub_keys": nrm(ks[16], (L, PEER_HEADS, 2, PEER_NKEYS, PEER_HALF), PEER_HALF ** -0.5),
        "peer_u": nrm(ks[17], (L, PEER_N_EXPERTS, D), D ** -0.5),
        "peer_v": nrm(ks[18], (L, PEER_N_EXPERTS, D), (PEER_HEADS * PEER_TOPK) ** -0.5),
    }

def first_block(x, c, ctx, c_ctx, w_mod, b_mod, norm1_g, norm2_g, w_in, ret_decay_logit, ret_norm_g, diff_qk_norm_g, diff_lambda, diff_norm_g, w_out, peer_w_query, peer_sub_keys, peer_u, peer_v):
    rows = x.shape[1] // GRID_W
    cos, sin = axial_rope_tables(rows, ROPE_DIM, x.dtype)
    for layer in range(DEPTH):
        last = layer == DEPTH - 1
        lam_init = 0.8 - 0.6 * math.exp(-0.3 * layer)
        mod = adaln_params(c, w_mod[layer], b_mod[layer])
        mod_c = adaln_params(c_ctx[None, :], w_mod[layer], b_mod[layer])
        h = modulate(x, norm1_g[layer], mod[:, 0], mod[:, 1])
        hc = modulate(ctx, norm1_g[layer], mod_c[:, 0], mod_c[:, 1])
        rq, rk, rv, rg, dq, dk, dv = jnp.split(h @ w_in[layer], IN_SPLITS, axis=-1)
        crq, crk, crv, crg, cdq, cdk, cdv = jnp.split(hc @ w_in[layer], IN_SPLITS, axis=-1)
        ret_lat, ret_ctx = retention_group(rq, rk, rv, rg, crq, crk, crv, crg, ret_decay_logit[layer], ret_norm_g[layer], cos, sin, not last)
        diff_lat, diff_ctx = diff_attention_group(dq, dk, dv, cdq, cdk, cdv, diff_qk_norm_g[layer], diff_lambda[layer], diff_norm_g[layer], lam_init, cos, sin, not last)
        x = x + mod[:, 2] * (jnp.concatenate([ret_lat, diff_lat], axis=-1) @ w_out[layer])
        h2 = modulate(x, norm2_g[layer], mod[:, 3], mod[:, 4])
        x = x + mod[:, 5] * peer_ffn(h2, peer_w_query[layer], peer_sub_keys[layer], peer_u[layer], peer_v[layer])
        if not last:
            ctx = ctx + mod_c[:, 2] * (jnp.concatenate([ret_ctx, diff_ctx], axis=-1) @ w_out[layer])
            hc2 = modulate(ctx, norm2_g[layer], mod_c[:, 3], mod_c[:, 4])
            ctx = ctx + mod_c[:, 5] * peer_ffn(hc2, peer_w_query[layer], peer_sub_keys[layer], peer_u[layer], peer_v[layer])
    return x


MIX_WIDTH_2 = D_MODEL
MOBA_HEAD_DIM = 64
MOBA_WIDTH = MIX_WIDTH_2 // 2
MOBA_HEADS = MOBA_WIDTH // MOBA_HEAD_DIM
MOBA_BLOCK = 256
MOBA_TOPK = 3
MOBA_Q_CHUNK = 64
GDN_HEAD_DIM = 128
GDN_WIDTH = MIX_WIDTH_2 - MOBA_WIDTH
GDN_HEADS = GDN_WIDTH // GDN_HEAD_DIM
GDN_CONV = 4
GDN_CHUNK = 64
N_GROUPS = 4
EXPERTS_PER_GROUP = 8
EXPERT_TOPK = 2
EXPERT_FF = D_MODEL // 4
RMS_EPS = 1e-6
IN_SPLITS_2 = (MOBA_WIDTH, MOBA_WIDTH, MOBA_WIDTH, 3 * GDN_WIDTH, GDN_WIDTH, GDN_HEADS, GDN_HEADS)
IN_PROJ_WIDTH = 3 * MOBA_WIDTH + 4 * GDN_WIDTH + 2 * GDN_HEADS


def rmsnorm(x, gain):
    x32 = x.astype(jnp.float32)
    y = x32 * lax.rsqrt(jnp.mean(x32 * x32, axis=-1, keepdims=True) + RMS_EPS)
    return (y * gain.astype(jnp.float32)).astype(x.dtype)

def l2norm(x):
    return x * lax.rsqrt(jnp.sum(x * x, axis=-1, keepdims=True) + 1e-6)

def moba_attention(q, k, v):
    B, S, H, Dh = q.shape
    nb = -(-S // MOBA_BLOCK)
    pad = nb * MOBA_BLOCK - S
    topk = min(MOBA_TOPK, nb)
    scale = Dh ** -0.5
    q = q.transpose(0, 2, 1, 3)
    kp = jnp.pad(k.transpose(0, 2, 1, 3), ((0, 0), (0, 0), (0, pad), (0, 0)))
    vp = jnp.pad(v.transpose(0, 2, 1, 3), ((0, 0), (0, 0), (0, pad), (0, 0)))
    kb = kp.reshape(B, H, nb, MOBA_BLOCK, Dh)
    vb = vp.reshape(B, H, nb, MOBA_BLOCK, Dh)
    k_mean = jnp.mean(kb.astype(jnp.float32), axis=3)
    b_idx = jnp.arange(B)[:, None, None, None]
    h_idx = jnp.arange(H)[None, :, None, None]
    blk_ids = jnp.arange(nb)
    n_chunks = S // MOBA_Q_CHUNK

    def chunk(c):
        start = c * MOBA_Q_CHUNK
        qc = lax.dynamic_slice_in_dim(q, start, MOBA_Q_CHUNK, axis=2)
        qpos = start + jnp.arange(MOBA_Q_CHUNK)
        own = start // MOBA_BLOCK
        gate = jnp.einsum('bhqd,bhnd->bhqn', qc.astype(jnp.float32), k_mean)
        gate = jnp.where(blk_ids < own, gate, -jnp.inf)
        _, gidx = lax.top_k(gate, topk)
        sel_ok = jnp.arange(topk) < own
        k_sel = kb[b_idx, h_idx, gidx]
        v_sel = vb[b_idx, h_idx, gidx]
        s_sel = jnp.einsum('bhqd,bhqkld->bhqkl', qc, k_sel).astype(jnp.float32) * scale
        s_sel = jnp.where(sel_ok[:, None], s_sel, -jnp.inf)
        k_own = lax.dynamic_slice_in_dim(kb, own, 1, axis=2)[:, :, 0]
        v_own = lax.dynamic_slice_in_dim(vb, own, 1, axis=2)[:, :, 0]
        s_own = jnp.einsum('bhqd,bhld->bhql', qc, k_own).astype(jnp.float32) * scale
        kpos = own * MOBA_BLOCK + jnp.arange(MOBA_BLOCK)
        s_own = jnp.where(kpos[None, :] <= qpos[:, None], s_own, -jnp.inf)
        s = jnp.concatenate([s_sel.reshape(B, H, MOBA_Q_CHUNK, topk * MOBA_BLOCK), s_own], axis=-1)
        p = jax.nn.softmax(s, axis=-1).astype(v.dtype)
        p_sel = p[..., :topk * MOBA_BLOCK].reshape(B, H, MOBA_Q_CHUNK, topk, MOBA_BLOCK)
        p_own = p[..., topk * MOBA_BLOCK:]
        return (jnp.einsum('bhqkl,bhqkld->bhqd', p_sel, v_sel)
                + jnp.einsum('bhql,bhld->bhqd', p_own, v_own))

    out = lax.map(chunk, jnp.arange(n_chunks))
    return out.transpose(1, 0, 3, 2, 4).reshape(B, S, H, Dh)

def causal_depthwise_conv(x, w):
    C = x.shape[-1]
    return lax.conv_general_dilated(
        x, w[:, None, :].astype(x.dtype), window_strides=(1,),
        padding=((GDN_CONV - 1, 0),), dimension_numbers=('NWC', 'WIO', 'NWC'),
        feature_group_count=C)

def gated_delta_rule(q, k, v, g, beta):
    B, S, H, Dk = q.shape
    Dv = v.shape[-1]
    C = GDN_CHUNK
    N = S // C

    def to_chunks(t):
        return t.reshape(B, N, C, H, *t.shape[3:]).swapaxes(2, 3)

    q, k, v, g, beta = (to_chunks(t) for t in (q, k, v, g, beta))
    G = jnp.cumsum(g, axis=-1)
    incl = jnp.tril(jnp.ones((C, C), dtype=bool))
    strict = jnp.tril(jnp.ones((C, C), dtype=bool), k=-1)
    decay = jnp.exp(jnp.where(incl, G[..., :, None] - G[..., None, :], -jnp.inf))
    kk = jnp.einsum('bnhid,bnhjd->bnhij', k, k)
    A = jnp.where(strict, beta[..., :, None] * kk * decay, 0.0)
    eye = jnp.eye(C, dtype=A.dtype)
    gam = jnp.exp(G)
    rhs = jnp.concatenate([beta[..., None] * v, (beta * gam)[..., None] * k], axis=-1)
    sol = lax.linalg.triangular_solve(eye + A, rhs, left_side=True, lower=True, unit_diagonal=True)
    u_v, w = sol[..., :Dv], sol[..., Dv:]
    qk = jnp.einsum('bnhid,bnhjd->bnhij', q, k) * decay
    q_dec = q * gam[..., None]
    k_dec = k * jnp.exp(G[..., -1:] - G)[..., None]
    g_last = jnp.exp(G[..., -1])

    def step(state, xs):
        u_v_c, w_c, qk_c, q_dec_c, k_dec_c, g_last_c = xs
        u = u_v_c - jnp.einsum('bhck,bhkv->bhcv', w_c, state)
        o = jnp.einsum('bhck,bhkv->bhcv', q_dec_c, state) + jnp.einsum('bhij,bhjv->bhiv', qk_c, u)
        new_state = g_last_c[..., None, None] * state + jnp.einsum('bhck,bhcv->bhkv', k_dec_c, u)
        return new_state, o

    xs = tuple(t.swapaxes(0, 1) for t in (u_v, w, qk, q_dec, k_dec, g_last))
    state0 = jnp.zeros((B, H, Dk, Dv), dtype=q.dtype)
    _, o = lax.scan(step, state0, xs)
    return o.transpose(1, 0, 3, 2, 4).reshape(B, S, H, Dv)

def hierarchical_moe(h, w_group, w_router, w_gate, w_up, w_down):
    T = h.shape[0]
    group_logits = jnp.einsum('td,dg->tg', h, w_group).astype(jnp.float32)
    group_prob = jax.nn.softmax(group_logits, axis=-1)
    g_sel = jnp.argmax(group_logits, axis=-1)
    p_group = jnp.take_along_axis(group_prob, g_sel[:, None], axis=-1)
    expert_logits = jnp.einsum('td,de->te', h, w_router).astype(jnp.float32)
    expert_logits = expert_logits.reshape(T, N_GROUPS, EXPERTS_PER_GROUP)
    in_group = jnp.take_along_axis(expert_logits, g_sel[:, None, None], axis=1)[:, 0]
    in_prob = jax.nn.softmax(in_group, axis=-1)
    top_p, top_i = lax.top_k(in_prob, EXPERT_TOPK)
    top_p = top_p / jnp.sum(top_p, axis=-1, keepdims=True)
    within = jnp.sum(jax.nn.one_hot(top_i, EXPERTS_PER_GROUP, dtype=jnp.float32) * top_p[..., None], axis=1)
    combine = (jax.nn.one_hot(g_sel, N_GROUPS, dtype=jnp.float32)[:, :, None]
               * p_group[:, :, None] * within[:, None, :]).astype(h.dtype)
    y = jnp.zeros_like(h)
    for grp in range(N_GROUPS):
        hid = (jax.nn.silu(jnp.einsum('td,edf->tef', h, w_gate[grp]))
               * jnp.einsum('td,edf->tef', h, w_up[grp])) * combine[:, grp, :, None]
        y = y + jnp.einsum('tef,efd->td', hid, w_down[grp])
    return y

def second_inputs(seed: int = 0) -> dict:
    key = jax.random.key(seed)
    ks = jax.random.split(key, 16)
    f32 = jnp.float32
    D = D_MODEL
    x = jax.random.normal(ks[0], (BATCH, SEQ, D), f32)
    attn_norm = 1.0 + 0.02 * jax.random.normal(ks[1], (DEPTH, D), f32)
    w_in = jax.random.normal(ks[2], (DEPTH, D, IN_PROJ_WIDTH), f32) * D ** -0.5
    conv_w = jax.random.normal(ks[3], (DEPTH, GDN_CONV, 3 * GDN_WIDTH), f32) * GDN_CONV ** -0.5
    A_log = jnp.log(jax.random.uniform(ks[4], (DEPTH, GDN_HEADS), f32, 1.0, 16.0))
    dt = jnp.exp(jax.random.uniform(ks[5], (DEPTH, GDN_HEADS), f32, np.log(1e-3), np.log(1e-1)))
    dt_bias = dt + jnp.log(-jnp.expm1(-dt))
    gdn_norm = 1.0 + 0.02 * jax.random.normal(ks[6], (DEPTH, GDN_HEAD_DIM), f32)
    w_out = jax.random.normal(ks[7], (DEPTH, MIX_WIDTH_2, D), f32) * MIX_WIDTH_2 ** -0.5
    ffn_norm = 1.0 + 0.02 * jax.random.normal(ks[8], (DEPTH, D), f32)
    w_group = jax.random.normal(ks[9], (DEPTH, D, N_GROUPS), f32) * D ** -0.5
    w_router = jax.random.normal(ks[10], (DEPTH, D, N_GROUPS * EXPERTS_PER_GROUP), f32) * D ** -0.5
    w_gate = jax.random.normal(ks[11], (DEPTH, N_GROUPS, EXPERTS_PER_GROUP, D, EXPERT_FF), f32) * D ** -0.5
    w_up = jax.random.normal(ks[12], (DEPTH, N_GROUPS, EXPERTS_PER_GROUP, D, EXPERT_FF), f32) * D ** -0.5
    w_down = jax.random.normal(ks[13], (DEPTH, N_GROUPS, EXPERTS_PER_GROUP, EXPERT_FF, D), f32) * EXPERT_FF ** -0.5
    final_norm = 1.0 + 0.02 * jax.random.normal(ks[14], (D,), f32)
    return {'x': x, 'attn_norm': attn_norm, 'w_in': w_in, 'conv_w': conv_w, 'A_log': A_log,
            'dt_bias': dt_bias, 'gdn_norm': gdn_norm, 'w_out': w_out, 'ffn_norm': ffn_norm,
            'w_group': w_group, 'w_router': w_router, 'w_gate': w_gate, 'w_up': w_up,
            'w_down': w_down, 'final_norm': final_norm}

def second_block(x, attn_norm, w_in, conv_w, A_log, dt_bias, gdn_norm, w_out, ffn_norm,
              w_group, w_router, w_gate, w_up, w_down, final_norm):
    B, S, D = x.shape
    offsets = np.cumsum(IN_SPLITS_2)[:-1].tolist()
    f32 = jnp.float32
    for l in range(DEPTH):
        h = rmsnorm(x, attn_norm[l])
        proj = jnp.einsum('bsd,de->bse', h, w_in[l])
        mq, mk, mv, gqkv, gz, ga, gb = jnp.split(proj, offsets, axis=-1)
        to_a = lambda t: t.reshape(B, S, MOBA_HEADS, MOBA_HEAD_DIM)
        y_a = moba_attention(to_a(mq), to_a(mk), to_a(mv)).reshape(B, S, MOBA_WIDTH)
        gqkv = jax.nn.silu(causal_depthwise_conv(gqkv, conv_w[l]))
        gq, gk, gv = jnp.split(gqkv, 3, axis=-1)
        to_b = lambda t: t.reshape(B, S, GDN_HEADS, GDN_HEAD_DIM).astype(f32)
        gq = l2norm(to_b(gq)) * GDN_HEAD_DIM ** -0.5
        gk = l2norm(to_b(gk))
        log_decay = -jnp.exp(A_log[l].astype(f32)) * jax.nn.softplus(ga.astype(f32) + dt_bias[l].astype(f32))
        beta = jax.nn.sigmoid(gb.astype(f32))
        o_b = gated_delta_rule(gq, gk, to_b(gv), log_decay, beta)
        o_b = rmsnorm(o_b, gdn_norm[l]) * jax.nn.silu(to_b(gz))
        y_b = o_b.reshape(B, S, GDN_WIDTH).astype(x.dtype)
        mix = jnp.concatenate([y_a, y_b], axis=-1)
        x = x + jnp.einsum('bse,ed->bsd', mix, w_out[l])
        h = rmsnorm(x, ffn_norm[l]).reshape(B * S, D)
        y = hierarchical_moe(h, w_group[l], w_router[l], w_gate[l], w_up[l], w_down[l])
        x = x + y.reshape(B, S, D)
    return rmsnorm(x, final_norm)


def setup_inputs(seed=0):
    out = dict(first_inputs(seed))
    for name, value in second_inputs(seed + 1).items():
        if name != "x":
            out[name + "_2"] = value
    return out


def reference(
    x, c, ctx, c_ctx, w_mod, b_mod, norm1_g, norm2_g, w_in, ret_decay_logit, ret_norm_g,
    diff_qk_norm_g, diff_lambda, diff_norm_g, w_out, peer_w_query, peer_sub_keys, peer_u,
    peer_v, attn_norm_2, w_in_2, conv_w_2, A_log_2, dt_bias_2, gdn_norm_2, w_out_2, ffn_norm_2,
    w_group_2, w_router_2, w_gate_2, w_up_2, w_down_2, final_norm_2,
):
    x = first_block(
        x, c, ctx, c_ctx, w_mod, b_mod, norm1_g, norm2_g, w_in, ret_decay_logit, ret_norm_g,
        diff_qk_norm_g, diff_lambda, diff_norm_g, w_out, peer_w_query, peer_sub_keys, peer_u,
        peer_v,
    )
    return second_block(
        x, attn_norm_2, w_in_2, conv_w_2, A_log_2, dt_bias_2, gdn_norm_2, w_out_2, ffn_norm_2,
        w_group_2, w_router_2, w_gate_2, w_up_2, w_down_2, final_norm_2,
    )


_drawn_inputs = setup_inputs


def setup_inputs(seed=0):
    import zlib

    import numpy as np

    out = dict(_drawn_inputs(seed))
    spreads = {}
    factors = {'norm1_g': 7.194,
     'norm2_g': 41.216,
     'ret_norm_g': 21.682,
     'diff_qk_norm_g': 5.104,
     'diff_lambda': 3.569,
     'diff_norm_g': 64.0,
     'peer_u': 2.799,
     'gdn_norm_2': 25.984,
     'final_norm_2': 8.17,
     'attn_norm_2': 8.0,
     'ffn_norm_2': 8.0}
    for name, (base, spread) in spreads.items():
        noise = np.random.default_rng([zlib.crc32(name.encode()), seed]).standard_normal(out[name].shape)
        drawn = base * np.exp(spread * noise) if base else spread * noise
        out[name] = __import__('jax').numpy.asarray(drawn.astype(out[name].dtype))
    for name, factor in factors.items():
        out[name] = (out[name] * factor).astype(out[name].dtype)
    return out
```

```python
from contextlib import ExitStack

import numpy as np
import concourse.bass as bass
from concourse import mybir

P = 128
D = 1024
T = 256
NT = T // P
KD = D // P
EPS = 1e-6
RH, RK, RV = 4, 64, 128
DH, DD = 4, 64
IN1 = 3072
PH, NK, TOPK = 8, 128, 16
SLOTS = PH * TOPK
MH, MD = 8, 64
GH, GD = 4, 128
CONV = 4
NG, EG, FF = 4, 8, 256
NE = NG * EG
LAM_INIT = 0.2

CHUNK = 2048
COLS = CHUNK // KD
N_MOD = 6 * D // COLS
N_IN1 = IN1 // COLS
N_OUT = D // COLS
N_Q = 2 * PH * NK // COLS
N_SK = 1
N_IN2 = 3584 // COLS
C_MOD = 0
C_IN1 = C_MOD + N_MOD
C_OUT1 = C_IN1 + N_IN1
C_Q = C_OUT1 + N_OUT
C_SK = C_Q + N_Q
C_IN2 = C_SK + N_SK
C_OUT2 = C_IN2 + N_IN2
N_CHUNKS = C_OUT2 + N_OUT
WSLOTS = 8

SM = {}
_at = 0
for _name, _n in [("cond", 16), ("b_mod", 48), ("g1", 8), ("g2", 8), ("g3", 8), ("g4", 8), ("g5", 8),
                  ("conv", 48)]:
    SM[_name] = slice(_at, _at + _n)
    _at += _n
SM_N = _at
RW = {}
_at = 0
for _name, _n in [("ret_g", 512), ("diff_g", 512), ("qk_g", 128), ("lam", 256), ("decay", 8),
                  ("gdn_g", 128), ("A_log", 4), ("dt", 4)]:
    RW[_name] = slice(_at, _at + _n)
    _at += _n
RW_N = _at
CN = {}
_at = 0
for _name, _n in [("ident", 128), ("ones", 128), ("cos", NT * 64), ("sin", NT * 64), ("dist", NT * T),
                  ("iota", 16), ("eps", 1), ("upper", 128), ("lower", 128), ("causal", 128)]:
    CN[_name] = slice(_at, _at + _n)
    _at += _n
CN_N = _at
ARENA = 28928
LEVELS = 7

fp32 = mybir.dt.float32
u32 = mybir.dt.uint32
ALU = mybir.AluOpType
ACT = mybir.ActivationFunctionType
AX = mybir.AxisListType.X


class Carve:

    def __init__(self, tensor, at=0):
        self.tensor, self.at = tensor, at

    def take(self, *dims, dt=fp32):
        n = int(np.prod(dims))
        ap = self.tensor[:, self.at:self.at + n]
        self.at += n
        if dt is not fp32:
            ap = ap.bitcast(dt)
        if len(dims) > 1:
            names = "abcd"[:len(dims)]
            ap = ap.rearrange(f"p ({' '.join(names)}) -> p {' '.join(names)}",
                              **dict(zip(names, dims)))
        return ap


def bc(ap, axis, n):
    shape = list(ap.shape)
    shape.insert(axis, n)
    return ap.unsqueeze(axis).to_broadcast(shape)


def last_chunk_in(slot, before):
    return max(n for n in range(before) if n % WSLOTS == slot)


def two_blocks(nc, xT_d, ctxT_d, small_d, rows_d, const_d, masks_d, wstream_d, gate2_d, uv_d, route_d,
               moe_d, out_d):
    ctx = ExitStack()
    with ctx:
        def sb(name, n, dt=fp32):
            return ctx.enter_context(nc.sbuf_tensor(name, [P, n], dt))

        def sem(name):
            return ctx.enter_context(nc.semaphore(name))

        wring = sb("wring", WSLOTS * CHUNK)
        arena = sb("arena", ARENA)
        xT = sb("xT", KD * T)[:, :].rearrange("p (k t) -> p k t", k=KD)
        small = sb("small", SM_N)
        rows = sb("rows", RW_N)
        const = sb("const", CN_N)
        tiny = Carve(sb("tiny", 1024))
        bank = [ctx.enter_context(nc.psum_tensor(f"bank{i}", [P, 512], fp32)) for i in range(8)]

        ident, ones, epsc = const[:, CN["ident"]], const[:, CN["ones"]], const[:, CN["eps"]]

        def wchunk(n):
            s = n % WSLOTS
            return wring[:, s * CHUNK:(s + 1) * CHUNK].rearrange("p (k c) -> p k c", k=KD)

        condS = tiny.take(KD, 2)
        modv = tiny.take(6 * KD, 2)
        scale1 = tiny.take(2, KD)
        scale2 = tiny.take(KD)
        lg = tiny.take(8)
        lgL = tiny.take(8)
        nlg = tiny.take(8)
        lt = tiny.take(6, 8)
        lamt = tiny.take(2, 64)
        lam2 = tiny.take(4)
        ss = tiny.take(48)
        sr = tiny.take(48)
        zm = tiny.take(2, 2)
        zz = tiny.take(2, 2)
        zr = tiny.take(2, 2)

        m1 = Carve(arena)
        proj = m1.take(NT, IN1)
        cproj = m1.take(NT, 1792)
        hT = m1.take(KD, T)
        chT = m1.take(KD, T)
        tmp = m1.take(2, 1024)
        rqT = m1.take(2, T)
        rkT = m1.take(2, 2 * T)
        dqT = m1.take(4, T)
        dkT = m1.take(4, 2 * T)
        SD = m1.take(2, 4, T)
        DC = m1.take(2, 4, T)
        prob = m1.take(2, 2 * T)
        aT = m1.take(2, 4, P)
        Y = m1.take(NT, D)
        mixT = chT
        assert m1.at <= ARENA
        sq = tmp.rearrange("p a b -> p (a b)").rearrange("p (k t) -> p k t", k=KD)
        csq = Y.rearrange("p a b -> p (a b)").rearrange("p (k t) -> p k t", k=KD)
        rstd = prob[:, 0, :].rearrange("p (a t) -> p a t", a=2)

        GS = 8
        m2 = Carve(arena)
        G = m2.take(GS, 2 * D)
        early = Carve(arena)
        h2T = early.take(KD, T)
        sq2 = early.take(KD, T)
        qT = early.take(2 * PH, T)
        rstd2 = early.take(T)
        h2 = m2.take(NT, D)
        keyS = m2.take(NT, 2 * PH, NK)
        cand = m2.take(PH, TOPK * TOPK)
        hot = m2.take(SLOTS, TOPK)
        topv = m2.take(PH, 2, TOPK)
        topi = m2.take(PH, 2, TOPK, dt=u32)
        topf = m2.take(PH, 2, TOPK)
        pos = m2.take(SLOTS, dt=u32)
        posu = m2.take(2, SLOTS, dt=u32)
        posf = m2.take(2, SLOTS)
        chosen = m2.take(2, SLOTS)
        expert = m2.take(NT, SLOTS, dt=u32)
        gates = m2.take(NT, SLOTS)
        gsum = m2.take(PH)
        stage = m2.take(GS, dt=u32)
        dots = m2.take(2, 4)
        gelu = m2.take(2, 4)
        weight = m2.take(2, 4)
        assert m2.at <= ARENA
        diag = keyS[:, 0, 0:GS, :]
        zeros = hot.rearrange("p a b -> p (a b)")[:, 0:512]
        junk = cand.rearrange("p (c a) b -> p c (a b)", c=2)
        ffn = junk[:, 0, :]

        m3 = Carve(arena)
        h3T = m3.take(KD, T)
        sq3 = m3.take(KD, T)
        cvin = m3.take(12, CONV - 1 + T)
        rstd3 = m3.take(T)
        assert m3.at <= 8192
        late = Carve(arena)
        gD, gDT, gA, gAT, gT_, gTT, gM, gMT = (late.take(8, P) for _ in range(8))
        m3 = Carve(arena, late.at)
        mqT = m3.take(4, T)
        mkT = m3.take(4, T)
        mv = m3.take(NT, 512)
        gz = m3.take(NT, 512)
        cvT = m3.take(12, T)
        masks = m3.take(2, LEVELS, P)
        gate2 = m3.take(KD, 8)
        kTM = m3.take(8, P)
        vTM = m3.take(8, P)
        gW = m3.take(8, P)
        gR = m3.take(8, P)
        gU = m3.take(8, P)
        gS = m3.take(4, P)
        gwT = m3.take(4, P)
        soft = m3.take(384)
        softT = m3.take(384)
        Y2 = m3.take(NT, D)
        ab = m3.take(2, NT, 4)
        spt = m3.take(5, 8)
        g8 = m3.take(8)
        beta = m3.take(8)
        bg = m3.take(8)
        kd = m3.take(8)
        gc = m3.take(8)
        egc = m3.take(8)
        rz = m3.take(NT, MH)
        mx = m3.take(2, 2)
        ms2 = m3.take(8)
        assert m3.at <= ARENA
        nsq = Carve(arena, 6 * 1024).take(8, T)
        nrm = Carve(arena, 2 * 1024).take(8, T)
        mix2T = cvT[:, 0:KD, :]

        m4 = Carve(arena)
        h4T = m4.take(KD, T)
        sq4 = m4.take(KD, T)
        rstd4 = m4.take(T)
        CB = m4.take(NE, T)
        routeW = m4.take(KD, NG + NE)
        hid = m4.take(2, 2, T)
        sg = m4.take(2, 2, T)
        up = m4.take(2, 2, T)
        zero4 = m4.take(512)
        logit = m4.take(NT, NG + NE)
        pad8 = m4.take(NT, 8)
        gm8 = m4.take(NT, 8)
        gi8 = m4.take(NT, 8, dt=u32)
        gif = m4.take(NT, 8)
        ghot = m4.take(NT, NG)
        gex = m4.take(NT, NG)
        gsel = m4.take(NT, 8, NG)
        ing = m4.take(NT, 8)
        im8 = m4.take(NT, 8)
        ii8 = m4.take(NT, 8, dt=u32)
        iif = m4.take(NT, 8)
        pw = m4.take(NT, 4)
        within = m4.take(2, NT, 8)
        comb = m4.take(NT, NG, 8)
        assert m4.at <= ARENA

        chunk_here = [sem(f"chunk_here{i}") for i in range(WSLOTS)]
        chunk_used = sem("chunk_used")
        x_here = sem("x_here")
        small_here = sem("small_here")
        const_here = sem("const_here")
        act_step = sem("act_step")
        dve_step = sem("dve_step")
        cond_ready = sem("cond_ready")
        squares1 = sem("squares1")
        sums1 = sem("sums1")
        root1 = sem("root1")
        h_ready = sem("h_ready")
        proj_x_out = sem("proj_x_out")
        proj_c_out = sem("proj_c_out")
        qk_sq = sem("qk_sq")
        qk_root = sem("qk_root")
        roped = sem("roped")
        turned = sem("turned")
        turned_out = sem("turned_out")
        gam_e = sem("gam_e")
        gam_ready = sem("gam_ready")
        decay_args = sem("decay_args")
        decay_ready = sem("decay_ready")
        ret_scores = sem("ret_scores")
        ret_masked = sem("ret_masked")
        ret_y = sem("ret_y")
        ret_y_out = sem("ret_y_out")
        lam_dots = sem("lam_dots")
        lam_exp = sem("lam_exp")
        diff_scores = sem("diff_scores")
        diff_max = sem("diff_max")
        diff_exp = sem("diff_exp")
        diff_a = sem("diff_a")
        diff_aT = sem("diff_aT")
        diff_aT_out = sem("diff_aT_out")
        diff_y = sem("diff_y")
        y_ms = sem("y_ms")
        y_root = sem("y_root")
        mix_ready = sem("mix_ready")
        mixT_done = sem("mixT_done")
        mixT_out = sem("mixT_out")

        rms_sq = sem("rms_sq")
        rms_sum = sem("rms_sum")
        rms_root = sem("rms_root")
        h2_ready = sem("h2_ready")
        q_out = sem("q_out")
        keys_done = sem("keys_done")
        keys_out = sem("keys_out")
        h2_done = sem("h2_done")
        h2_out = sem("h2_out")
        top_exp = sem("top_exp")
        top_expd = sem("top_expd")
        top_ready = sem("top_ready")
        idx_staged = sem("idx_staged")
        dot_done = sem("dot_done")
        gelu_step = sem("gelu_step")
        diag_ready = sem("diag_ready")
        slot_used = sem("slot_used")
        zero_set = sem("zero_set")
        ffn_out = sem("ffn_out")
        ffnT_done = sem("ffnT_done")
        x2_ready = sem("x2_ready")
        h3_ready = sem("h3_ready")
        masks_here = sem("masks_here")
        in2_out = sem("in2_out")
        ab_done = sem("ab_done")
        ab_exp = sem("ab_exp")
        ab_expd = sem("ab_expd")
        conv_ready = sem("conv_ready")
        conv_silu = sem("conv_silu")
        lnorm_sq = sem("lnorm_sq")
        lnorm_sum = sem("lnorm_sum")
        lnorm_root = sem("lnorm_root")
        lnorm_done = sem("lnorm_done")
        tm_done = sem("tm_done")
        tm_out = sem("tm_out")
        g_ready = sem("g_ready")
        g_done = sem("g_done")
        gx_ready = sem("gx_ready")
        gx_exp = sem("gx_exp")
        kk_done = sem("kk_done")
        a_ready = sem("a_ready")
        at_done = sem("at_done")
        at_out = sem("at_out")
        level_ready = sem("level_ready")
        w_done = sem("w_done")
        w_out = sem("w_out")
        t_done = sem("t_done")
        uv_ready = sem("uv_ready")
        uv_done = sem("uv_done")
        uv_out = sem("uv_out")
        s_done = sem("s_done")
        s_out = sem("s_out")
        pt_done = sem("pt_done")
        pt_ready = sem("pt_ready")
        u1_done = sem("u1_done")
        u1_ready = sem("u1_ready")
        o_done = sem("o_done")
        moba_s = sem("moba_s")
        moba_m = sem("moba_m")
        moba_e = sem("moba_e")
        moba_T = sem("moba_T")
        moba_T_out = sem("moba_T_out")
        moba_y = sem("moba_y")
        y2_ms = sem("y2_ms")
        y2_root = sem("y2_root")
        mix2_ready = sem("mix2_ready")
        x3_ready = sem("x3_ready")
        h4_ready = sem("h4_ready")
        route_here = sem("route_here")
        route_done = sem("route_done")
        route_exp = sem("route_exp")
        route_expd = sem("route_expd")
        comb_ready = sem("comb_ready")
        cb_done = sem("cb_done")
        cb_even_out = sem("cb_even_out")
        cb_odd_out = sem("cb_odd_out")
        gu_done = sem("gu_done")
        gu_free = sem("gu_free")
        silu_ready = sem("silu_ready")
        hid_ready = sem("hid_ready")
        down_used = sem("down_used")
        out_ready = sem("out_ready")
        out_gone = sem("out_gone")
        gathered = [sem(f"gathered{j}") for j in range(GS)]
        gu_here = [sem(f"gu_here{b}") for b in range(2)]
        down_here = [sem(f"down_here{b}") for b in range(2)]

        block = ctx.enter_context(nc.Block())

        def chunk_ready(eng, n):
            eng.wait_ge(chunk_here[n % WSLOTS], 16 * (n // WSLOTS + 1))

        def chunk_done(eng, n):
            eng.wait_ge(chunk_used, n + 1)

        def project_fm(pe, c0, count, act_T, at=0):
            for n in range(count):
                chunk_ready(pe, c0 + n)
                w = wchunk(c0 + n)
                for j in range(2):
                    for k in range(KD):
                        ins = nc.tensor.matmul(bank[1 + (at + n) % 4][:, j * T:(j + 1) * T],
                                               w[:, k, j * P:(j + 1) * P], act_T[:, k, :],
                                               start=k == 0, stop=k == KD - 1)
                ins.then_inc(chunk_used, 1)

        def sums_over_features(pe, squares, nth):
            pe.wait_ge(rms_sq, nth)
            for k in range(KD):
                ins = nc.tensor.matmul(bank[7][:, 0:T], ones, squares[:, k, :], start=k == 0, stop=k == KD - 1)
            ins.then_inc(rms_sum, 1)

        def transposes(pe, out, blocks):
            for i, b in enumerate(blocks):
                ins = nc.tensor.transpose(out[:, i * P:(i + 1) * P], b, ident)
            return ins

        @block.sync
        def _(sp):
            for n in range(WSLOTS):
                sp.dma_start(wring[:, n * CHUNK:(n + 1) * CHUNK], wstream_d[n]).then_inc(chunk_here[n], 16)
            full = N_CHUNKS // WSLOTS
            with sp.Fori(1, full) as turn:
                for s in range(WSLOTS):
                    sp.wait_ge(chunk_used, turn * WSLOTS + (s + 1 - WSLOTS))
                    sp.dma_start(wring[:, s * CHUNK:(s + 1) * CHUNK],
                                 wstream_d[bass.ds(turn * WSLOTS + s, 1)].rearrange("a p c -> (a p) c"))\
                      .then_inc(chunk_here[s], 16)
            for n in range(full * WSLOTS, N_CHUNKS):
                sp.wait_ge(chunk_used, n + 1 - WSLOTS)
                s = n % WSLOTS
                sp.dma_start(wring[:, s * CHUNK:(s + 1) * CHUNK], wstream_d[n]).then_inc(chunk_here[s], 16)

            def gu_buf(b):
                return wring[:, 2 * b * CHUNK:(2 * b + 2) * CHUNK]

            def down_buf(b):
                return wring[:, (4 + b) * CHUNK:(5 + b) * CHUNK]

            for b in range(2):
                sp.wait_ge(chunk_used, last_chunk_in(2 * b, N_CHUNKS) + 1)
                sp.wait_ge(chunk_used, last_chunk_in(2 * b + 1, N_CHUNKS) + 1)
                sp.dma_start(gu_buf(b), moe_d[b, :, 0:2 * CHUNK]).then_inc(gu_here[b], 16)
                sp.wait_ge(chunk_used, last_chunk_in(4 + b, N_CHUNKS) + 1)
                sp.dma_start(down_buf(b), moe_d[b, :, 2 * CHUNK:3 * CHUNK]).then_inc(down_here[b], 16)
            with sp.Fori(1, NE // 2) as i:
                for b in range(2):
                    src = moe_d[bass.ds(2 * i + b, 1)].rearrange("a p c -> (a p) c")
                    sp.wait_ge(gu_done, 2 * i + (b - 1))
                    sp.dma_start(gu_buf(b), src[:, 0:2 * CHUNK]).then_inc(gu_here[b], 16)
                    sp.wait_ge(down_used, 2 * i + (b - 1))
                    sp.dma_start(down_buf(b), src[:, 2 * CHUNK:3 * CHUNK]).then_inc(down_here[b], 16)
            sp.wait_ge(out_ready, 1)
            sp.dma_start(out_d, h4T).then_inc(out_gone, 16)
            sp.wait_ge(out_gone, 16)

        @block.gpsimd
        def _(pool):
            def gather(t, j, column):
                src = bass.IndirectOffsetOnAxis(ap=column, axis=0)
                pool.indirect_dma_start(G[:, j, :], None, uv_d, src).then_inc(gathered[j], 16)

            for t in range(NT):
                pool.wait_ge(top_ready, t + 1)
                if t == 0:
                    chunk_done(pool, C_SK)
                    pool.wait_ge(h2_done, 4)
                    for j in range(GS):
                        gather(0, j, expert[:, 0, j:j + 1])
                with pool.Fori(1 if t == 0 else 0, SLOTS // GS) as turn:
                    for j in range(GS):
                        pool.wait_ge(slot_used, turn * GS + (t * SLOTS + j + 1 - GS))
                        nc.gpsimd.tensor_copy(stage[:, j:j + 1], expert[:, t, bass.ds(turn * GS + j, 1)])\
                          .then_inc(idx_staged, 1)
                        pool.wait_ge(top_ready, t + 1)
                        pool.wait_ge(idx_staged, turn * GS + (t * SLOTS + j + 1 - GS))
                        gather(t, j, stage[:, j:j + 1])

        @block.scalar
        def _(act):
            steps = [0]

            def own(ins):
                steps[0] += 1
                ins.then_inc(act_step, 1)
                act.wait_ge(act_step, steps[0])

            act.dma_start(small[:, :], small_d).then_inc(small_here, 16)
            act.dma_start(xT, xT_d).then_inc(x_here, 16)
            act.dma_start(chT, ctxT_d).then_inc(x_here, 16)
            act.dma_start(const[:, :], const_d).then_inc(const_here, 16)
            act.dma_start(rows[:, :], rows_d).then_inc(const_here, 16)
            act.wait_ge(small_here, 16)
            nc.scalar.activation(condS.rearrange("p k c -> p (k c)"), small[:, SM["cond"]], ACT.Silu)\
              .then_inc(cond_ready, 1)
            act.wait_ge(x_here, 32)
            act.wait_ge(const_here, 32)
            nc.scalar.activation(sq, xT, ACT.Square).then_inc(squares1, 1)
            nc.scalar.activation(csq, chT, ACT.Square).then_inc(squares1, 1)
            act.wait_ge(sums1, 1)
            nc.scalar.activation(rstd.rearrange("p a t -> p (a t)"), bank[7][:, :], ACT.Sqrt,
                                 bias=epsc, scale=1.0 / D).then_inc(root1, 1)
            for n in range(N_IN1):
                chunk_done(act, C_IN1 + n)
                func = ACT.Silu if n in (4, 5) else ACT.Copy
                nc.scalar.activation(proj[:, :, n * COLS:(n + 1) * COLS],
                                     bank[1 + 2 * (n % 2)][:, :].rearrange("p (t c) -> p t c", t=NT),
                                     func).then_inc(proj_x_out, 1)
            act.wait_ge(qk_sq, 1)
            nc.scalar.activation(sr, ss, ACT.Sqrt, bias=epsc, scale=1.0 / DD).then_inc(qk_root, 1)
            act.wait_ge(gam_e, 1)
            nc.scalar.activation(lt[:, 1, :], lt[:, 0, :], ACT.Exp).then_inc(gam_e, 1)
            act.wait_ge(lam_dots, 1)
            nc.scalar.activation(lam2[:, 0:2], lam2[:, 0:2], ACT.Exp).then_inc(lam_exp, 1)
            act.wait_ge(gam_ready, 1)
            for h in range(RH):
                act.wait_ge(decay_args, h + 1)
                d = DC[:, h % 2]
                dist = const[:, CN["dist"]].rearrange("p (k t) -> p k t", k=NT)
                if h >= 2:
                    act.wait_ge(ret_masked, h - 1)
                nc.scalar.activation(d[:, 0:2, :], dist, ACT.Exp, bias=lgL[:, h:h + 1],
                                     scale=lg[:, h:h + 1])
                nc.scalar.activation(tmp[:, h % 2, 0:512].rearrange("p (k t) -> p k t", k=NT), dist,
                                     ACT.Exp, bias=lgL[:, 4 + h:5 + h], scale=nlg[:, 4 + h:5 + h])
                nc.scalar.activation(d[:, 2:4, :].rearrange("p k t -> p (k t)"),
                                     tmp[:, h % 2, 512:1024], ACT.Exp).then_inc(decay_ready, 1)
            for i in range(DH * NT):
                for c in range(2):
                    act.wait_ge(diff_max, 2 * i + c + 1)
                    if i >= 1:
                        act.wait_ge(diff_a, i)
                    nc.scalar.activation(prob[:, c, :], bank[1 + 2 * (i % 2) + c][:, :], ACT.Exp,
                                         bias=zm[:, 1, c:c + 1], scale=DD ** -0.5,
                                         accum_out=zz[:, 0, c:c + 1]).then_inc(diff_exp, 1)
                act.wait_ge(diff_aT, i + 1)
                if i >= 2:
                    act.wait_ge(diff_y, i - 1)
                nc.scalar.activation(aT[:, i % 2].rearrange("p k t -> p (k t)"), bank[5 + i % 2][:, :],
                                     ACT.Copy).then_inc(diff_aT_out, 1)
            act.wait_ge(y_ms, 1)
            nc.scalar.activation(sr[:, 0:16], ss[:, 0:16], ACT.Sqrt, bias=epsc, scale=1.0 / RV)\
              .then_inc(y_root, 1)
            for g in range(4):
                act.wait_ge(mixT_done, g + 1)
                nc.scalar.activation(mixT[:, 2 * g:2 * g + 2, :].rearrange("p k t -> p (k t)"),
                                     bank[5 + g % 2][:, :], ACT.Copy).then_inc(mixT_out, 1)

            chunk_done(act, C_OUT1 + N_OUT - 1)
            act.wait_ge(x2_ready, 1)
            nc.scalar.activation(sq2, xT, ACT.Square).then_inc(rms_sq, 1)
            act.wait_ge(rms_sum, 1)
            nc.scalar.activation(rstd2, bank[7][:, 0:T], ACT.Sqrt, bias=epsc, scale=1.0 / D)\
              .then_inc(rms_root, 1)
            for n in range(N_Q):
                chunk_done(act, C_Q + n)
                nc.scalar.activation(qT[:, 2 * n:2 * n + 2, :].rearrange("p k t -> p (k t)"),
                                     bank[1 + n % 4][:, :], ACT.Copy).then_inc(q_out, 1)
            for g in range(4):
                act.wait_ge(h2_done, g + 1)
                nc.scalar.activation(h2[:, g // 2, (g % 2) * 512:(g % 2 + 1) * 512], bank[5 + g % 2][:, :],
                                     ACT.Copy).then_inc(h2_out, 1)
            for i in range(2 * NT):
                if i < 2 * NT - 1:
                    act.wait_ge(keys_done, i + 1)
                else:
                    chunk_done(act, C_SK)
                for b in range(2):
                    ins = nc.scalar.activation(
                        keyS[:, i // 2, 8 * (i % 2) + 4 * b:8 * (i % 2) + 4 * b + 4, :]
                        .rearrange("p h n -> p (h n)"), bank[(1, 3)[i % 2] + b][:, :], ACT.Copy)
                ins.then_inc(keys_out, 1)
            for t in range(NT):
                act.wait_ge(top_exp, t + 1)
                nc.scalar.activation(gates[:, t, :], gates[:, t, :], ACT.Exp).then_inc(top_expd, 1)
            n_step = 5
            for t in range(NT):
                with act.Fori(0, SLOTS // GS) as turn:
                    for g in range(2):
                        act.wait_ge(dot_done, turn * GS + (t * SLOTS + 4 * g + 4 + 2))
                        nc.scalar.activation(gelu[:, g, :], dots[:, g, :], ACT.Gelu).then_inc(gelu_step, 1)
                        done = turn * (2 * n_step) + (t * 2 * n_step * SLOTS // GS + g * n_step)
                        act.wait_ge(gelu_step, done + 1)
                        for q in range(4):
                            nc.scalar.activation(weight[:, g, q:q + 1], gelu[:, g, q:q + 1], ACT.Copy,
                                                 scale=gates[:, t, bass.ds(turn * GS + (4 * g + q), 1)])\
                              .then_inc(gelu_step, 1)
                        for q in range(4):
                            act.wait_ge(gelu_step, done + (q + 2))
                            nc.scalar.activation(diag[:, 4 * g + q, :], ident, ACT.Copy,
                                                 scale=weight[:, g, q:q + 1]).then_inc(diag_ready, 1)
                act.wait_ge(slot_used, (t + 1) * SLOTS)
                if t == 1:
                    act.wait_ge(ffnT_done, 2)
                for c in range(2):
                    ins = nc.scalar.activation(ffn[:, c * 512:(c + 1) * 512], bank[1 + 2 * t + c][:, :], ACT.Copy)
                ins.then_inc(ffn_out, 1)
            act.wait_ge(x2_ready, 2)
            act.dma_start(masks.rearrange("p w s n -> p (w s n)"), masks_d).then_inc(masks_here, 16)
            act.dma_start(gate2.rearrange("p k c -> p (k c)"), gate2_d).then_inc(masks_here, 16)
            nc.scalar.activation(sq3, xT, ACT.Square).then_inc(rms_sq, 1)
            act.wait_ge(rms_sum, 2)
            nc.scalar.activation(rstd3, bank[7][:, 0:T], ACT.Sqrt, bias=epsc, scale=1.0 / D)\
              .then_inc(rms_root, 1)
            for n in range(N_IN2):
                chunk_done(act, C_IN2 + n)
                b = bank[1 + n % 4]
                two = b[:, :].rearrange("p (k t) -> p k t", k=2)
                if n < 4:
                    dst, src = (mqT, mkT)[n // 2][:, 2 * (n % 2):2 * (n % 2) + 2, :], two
                elif n < 6:
                    dst, src = mv[:, :, (n - 4) * COLS:(n - 3) * COLS], two
                elif n < 12:
                    dst, src = cvin[:, 2 * (n - 6):2 * (n - 6) + 2, CONV - 1:], two
                else:
                    dst, src = gz[:, :, (n - 12) * COLS:(n - 11) * COLS], two
                nc.scalar.activation(dst, src, ACT.Silu if n >= 12 else ACT.Copy).then_inc(in2_out, 1)
            act.wait_ge(ab_exp, 1)
            nc.scalar.activation(spt[:, 1, :], spt[:, 0, :], ACT.Exp)
            nc.scalar.activation(beta, beta, ACT.Exp, scale=-1.0)
            nc.scalar.activation(kd[:, 0:4], rows[:, RW["A_log"]], ACT.Exp).then_inc(ab_expd, 1)
            act.wait_ge(conv_ready, 1)
            nc.scalar.activation(cvT, cvT, ACT.Silu).then_inc(conv_silu, 1)
            act.wait_ge(lnorm_sum, 1)
            for i in range(4):
                ins = nc.scalar.activation(nrm[:, 2 * i:2 * i + 2, :].rearrange("p a b -> p (a b)"),
                                           bank[1 + i][:, :], ACT.Sqrt, bias=epsc)
            ins.then_inc(lnorm_root, 1)
            act.wait_ge(g_done, 1)
            nc.scalar.activation(gc, bank[7][:, 0:8], ACT.Copy)
            for i in range(2):
                ins = nc.scalar.activation(gR[:, 4 * i:4 * i + 4, :].rearrange("p a b -> p (a b)"),
                                           bank[5 + i][:, :], ACT.Copy)
            ins.then_inc(g_done, 1)
            for i, dst in enumerate((kTM, vTM)):
                for c in range(2):
                    act.wait_ge(tm_done, 2 * i + c + 1)
                    nc.scalar.activation(dst[:, 4 * c:4 * c + 4, :].rearrange("p a b -> p (a b)"),
                                         bank[5 + c][:, :], ACT.Copy).then_inc(tm_out, 1)
            act.wait_ge(gx_ready, 1)
            nc.scalar.activation(gD, gD, ACT.Exp)
            nc.scalar.activation(gDT, gDT, ACT.Exp)
            nc.scalar.activation(egc, gc, ACT.Exp)
            nc.scalar.activation(kd, kd, ACT.Exp)
            nc.scalar.activation(gR, gR, ACT.Exp).then_inc(gx_exp, 1)
            act.wait_ge(at_done, 1)
            for i in range(2):
                ins = nc.scalar.activation(gAT[:, 4 * i:4 * i + 4, :].rearrange("p a b -> p (a b)"),
                                           bank[5 + i][:, :], ACT.Copy)
            ins.then_inc(at_out, 1)
            for s in range(1, LEVELS):
                act.wait_ge(w_done, s)
                for i in range(2):
                    ins = nc.scalar.activation(gW[:, 4 * i:4 * i + 4, :].rearrange("p a b -> p (a b)"),
                                               bank[1 + i][:, :], ACT.Copy)
                ins.then_inc(w_out, 1)
            act.wait_ge(uv_done, 1)
            for i in range(2):
                nc.scalar.activation(gU[:, 4 * i:4 * i + 4, :].rearrange("p a b -> p (a b)"),
                                     bank[1 + i][:, :], ACT.Copy)
            nc.scalar.activation(gwT.rearrange("p a b -> p (a b)"), bank[3][:, :], ACT.Copy).then_inc(uv_out, 1)
            act.wait_ge(s_done, 1)
            nc.scalar.activation(gS.rearrange("p a b -> p (a b)"), bank[4][:, :], ACT.Copy).then_inc(s_out, 1)
            for h in range(MH):
                act.wait_ge(moba_m, h + 1)
                if h >= 1:
                    act.wait_ge(moba_T, h)
                nc.scalar.activation(soft[:, 0:P], soft[:, 0:P], ACT.Exp, bias=mx[:, 1, 0:1],
                                     accum_out=rz[:, 0, h:h + 1])
                nc.scalar.activation(soft[:, P:3 * P], soft[:, P:3 * P], ACT.Exp, bias=mx[:, 1, 1:2],
                                     accum_out=rz[:, 1, h:h + 1]).then_inc(moba_e, 1)
                act.wait_ge(moba_T, h + 1)
                if h >= 1:
                    act.wait_ge(moba_y, h)
                nc.scalar.activation(softT, bank[7][:, 0:3 * P], ACT.Copy).then_inc(moba_T_out, 1)
            act.wait_ge(y2_ms, 1)
            nc.scalar.activation(ms2, ms2, ACT.Sqrt, bias=epsc, scale=1.0 / GD).then_inc(y2_root, 1)
            for g in range(4):
                act.wait_ge(mixT_done, 4 + g + 1)
                nc.scalar.activation(mix2T[:, 2 * g:2 * g + 2, :].rearrange("p k t -> p (k t)"),
                                     bank[5 + g % 2][:, :], ACT.Copy).then_inc(mixT_out, 1)
            act.wait_ge(x3_ready, 1)
            act.dma_start(routeW.rearrange("p k e -> p (k e)"), route_d).then_inc(route_here, 16)
            nc.scalar.activation(sq4, xT, ACT.Square).then_inc(rms_sq, 1)
            act.wait_ge(rms_sum, 3)
            nc.scalar.activation(rstd4, bank[7][:, 0:T], ACT.Sqrt, bias=epsc, scale=1.0 / D)\
              .then_inc(rms_root, 1)
            act.wait_ge(route_exp, 1)
            nc.scalar.activation(gex, gex, ACT.Exp)
            nc.scalar.activation(pw[:, :, 1:2], pw[:, :, 0:1], ACT.Exp).then_inc(route_expd, 1)
            for i in range(0, NE // 2, 2):
                act.wait_ge(cb_done, i + 1)
                nc.scalar.activation(CB[:, 2 * i:2 * i + 2, :].rearrange("p e t -> p (e t)"),
                                     bank[4][:, :], ACT.Copy).then_inc(cb_even_out, 1)
            with act.Fori(0, NE // 2) as i:
                for b in range(2):
                    act.wait_ge(gu_done, 2 * i + (b + 1))
                    nc.scalar.activation(sg[:, b].rearrange("p f t -> p (f t)"), bank[4 + 2 * b][:, :],
                                         ACT.Silu).then_inc(silu_ready, 1)
            act.wait_ge(x3_ready, 2)
            nc.scalar.activation(sq4, xT, ACT.Square).then_inc(rms_sq, 1)
            act.wait_ge(rms_sum, 4)
            nc.scalar.activation(rstd4, bank[7][:, 0:T], ACT.Sqrt, bias=epsc, scale=1.0 / D)\
              .then_inc(rms_root, 1)

        @block.vector
        def _(dve):
            v = nc.vector
            steps = [0]

            def link(ins):
                steps[0] += 1
                ins.then_inc(dve_step, 1)
                dve.wait_ge(dve_step, steps[0])

            dve.wait_ge(const_here, 32)
            x = rows[:, RW["decay"]]
            link(v.tensor_scalar(lt[:, 2, :], x, -1.0, None, ALU.mult))
            link(v.tensor_tensor(lt[:, 0, :], x, lt[:, 2, :], ALU.min))
            v.memset(ss, 0.0).then_inc(gam_e, 1)
            lam = rows[:, RW["lam"]].rearrange("p (a c) -> p a c", a=4)
            link(v.tensor_tensor(lamt[:, 0, :], lam[:, 0, :], lam[:, 1, :], ALU.mult))
            link(v.tensor_tensor(lamt[:, 1, :], lam[:, 2, :], lam[:, 3, :], ALU.mult))
            v.tensor_reduce(lam2[:, 0:2], lamt, AX, ALU.add).then_inc(lam_dots, 1)

            dve.wait_ge(root1, 1)
            link(v.reciprocal(rstd, rstd))
            link(v.tensor_tensor(hT, xT, bc(rstd[:, 0, :], 1, KD), ALU.mult))
            link(v.tensor_tensor(chT, chT, bc(rstd[:, 1, :], 1, KD), ALU.mult))
            chunk_done(dve, C_MOD + N_MOD - 1)
            link(v.tensor_tensor(modv, bank[0][:, 0:96].rearrange("p (m c) -> p m c", c=2),
                                 bc(small[:, SM["b_mod"]], 2, 2), ALU.add))
            for c in range(2):
                link(v.scalar_tensor_tensor(scale1[:, c, :], modv[:, KD:2 * KD, c], 1.0,
                                            small[:, SM["g1"]], ALU.add, ALU.mult))
            link(v.scalar_tensor_tensor(scale2, modv[:, 4 * KD:5 * KD, 0], 1.0,
                                        small[:, SM["g2"]], ALU.add, ALU.mult))
            for k in range(KD):
                for c, h in enumerate((hT, chT)):
                    ins = v.tensor_scalar(h[:, k, :], h[:, k, :], scale1[:, c, k:k + 1],
                                          modv[:, k, c:c + 1], ALU.mult, ALU.add)
            ins.then_inc(h_ready, 1)
            at = 0
            for n in range(N_IN1):
                if n in CTX_CHUNKS:
                    chunk_done(dve, C_IN1 + n)
                    v.tensor_copy(cproj[:, :, at:at + COLS],
                                  bank[2 + 2 * (n % 2)][:, :].rearrange("p (t c) -> p t c", t=NT))\
                     .then_inc(proj_c_out, 1)
                    at += COLS
            dve.wait_ge(proj_c_out, 7)
            dve.wait_ge(proj_x_out, N_IN1)
            qk = [(proj[:, t, 1536:2560], 16, 16 * t) for t in range(NT)]
            qk += [(cproj[:, t, 768:1280], 8, 32 + 8 * t) for t in range(NT)]
            for ap, n, at in qk:
                flat = tmp[:, 0, 0:n * DD]
                link(v.tensor_tensor(flat, ap, ap, ALU.mult))
                ins = v.tensor_reduce(ss[:, at:at + n], flat.rearrange("p (h c) -> p h c", h=n), AX, ALU.add)
                if at == 40:
                    ins.then_inc(qk_sq, 1)
                else:
                    link(ins)
            dve.wait_ge(qk_root, 1)
            link(v.reciprocal(sr, sr))
            gq, gk = rows[:, RW["qk_g"]][:, 0:DD], rows[:, RW["qk_g"]][:, DD:2 * DD]
            for ap, n, at in qk:
                a3 = ap.rearrange("p (h c) -> p h c", h=n)
                link(v.tensor_tensor(a3, a3, bc(sr[:, at:at + n], 2, DD), ALU.mult))
                if n == 16:
                    link(v.tensor_tensor(a3[:, 0:8], a3[:, 0:8], bc(gq, 1, 8), ALU.mult))
                    link(v.tensor_tensor(a3[:, 8:16], a3[:, 8:16], bc(gk, 1, 8), ALU.mult))
                else:
                    link(v.tensor_tensor(a3, a3, bc(gk, 1, 8), ALU.mult))
            for t in range(NT):
                cos = const[:, CN["cos"]][:, t * 64:(t + 1) * 64]
                sin = const[:, CN["sin"]][:, t * 64:(t + 1) * 64]
                for lo, n in ((0, 8), (1536, 16)):
                    a = proj[:, t, lo:lo + n * 64]
                    t0, t1 = tmp[:, 0, 0:n * 64], tmp[:, 1, 0:n * 64]

                    def parts(ap):
                        return ap.rearrange("p (h r c) -> p h r c", r=2, c=16)
                    link(v.tensor_tensor(t0.rearrange("p (h c) -> p h c", h=n),
                                         a.rearrange("p (h c) -> p h c", h=n), bc(cos, 1, n), ALU.mult))
                    for half in range(2):
                        x4 = a.rearrange("p (h r s c) -> p h r s c", r=2, s=2, c=16)
                        o4 = t1.rearrange("p (h r s c) -> p h r s c", r=2, s=2, c=16)
                        s4 = sin.rearrange("p (r s c) -> p r s c", r=2, s=2)
                        link(v.tensor_tensor(o4[:, :, :, half, :], x4[:, :, :, 1 - half, :],
                                             bc(s4[:, :, half, :], 1, n), ALU.mult))
                    link(v.tensor_tensor(a, t0, t1, ALU.add))
            v.memset(lamt, 0.0).then_inc(roped, 1)
            dve.wait_ge(gam_e, 2)
            e = lt[:, 1, :]
            link(v.tensor_scalar(lt[:, 2, :], e, 2.0, None, ALU.add))
            link(v.reciprocal(lt[:, 2, :], lt[:, 2, :]))
            link(v.tensor_tensor(lt[:, 3, :], e, lt[:, 2, :], ALU.mult))
            link(v.tensor_tensor(lt[:, 4, :], lt[:, 3, :], lt[:, 3, :], ALU.mult))
            link(v.tensor_scalar(lt[:, 5, :], lt[:, 4, :], 2.0 / 17, 2.0 / 15, ALU.mult, ALU.add))
            for k in (13, 11, 9, 7, 5, 3, 1):
                link(v.tensor_tensor(lt[:, 5, :], lt[:, 5, :], lt[:, 4, :], ALU.mult))
                link(v.tensor_scalar(lt[:, 5, :], lt[:, 5, :], 2.0 / k, None, ALU.add))
            link(v.tensor_tensor(lt[:, 5, :], lt[:, 5, :], lt[:, 3, :], ALU.mult))
            link(v.scalar_tensor_tensor(lg, x, 0.0, lt[:, 5, :], ALU.min, ALU.subtract))
            link(v.tensor_scalar(nlg, lg, -1.0, None, ALU.mult))
            v.tensor_scalar(lgL, lg, float(T), None, ALU.mult).then_inc(gam_ready, 1)
            dve.wait_ge(lam_exp, 1)
            link(v.tensor_tensor(lam2[:, 2:3], lam2[:, 1:2], lam2[:, 0:1], ALU.subtract))
            link(v.tensor_scalar(lam2[:, 3:4], lam2[:, 2:3], -LAM_INIT, None, ALU.add))
            dve.wait_ge(gam_ready, 1)

            for i, dst in enumerate(turned_views(rqT, rkT, dqT, dkT)):
                dve.wait_ge(turned, i + 1)
                v.tensor_copy(dst, bank[5 + i % 2][:, :].rearrange("p (b t) -> p b t", b=2))\
                 .then_inc(turned_out, 1)
            dist = const[:, CN["dist"]].rearrange("p (k t) -> p k t", k=NT)

            def decay_arg(h):
                w = tmp[:, h % 2, 512:1024].rearrange("p (k t) -> p k t", k=NT)
                u = prob[:, h % 2, :].rearrange("p (k t) -> p k t", k=NT)
                link(v.tensor_scalar(w, dist, 0.0, lg[:, h:h + 1], ALU.max, ALU.mult))
                link(v.tensor_scalar(u, dist, 0.0, nlg[:, 4 + h:5 + h], ALU.min, ALU.mult))
                v.tensor_tensor(w, w, u, ALU.add).then_inc(decay_args, 1)

            decay_arg(0)
            for h in range(RH):
                if h + 1 < RH:
                    decay_arg(h + 1)
                dve.wait_ge(decay_ready, h + 1)
                d = DC[:, h % 2]
                link(v.tensor_tensor(d[:, 0:2, :].rearrange("p k t -> p (k t)"),
                                     d[:, 0:2, :].rearrange("p k t -> p (k t)"),
                                     tmp[:, h % 2, 0:512], ALU.add))
                dve.wait_ge(ret_scores, h + 1)
                if h >= 2:
                    dve.wait_ge(ret_y, h - 1)
                for half in range(2):
                    ins = v.scalar_tensor_tensor(
                        SD[:, h % 2, 2 * half:2 * half + 2].rearrange("p k t -> p (k t)"),
                        bank[1 + 2 * (h % 2) + half][:, :], RK ** -0.5,
                        d[:, 2 * half:2 * half + 2].rearrange("p k t -> p (k t)"), ALU.mult, ALU.mult)
                ins.then_inc(ret_masked, 1)
            for j in range(2):
                dve.wait_ge(ret_y, 2 * j + 2)
                v.tensor_copy(Y[:, :, 256 * j:256 * j + 256].rearrange("p t (h e) -> p h t e", h=2),
                              bank[(0, 7)[j]][:, :].rearrange("p (h t e) -> p h t e", h=2, t=NT))\
                 .then_inc(ret_y_out, 1)
            for i in range(DH * NT):
                for c in range(2):
                    dve.wait_ge(diff_scores, 2 * i + c + 1)
                    link(v.reduce_max(zm[:, 0, c:c + 1], bank[1 + 2 * (i % 2) + c][:, :], AX))
                    v.tensor_scalar(zm[:, 1, c:c + 1], zm[:, 0, c:c + 1], -DD ** -0.5, None, ALU.mult)\
                     .then_inc(diff_max, 1)
                dve.wait_ge(diff_exp, 2 * i + 2)
                link(v.reciprocal(zr[:, 0, :], zz[:, 0, :]))
                link(v.tensor_tensor(zr[:, 1, 0:1], zr[:, 0, 1:2], lam2[:, 3:4], ALU.mult))
                link(v.tensor_scalar(prob[:, 0, :], prob[:, 0, :], zr[:, 0, 0:1], None, ALU.mult))
                if i >= 1:
                    dve.wait_ge(diff_aT, i)
                v.scalar_tensor_tensor(tmp[:, 0, 0:512], prob[:, 1, :], zr[:, 1, 0:1], prob[:, 0, :],
                                       ALU.mult, ALU.add).then_inc(diff_a, 1)
            for j in range(2):
                dve.wait_ge(diff_y, 4 * j + 4)
                link(v.tensor_copy(
                    Y[:, :, 512 + 256 * j:768 + 256 * j].rearrange("p t (h e) -> p h t e", h=2),
                    bank[(0, 7)[j]][:, :].rearrange("p (h t e) -> p h t e", h=2, t=NT)))
            for t in range(NT):
                dve.wait_ge(diff_aT, DH * NT)
                link(v.tensor_tensor(tmp[:, t, :], Y[:, t, :], Y[:, t, :], ALU.mult))
                ins = v.tensor_reduce(ss[:, 8 * t:8 * t + 8], tmp[:, t, :].rearrange("p (h e) -> p h e", h=8),
                                      AX, ALU.add)
                if t == NT - 1:
                    ins.then_inc(y_ms, 1)
                else:
                    link(ins)
            dve.wait_ge(y_root, 1)
            link(v.reciprocal(sr[:, 0:16], sr[:, 0:16]))
            for t in range(NT):
                y = Y[:, t, :]
                y3 = y.rearrange("p (h e) -> p h e", h=8)
                link(v.tensor_tensor(y3, y3, bc(sr[:, 8 * t:8 * t + 8], 2, RV), ALU.mult))
                link(v.tensor_tensor(y[:, 0:512], y[:, 0:512], proj[:, t, 1024:1536], ALU.mult))
                link(v.tensor_tensor(y[:, 0:512], y[:, 0:512], rows[:, RW["ret_g"]], ALU.mult))
                v.scalar_tensor_tensor(y[:, 512:1024], y[:, 512:1024], 1.0 - LAM_INIT,
                                       rows[:, RW["diff_g"]], ALU.mult, ALU.mult).then_inc(mix_ready, 1)
            for n in range(N_OUT):
                chunk_done(dve, C_OUT1 + n)
                for m in (2 * n, 2 * n + 1):
                    link(v.scalar_tensor_tensor(xT[:, m, :], bank[1 + n][:, (m % 2) * T:(m % 2 + 1) * T],
                                                modv[:, 2 * KD + m, 0:1], xT[:, m, :], ALU.mult, ALU.add))
            v.memset(zr, 0.0).then_inc(x2_ready, 1)
            dve.wait_ge(rms_root, 1)
            link(v.reciprocal(rstd2, rstd2))
            link(v.tensor_tensor(h2T, xT, bc(rstd2, 1, KD), ALU.mult))
            for k in range(KD):
                ins = v.tensor_scalar(h2T[:, k, :], h2T[:, k, :], scale2[:, k:k + 1],
                                      modv[:, 3 * KD + k, 0:1], ALU.mult, ALU.add)
            ins.then_inc(h2_ready, 1)
            low = -3.0e38
            for t in range(NT):
                dve.wait_ge(keys_out, 2 * t + 2)
                halves = [(h, p) for h in range(PH) for p in range(2)]
                for first in (True, False):
                    r = slice(0, 8) if first else slice(8, 16)
                    for h, p in halves:
                        ins = v.max(topv[:, h, p, r], keyS[:, t, 2 * h + p, :])
                    link(ins)
                    for h, p in halves:
                        ins = v.max_index(topi[:, h, p, r], topv[:, h, p, r], keyS[:, t, 2 * h + p, :])
                    link(ins)
                    if first:
                        for h, p in halves:
                            s_ = keyS[:, t, 2 * h + p, :]
                            ins = v.match_replace(s_, topv[:, h, p, r], s_, low)
                        link(ins)
                link(v.tensor_copy(topf, topi))
                c4 = cand.rearrange("p h (a b) -> p h a b", a=TOPK)
                link(v.tensor_tensor(c4, bc(topv[:, :, 0, :], 3, TOPK), bc(topv[:, :, 1, :], 2, TOPK), ALU.add))
                best = gates[:, t, :].rearrange("p (h k) -> p h k", h=PH)
                pos3 = pos.rearrange("p (h k) -> p h k", h=PH)
                for first in (True, False):
                    r = slice(0, 8) if first else slice(8, 16)
                    for h in range(PH):
                        ins = v.max(best[:, h, r], cand[:, h, :])
                    link(ins)
                    for h in range(PH):
                        ins = v.max_index(pos3[:, h, r], best[:, h, r], cand[:, h, :])
                    link(ins)
                    if first:
                        for h in range(PH):
                            ins = v.match_replace(cand[:, h, :], best[:, h, r], cand[:, h, :], low)
                        link(ins)
                link(v.tensor_copy(gsum, best[:, :, 0]))
                v.tensor_tensor(best, best, bc(gsum, 2, TOPK), ALU.subtract).then_inc(top_exp, 1)
                link(v.tensor_scalar(posu[:, 0, :], pos, 4, None, ALU.logical_shift_right))
                link(v.tensor_scalar(posu[:, 1, :], pos, TOPK - 1, None, ALU.bitwise_and))
                link(v.tensor_copy(posf, posu))
                for p in range(2):
                    link(v.tensor_tensor(hot, bc(posf[:, p, :], 2, TOPK), bc(const[:, CN["iota"]], 1, SLOTS),
                                         ALU.is_equal))
                    h4 = hot.rearrange("p (h k) a -> p h k a", h=PH)
                    link(v.tensor_tensor(h4, h4, bc(topf[:, :, p, :], 2, TOPK), ALU.mult))
                    link(v.tensor_reduce(chosen[:, p, :], hot, AX, ALU.add))
                link(v.scalar_tensor_tensor(posf[:, 0, :], chosen[:, 0, :], float(NK), chosen[:, 1, :],
                                            ALU.mult, ALU.add))
                link(v.tensor_copy(expert[:, t, :], posf[:, 0, :]))
                dve.wait_ge(top_expd, t + 1)
                link(v.tensor_reduce(gsum, best, AX, ALU.add))
                link(v.reciprocal(gsum, gsum))
                v.tensor_tensor(best, best, bc(gsum, 2, TOPK), ALU.mult).then_inc(top_ready, 1)
            dve.wait_ge(top_ready, NT)
            v.memset(zeros, 0.0).then_inc(zero_set, 1)
            v.memset(zr, 0.0).then_inc(dot_done, 2)
            dve.wait_ge(h2_out, 4)
            for t in range(NT):
                with dve.Fori(0, SLOTS // GS) as turn:
                    for j in range(GS):
                        dve.wait_ge(gathered[j], turn * 16 + 16 * (t * SLOTS // GS + 1))
                        dve.wait_ge(dot_done, turn * GS + (t * SLOTS + j + 1))
                        v.tensor_tensor_reduce(out=junk[:, j % 2], in0=G[:, j, 0:D], in1=h2[:, t, :], scale=1.0,
                                               scalar=0.0, op0=ALU.mult, op1=ALU.add,
                                               accum_out=dots[:, j // 4, j % 4:j % 4 + 1])\
                         .then_inc(dot_done, 1)
                for i in range(2):
                    dve.wait_ge(ffnT_done, 2 * t + i + 1)
                    for m in range(4 * i, 4 * i + 4):
                        x_ = xT[:, m, t * P:(t + 1) * P]
                        ins = v.scalar_tensor_tensor(x_, bank[5 + i][:, (m % 4) * P:(m % 4 + 1) * P],
                                                     modv[:, 5 * KD + m, 0:1], x_, ALU.mult, ALU.add)
            ins.then_inc(x2_ready, 1)
            dve.wait_ge(rms_root, 2)
            v.memset(cvin[:, :, 0:CONV - 1], 0.0)
            link(v.reciprocal(rstd3, rstd3))
            link(v.tensor_tensor(h3T, xT, bc(rstd3, 1, KD), ALU.mult))
            v.tensor_tensor(h3T, h3T, bc(small[:, SM["g3"]], 2, T), ALU.mult).then_inc(h3_ready, 1)
            dve.wait_ge(ab_done, 1)
            both = bank[5][:, 0:NT * 8].rearrange("p (t c) -> p t c", t=NT)
            flat = lambda a: a.rearrange("p t h -> p (t h)")
            link(v.tensor_tensor(ab[:, 0], both[:, :, 0:4], bc(rows[:, RW["dt"]], 1, NT), ALU.add))
            link(v.tensor_copy(beta.rearrange("p (t h) -> p t h", t=NT), both[:, :, 4:8]))
            link(v.tensor_scalar(spt[:, 2, :], flat(ab[:, 0]), -1.0, None, ALU.mult))
            v.tensor_tensor(spt[:, 0, :], flat(ab[:, 0]), spt[:, 2, :], ALU.min).then_inc(ab_exp, 1)
            dve.wait_ge(ab_expd, 1)
            e = spt[:, 1, :]
            link(v.tensor_scalar(spt[:, 2, :], e, 2.0, None, ALU.add))
            link(v.reciprocal(spt[:, 2, :], spt[:, 2, :]))
            link(v.tensor_tensor(spt[:, 3, :], e, spt[:, 2, :], ALU.mult))
            link(v.tensor_tensor(spt[:, 4, :], spt[:, 3, :], spt[:, 3, :], ALU.mult))
            link(v.tensor_scalar(spt[:, 2, :], spt[:, 4, :], 2.0 / 17, 2.0 / 15, ALU.mult, ALU.add))
            for k in (13, 11, 9, 7, 5, 3, 1):
                link(v.tensor_tensor(spt[:, 2, :], spt[:, 2, :], spt[:, 4, :], ALU.mult))
                link(v.tensor_scalar(spt[:, 2, :], spt[:, 2, :], 2.0 / k, None, ALU.add))
            link(v.tensor_tensor(spt[:, 2, :], spt[:, 2, :], spt[:, 3, :], ALU.mult))
            link(v.scalar_tensor_tensor(spt[:, 3, :], flat(ab[:, 0]), 0.0, spt[:, 2, :], ALU.max, ALU.add))
            link(v.tensor_tensor(g8.rearrange("p (t h) -> p t h", t=NT),
                                 spt[:, 3, :].rearrange("p (t h) -> p t h", t=NT), bc(kd[:, 0:4], 1, NT),
                                 ALU.mult))
            link(v.tensor_scalar(g8, g8, -1.0, None, ALU.mult))
            link(v.tensor_scalar(beta, beta, 1.0, None, ALU.add))
            v.reciprocal(beta, beta).then_inc(g_ready, 1)
            dve.wait_ge(in2_out, 12)
            cw = small[:, SM["conv"]].rearrange("p (b i) -> p b i", i=CONV)
            for i in range(CONV):
                for b in range(12):
                    src = cvin[:, b, i:i + T]
                    if i == 0:
                        ins = v.tensor_scalar(cvT[:, b, :], src, cw[:, b, 0:1], None, ALU.mult)
                    else:
                        ins = v.scalar_tensor_tensor(cvT[:, b, :], src, cw[:, b, i:i + 1], cvT[:, b, :],
                                                     ALU.mult, ALU.add)
                if i < CONV - 1:
                    link(ins)
            ins.then_inc(conv_ready, 1)
            dve.wait_ge(conv_silu, 1)
            qk = cvT[:, 0:8, :]
            v.tensor_tensor(nsq, qk, qk, ALU.mult).then_inc(lnorm_sq, 1)
            dve.wait_ge(lnorm_root, 1)
            link(v.reciprocal(nrm, nrm))
            link(v.tensor_tensor(qk, qk, nrm, ALU.mult))
            v.tensor_scalar(cvT[:, 0:4, :], cvT[:, 0:4, :], GD ** -0.5, None, ALU.mult)\
             .then_inc(lnorm_done, 1)
            dve.wait_ge(g_done, 2)
            last = gR[:, :, P - 1]
            link(v.tensor_tensor(gM, gR, bc(gc, 2, P), ALU.subtract))
            link(v.tensor_scalar(gD, gM, 0.0, -1.0, ALU.max, ALU.mult))
            link(v.tensor_scalar(gDT, gM, 0.0, None, ALU.min))
            v.tensor_tensor(kd, last, gc, ALU.subtract).then_inc(gx_ready, 1)
            dve.wait_ge(gx_exp, 1)
            link(v.tensor_tensor(gDT, gDT, bc(const[:, CN["upper"]], 1, 8), ALU.mult))
            dve.wait_ge(kk_done, 1)
            for p in range(8):
                ins = v.scalar_tensor_tensor(gA[:, p, :], bank[3 + p // 4][:, (p % 4) * P:(p % 4 + 1) * P],
                                             beta[:, p:p + 1], gD[:, p, :], ALU.mult, ALU.mult)
            ins.then_inc(a_ready, 1)
            link(v.tensor_tensor(bg, beta, egc, ALU.mult))
            dve.wait_ge(tm_out, 4)
            link(v.tensor_tensor(vTM, vTM, bc(beta, 2, P), ALU.mult))
            dve.wait_ge(a_ready, 1)
            link(v.tensor_tensor(gD[:, 4:8, :], kTM[:, 4:8, :], bc(bg[:, 4:8], 2, P), ALU.mult))
            link(v.tensor_tensor(gD[:, 0:4, :], kTM[:, 0:4, :], bc(kd[:, 0:4], 2, P), ALU.mult))
            link(v.tensor_tensor(gR[:, 4:8, :], cvT[:, 0:4, P:2 * P], gR[:, 4:8, :], ALU.mult))
            dve.wait_ge(at_out, 1)
            dve.wait_ge(masks_here, 32)

            def masked(out, a, which, s):
                link(v.tensor_tensor(out, a, bc(masks[:, which, s, :], 1, 8), ALU.mult))

            masked(gM, gA, 0, 0)
            masked(gMT, gAT, 1, 0)
            link(v.tensor_tensor(gT_, bc(ident, 1, 8), gM, ALU.subtract))
            link(v.tensor_tensor(gTT, bc(ident, 1, 8), gMT, ALU.subtract))
            for s in range(1, LEVELS):
                masked(gM, gA, 0, s)
                link(v.tensor_tensor(gMT, gAT, bc(masks[:, 1, s, :], 1, 8), ALU.mult))
                v.memset(zr, 0.0).then_inc(level_ready, 1)
                dve.wait_ge(t_done, s)
                for i in range(2):
                    q4 = slice(4 * i, 4 * i + 4)
                    link(v.tensor_tensor(gT_[:, q4, :], gT_[:, q4, :],
                                         bank[3 + i][:, :].rearrange("p (a b) -> p a b", a=4), ALU.subtract))
                    link(v.tensor_tensor(gTT[:, q4, :], gTT[:, q4, :],
                                         bank[5 + i][:, :].rearrange("p (a b) -> p a b", a=4), ALU.subtract))
            v.memset(zr, 0.0).then_inc(uv_ready, 1)
            dve.wait_ge(pt_done, 1)
            for i in range(2):
                q4 = slice(4 * i, 4 * i + 4)
                ins = v.tensor_tensor(gM[:, q4, :], gDT[:, q4, :],
                                      bank[5 + i][:, :].rearrange("p (a b) -> p a b", a=4), ALU.mult)
            ins.then_inc(pt_ready, 1)
            dve.wait_ge(u1_done, 1)
            v.tensor_tensor(gU[:, 4:8, :], gU[:, 4:8, :],
                            bank[3][:, :].rearrange("p (a b) -> p a b", a=4), ALU.subtract).then_inc(u1_ready, 1)
            dve.wait_ge(o_done, 1)
            for c in range(2):
                link(v.tensor_copy(Y2[:, c, 512:1024], bank[1 + c][:, :]))
                link(v.tensor_tensor(vTM[:, 4 * c:4 * c + 4, :].rearrange("p a b -> p (a b)"),
                                     Y2[:, c, 512:1024], Y2[:, c, 512:1024], ALU.mult))
            link(v.tensor_reduce(ms2, vTM, AX, ALU.add))
            v.memset(zr, 0.0).then_inc(y2_ms, 1)
            for h in range(MH):
                b = bank[3 + h % 2]
                dve.wait_ge(moba_s, h + 1)
                if h >= 1:
                    dve.wait_ge(moba_T, h)
                causal = const[:, CN["causal"]]
                link(v.scalar_tensor_tensor(soft[:, 0:P], b[:, 0:P], MD ** -0.5, causal, ALU.mult, ALU.add))
                link(v.tensor_scalar(soft[:, P:2 * P], b[:, P:2 * P], MD ** -0.5, None, ALU.mult))
                link(v.scalar_tensor_tensor(soft[:, 2 * P:3 * P], b[:, 2 * P:3 * P], MD ** -0.5, causal,
                                            ALU.mult, ALU.add))
                link(v.reduce_max(mx[:, 0, 0:1], soft[:, 0:P], AX))
                link(v.reduce_max(mx[:, 0, 1:2], soft[:, P:3 * P], AX))
                v.tensor_scalar(mx[:, 1, :], mx[:, 0, :], -1.0, None, ALU.mult).then_inc(moba_m, 1)
            dve.wait_ge(y2_root, 1)
            link(v.reciprocal(ms2, ms2))
            for c in range(2):
                y = Y2[:, c, 512:1024]
                y3 = y.rearrange("p (h e) -> p h e", h=GH)
                link(v.tensor_tensor(y3, y3, bc(ms2[:, 4 * c:4 * c + 4], 2, GD), ALU.mult))
                link(v.tensor_tensor(y3, y3, bc(rows[:, RW["gdn_g"]], 1, GH), ALU.mult))
                link(v.tensor_tensor(y, y, gz[:, c, :], ALU.mult))
            dve.wait_ge(moba_e, MH)
            link(v.reciprocal(rz, rz))
            dve.wait_ge(moba_y, MH)
            for t in range(NT):
                ins = v.tensor_tensor(Y2[:, t, 0:512].rearrange("p (h e) -> p h e", h=MH),
                                      bank[1 + t][:, :].rearrange("p (h e) -> p h e", h=MH),
                                      bc(rz[:, t, :], 2, MD), ALU.mult)
            ins.then_inc(mix2_ready, 1)
            for n in range(N_OUT):
                chunk_done(dve, C_OUT2 + n)
                x_ = xT[:, 2 * n:2 * n + 2, :]
                ins = v.tensor_tensor(x_, x_, bank[1 + n][:, :].rearrange("p (k t) -> p k t", k=2), ALU.add)
            ins.then_inc(x3_ready, 1)
            dve.wait_ge(rms_root, 3)
            v.memset(zero4, 0.0)
            link(v.reciprocal(rstd4, rstd4))
            link(v.tensor_tensor(h4T, xT, bc(rstd4, 1, KD), ALU.mult))
            v.tensor_tensor(h4T, h4T, bc(small[:, SM["g4"]], 2, T), ALU.mult).then_inc(h4_ready, 1)
            dve.wait_ge(route_done, 1)
            link(v.tensor_copy(logit, bank[4][:, 0:NT * (NG + NE)].rearrange("p (t e) -> p t e", t=NT)))
            link(v.memset(pad8, low))
            link(v.tensor_copy(pad8[:, :, 0:NG], logit[:, :, 0:NG]))
            for t in range(NT):
                link(v.max(gm8[:, t, :], pad8[:, t, :]))
                link(v.max_index(gi8[:, t, :], gm8[:, t, :], pad8[:, t, :]))
            link(v.tensor_copy(gif, gi8))
            iota = const[:, CN["iota"]]
            link(v.tensor_tensor(ghot, bc(iota[:, 0:NG], 1, NT), bc(gif[:, :, 0], 2, NG), ALU.is_equal))
            for t in range(NT):
                link(v.tensor_tensor(gsel[:, t], logit[:, t, NG:].rearrange("p (g e) -> p e g", g=NG),
                                     bc(ghot[:, t, :], 1, EG), ALU.mult))
            link(v.tensor_reduce(ing, gsel, AX, ALU.add))
            for t in range(NT):
                link(v.max(im8[:, t, :], ing[:, t, :]))
                link(v.max_index(ii8[:, t, :], im8[:, t, :], ing[:, t, :]))
            link(v.tensor_copy(iif, ii8))
            link(v.tensor_tensor(pw[:, :, 0], im8[:, :, 1], im8[:, :, 0], ALU.subtract))
            v.tensor_tensor(gex, logit[:, :, 0:NG], bc(gm8[:, :, 0], 2, NG), ALU.subtract).then_inc(route_exp, 1)
            dve.wait_ge(route_expd, 1)
            link(v.tensor_reduce(pw[:, :, 3], gex, AX, ALU.add))
            link(v.reciprocal(pw[:, :, 3], pw[:, :, 3]))
            link(v.tensor_scalar(pw[:, :, 2], pw[:, :, 1], 1.0, None, ALU.add))
            link(v.reciprocal(pw[:, :, 2], pw[:, :, 2]))
            link(v.tensor_tensor(pw[:, :, 2], pw[:, :, 2], pw[:, :, 3], ALU.mult))
            link(v.tensor_tensor(pw[:, :, 3], pw[:, :, 2], pw[:, :, 1], ALU.mult))
            for r in range(2):
                link(v.tensor_tensor(within[:, r], bc(iota[:, 0:EG], 1, NT), bc(iif[:, :, r], 2, EG),
                                     ALU.is_equal))
                link(v.tensor_tensor(within[:, r], within[:, r], bc(pw[:, :, 2 + r], 2, EG), ALU.mult))
            link(v.tensor_tensor(within[:, 0], within[:, 0], within[:, 1], ALU.add))
            for t in range(NT):
                ins = v.tensor_tensor(comb[:, t], bc(ghot[:, t, :], 2, EG), bc(within[:, 0, t, :], 1, NG), ALU.mult)
            ins.then_inc(comb_ready, 1)
            for i in range(1, NE // 2, 2):
                dve.wait_ge(cb_done, i + 1)
                v.tensor_copy(CB[:, 2 * i:2 * i + 2, :].rearrange("p e t -> p (e t)"), bank[6][:, :])\
                 .then_inc(cb_odd_out, 1)
            dve.wait_ge(cb_even_out, NE // 4)
            dve.wait_ge(cb_odd_out, NE // 4)
            v.memset(zr, 0.0).then_inc(gu_free, 2)
            with dve.Fori(0, NE // 2) as i:
                for b in range(2):
                    dve.wait_ge(silu_ready, 2 * i + (b + 1))
                    w = CB[:, bass.ds(2 * i + b, 1), :].to_broadcast([P, 2, T])
                    v.tensor_tensor(up[:, b], bank[5 + 2 * b][:, :].rearrange("p (f t) -> p f t", f=2), w,
                                    ALU.mult).then_inc(gu_free, 1)
                    dve.wait_ge(gu_free, 2 * i + (b + 3))
                    v.tensor_tensor(hid[:, b], up[:, b], sg[:, b], ALU.mult).then_inc(hid_ready, 1)
            dve.wait_ge(down_used, NE)
            for m in range(4):
                x_ = xT[:, 2 * m:2 * m + 2, :]
                ins = v.tensor_tensor(x_, x_, bank[m][:, :].rearrange("p (k t) -> p k t", k=2), ALU.add)
            ins.then_inc(x3_ready, 1)
            dve.wait_ge(rms_root, 4)
            link(v.reciprocal(rstd4, rstd4))
            link(v.tensor_tensor(h4T, xT, bc(rstd4, 1, KD), ALU.mult))
            v.tensor_tensor(h4T, h4T, bc(small[:, SM["g5"]], 2, T), ALU.mult).then_inc(out_ready, 1)

        @block.tensor
        def _(pe):
            mm = nc.tensor.matmul
            pe.wait_ge(const_here, 32)
            for i, s in enumerate((sq, csq)):
                pe.wait_ge(squares1, i + 1)
                for k in range(KD):
                    ins = mm(bank[7][:, i * T:(i + 1) * T], ones, s[:, k, :], start=k == 0, stop=k == KD - 1)
            ins.then_inc(sums1, 1)
            pe.wait_ge(cond_ready, 1)
            with pe.Fori(0, N_MOD // WSLOTS) as turn:
                for s in range(WSLOTS):
                    pe.wait_ge(chunk_here[s], turn * 16 + 16)
                    w = wchunk(s)
                    for j in range(2):
                        at = turn * (4 * WSLOTS) + (4 * s + 2 * j)
                        for k in range(KD):
                            ins = mm(bank[0][:, bass.ds(at, 2)], w[:, k, j * P:(j + 1) * P], condS[:, k, :],
                                     start=k == 0, stop=k == KD - 1)
                    ins.then_inc(chunk_used, 1)
            pe.wait_ge(h_ready, 1)
            n_c = 0
            for n in range(N_IN1):
                chunk_ready(pe, C_IN1 + n)
                w = wchunk(C_IN1 + n)
                if n >= 2:
                    pe.wait_ge(proj_x_out, n - 1)
                groups = [(bank[1 + 2 * (n % 2)], hT)]
                if n in CTX_CHUNKS:
                    n_c += 1
                    if n_c >= 2:
                        pe.wait_ge(proj_c_out, n_c - 1)
                    groups.append((bank[2 + 2 * (n % 2)], chT))
                for out, h in groups:
                    for t in range(NT):
                        for k in range(KD):
                            ins = mm(out[:, t * COLS:(t + 1) * COLS], h[:, k, t * P:(t + 1) * P],
                                     w[:, k, :], start=k == 0, stop=k == KD - 1)
                ins.then_inc(chunk_used, 1)
            pe.wait_ge(roped, 1)
            sources = [(proj, 0), (proj, 256), (cproj, 0)]
            sources += [(proj, 1536 + 256 * i) for i in range(4)] + [(cproj, 768 + 256 * i) for i in range(2)]
            for i, (src, at) in enumerate(sources):
                if i >= 2:
                    pe.wait_ge(turned_out, i - 1)
                for b in range(2):
                    for t in range(NT):
                        ins = nc.tensor.transpose(bank[5 + i % 2][:, b * T + t * P:b * T + (t + 1) * P],
                                                  src[:, t, at + b * P:at + (b + 1) * P], ident)
                ins.then_inc(turned, 1)
            pe.wait_ge(turned_out, len(sources))

            def scores(h):
                r = slice(RK * (h % 2), RK * (h % 2) + RK)
                if h >= 2:
                    pe.wait_ge(ret_masked, h - 1)
                for k in range(4):
                    ins = mm(bank[1 + 2 * (h % 2) + k // 2][:, (k % 2) * T:(k % 2 + 1) * T],
                             rkT[r, h // 2, k * P:(k + 1) * P], rqT[r, h // 2, :], start=True, stop=True)
                ins.then_inc(ret_scores, 1)

            def outputs(h):
                pe.wait_ge(ret_masked, h + 1)
                for t in range(NT):
                    for k in range(4):
                        val = cproj[:, k, 256 + h * RV:256 + (h + 1) * RV] if k < 2 else \
                            proj[:, k - 2, 512 + h * RV:512 + (h + 1) * RV]
                        ins = mm(bank[(0, 7)[h // 2]][:, (h % 2) * 256 + t * P:(h % 2) * 256 + (t + 1) * P],
                                 SD[:, h % 2, k, t * P:(t + 1) * P], val, start=k == 0, stop=k == 3)
                ins.then_inc(ret_y, 1)

            scores(0)
            for h in range(RH):
                if h + 1 < RH:
                    scores(h + 1)
                outputs(h)

            def diff_scores_of(i):
                h, t = i // NT, i % NT
                if i >= 2:
                    pe.wait_ge(diff_exp, 2 * i - 2)
                for c in range(2):
                    r = slice(DD * c, DD * (c + 1))
                    mm(bank[1 + 2 * (i % 2) + c][:, :], dqT[r, h, t * P:(t + 1) * P], dkT[r, h, :],
                       start=True, stop=True).then_inc(diff_scores, 1)

            def diff_outputs_of(i):
                h, t = i // NT, i % NT
                pe.wait_ge(diff_a, i + 1)
                if i >= 2:
                    pe.wait_ge(diff_aT_out, i - 1)
                for k in range(4):
                    ins = nc.tensor.transpose(bank[5 + i % 2][:, k * P:(k + 1) * P],
                                              tmp[:, 0, k * P:(k + 1) * P], ident)
                ins.then_inc(diff_aT, 1)
                pe.wait_ge(diff_aT_out, i + 1)
                if h % 2 == 0 and t == 0:
                    pe.wait_ge(ret_y_out, h // 2 + 1)
                for k in range(4):
                    val = cproj[:, k, 1280 + h * RV:1280 + (h + 1) * RV] if k < 2 else \
                        proj[:, k - 2, 2560 + h * RV:2560 + (h + 1) * RV]
                    ins = mm(bank[(0, 7)[h // 2]][:, (h % 2) * 256 + t * P:(h % 2) * 256 + (t + 1) * P],
                             aT[:, i % 2, k, :], val, start=k == 0, stop=k == 3)
                ins.then_inc(diff_y, 1)

            pe.wait_ge(ret_masked, RH)
            diff_scores_of(0)
            for i in range(DH * NT):
                if i + 1 < DH * NT:
                    diff_scores_of(i + 1)
                diff_outputs_of(i)
            pe.wait_ge(mix_ready, NT)
            for g in range(4):
                if g >= 2:
                    pe.wait_ge(mixT_out, g - 1)
                for b in range(2):
                    for t in range(NT):
                        ins = nc.tensor.transpose(bank[5 + g % 2][:, b * T + t * P:b * T + (t + 1) * P],
                                                  Y[:, t, (2 * g + b) * P:(2 * g + b + 1) * P], ident)
                ins.then_inc(mixT_done, 1)
            pe.wait_ge(mixT_out, 4)
            project_fm(pe, C_OUT1, N_OUT, mixT)
            sums_over_features(pe, sq2, 1)
            pe.wait_ge(h2_ready, 1)
            for n in range(N_Q):
                if n >= 4:
                    pe.wait_ge(q_out, n - 3)
                project_fm(pe, C_Q + n, 1, h2T, at=n)
            for g in range(4):
                if g >= 2:
                    pe.wait_ge(h2_out, g - 1)
                t = g // 2
                transposes(pe, bank[5 + g % 2], [h2T[:, 4 * (g % 2) + k, t * P:(t + 1) * P] for k in range(4)])\
                    .then_inc(h2_done, 1)
            pe.wait_ge(q_out, N_Q)
            chunk_ready(pe, C_SK)
            s_ = C_SK % WSLOTS
            keys = wring[:, s_ * CHUNK:(s_ + 1) * CHUNK].rearrange("p (h n) -> p h n", h=2 * PH)
            for i in range(2 * NT):
                t = i // 2
                if i >= 2:
                    pe.wait_ge(keys_out, i - 1)
                for q in range(8):
                    hp = 8 * (i % 2) + q
                    ins = mm(bank[(1, 3)[i % 2] + q // 4][:, (q % 4) * P:(q % 4 + 1) * P],
                             qT[:, hp, t * P:(t + 1) * P], keys[:, hp, :], start=True, stop=True)
                ins.then_inc(keys_done if i < 2 * NT - 1 else chunk_used, 1)
            pe.wait_ge(keys_out, 2 * NT)
            pe.wait_ge(zero_set, 1)
            for b in range(1, 5):
                mm(bank[b][:, :], zeros[:, 0:P], zeros, start=True, stop=False, skip_group_check=True)
            for t in range(NT):
                with pe.Fori(0, SLOTS // GS) as turn:
                    for j in range(GS):
                        pe.wait_ge(diag_ready, turn * GS + (t * SLOTS + j + 1))
                        for c in range(2):
                            ins = mm(bank[1 + 2 * t + c][:, :], diag[:, j, :],
                                     G[:, j, D + c * 512:D + (c + 1) * 512], start=False, stop=False,
                                     skip_group_check=True)
                        ins.then_inc(slot_used, 1)
                pe.wait_ge(ffn_out, t + 1)
                for i in range(2):
                    transposes(pe, bank[5 + i], [ffn[:, (4 * i + k) * P:(4 * i + k + 1) * P] for k in range(4)])\
                        .then_inc(ffnT_done, 1)
            sums_over_features(pe, sq3, 2)
            pe.wait_ge(h3_ready, 1)
            pe.wait_ge(masks_here, 32)
            for t in range(NT):
                for k in range(KD):
                    ins = mm(bank[5][:, t * 8:(t + 1) * 8], h3T[:, k, t * P:(t + 1) * P], gate2[:, k, :],
                             start=k == 0, stop=k == KD - 1)
            ins.then_inc(ab_done, 1)
            for n in range(N_IN2):
                if n >= 4:
                    pe.wait_ge(in2_out, n - 3)
                if n in (4, 5, 12, 13):
                    chunk_ready(pe, C_IN2 + n)
                    for t in range(NT):
                        for k in range(KD):
                            ins = mm(bank[1 + n % 4][:, t * COLS:(t + 1) * COLS], h3T[:, k, t * P:(t + 1) * P],
                                     wchunk(C_IN2 + n)[:, k, :], start=k == 0, stop=k == KD - 1)
                    ins.then_inc(chunk_used, 1)
                else:
                    project_fm(pe, C_IN2 + n, 1, h3T, at=n)
            pe.wait_ge(lnorm_sq, 1)
            pe.wait_ge(in2_out, N_IN2)
            for i in range(4):
                ins = mm(bank[1 + i][:, :], ones, nsq[:, 2 * i:2 * i + 2, :].rearrange("p a b -> p (a b)"),
                         start=True, stop=True)
            ins.then_inc(lnorm_sum, 1)
            pe.wait_ge(g_ready, 1)
            mm(bank[7][:, 0:8], const[:, CN["upper"]], g8, start=True, stop=True)
            for p in range(8):
                ins = mm(bank[5 + p // 4][:, (p % 4) * P:(p % 4 + 1) * P], bc(g8[:, p], 1, P),
                         const[:, CN["upper"]], start=True, stop=True)
            ins.then_inc(g_done, 1)
            pe.wait_ge(lnorm_done, 1)
            for p in range(8):
                c, h = p // 4, p % 4
                kT = cvT[:, 4 + h, c * P:(c + 1) * P]
                ins = mm(bank[3 + p // 4][:, (p % 4) * P:(p % 4 + 1) * P], kT, kT, start=True, stop=True)
            ins.then_inc(kk_done, 1)
            pe.wait_ge(g_done, 2)
            for i in range(2):
                for c in range(2):
                    if i:
                        pe.wait_ge(tm_out, c + 1)
                    transposes(pe, bank[5 + c], [cvT[:, 4 + 4 * i + h, c * P:(c + 1) * P] for h in range(4)])\
                        .then_inc(tm_done, 1)
            pe.wait_ge(a_ready, 1)
            pe.wait_ge(tm_out, 4)
            for i in range(2):
                ins = transposes(pe, bank[5 + i], [gA[:, 4 * i + k, :] for k in range(4)])
            ins.then_inc(at_done, 1)
            pe.wait_ge(at_out, 1)
            for s in range(1, LEVELS):
                pe.wait_ge(level_ready, s)
                for p in range(8):
                    ins = mm(bank[1 + p // 4][:, (p % 4) * P:(p % 4 + 1) * P], gMT[:, p, :], gT_[:, p, :],
                             start=True, stop=True)
                ins.then_inc(w_done, 1)
                pe.wait_ge(w_out, s)
                for p in range(8):
                    mm(bank[3 + p // 4][:, (p % 4) * P:(p % 4 + 1) * P], gTT[:, p, :], gW[:, p, :],
                       start=True, stop=True)
                    ins = mm(bank[5 + p // 4][:, (p % 4) * P:(p % 4 + 1) * P], gW[:, p, :], gTT[:, p, :],
                             start=True, stop=True)
                ins.then_inc(t_done, 1)
            pe.wait_ge(uv_ready, 1)
            for p in range(8):
                mm(bank[1 + p // 4][:, (p % 4) * P:(p % 4 + 1) * P], gTT[:, p, :], vTM[:, p, :],
                   start=True, stop=True)
            for h in range(GH):
                ins = mm(bank[3][:, h * P:(h + 1) * P], gD[:, 4 + h, :], gTT[:, 4 + h, :], start=True, stop=True)
            ins.then_inc(uv_done, 1)
            for p in range(8):
                c, h = p // 4, p % 4
                ins = mm(bank[5 + p // 4][:, (p % 4) * P:(p % 4 + 1) * P], cvT[:, 4 + h, c * P:(c + 1) * P],
                         cvT[:, h, c * P:(c + 1) * P], start=True, stop=True)
            ins.then_inc(pt_done, 1)
            pe.wait_ge(uv_out, 1)
            for h in range(GH):
                ins = mm(bank[4][:, h * P:(h + 1) * P], gD[:, h, :], gU[:, h, :], start=True, stop=True)
            ins.then_inc(s_done, 1)
            pe.wait_ge(s_out, 1)
            for h in range(GH):
                ins = mm(bank[3][:, h * P:(h + 1) * P], gwT[:, h, :], gS[:, h, :], start=True, stop=True)
            ins.then_inc(u1_done, 1)
            pe.wait_ge(pt_ready, 1)
            pe.wait_ge(u1_ready, 1)
            for p in range(8):
                out = bank[1 + p // 4][:, (p % 4) * P:(p % 4 + 1) * P]
                ins = mm(out, gM[:, p, :], gU[:, p, :], start=True, stop=p < 4)
                if p >= 4:
                    ins = mm(out, gR[:, p, :], gS[:, p - 4, :], start=False, stop=True)
            ins.then_inc(o_done, 1)

            def moba_scores(h):
                r = slice(MD * (h % 2), MD * (h % 2) + MD)
                if h >= 2:
                    pe.wait_ge(moba_m, h - 1)
                mm(bank[3 + h % 2][:, 0:P], mqT[r, h // 2, 0:P], mkT[r, h // 2, 0:P], start=True, stop=True)
                mm(bank[3 + h % 2][:, P:3 * P], mqT[r, h // 2, P:2 * P], mkT[r, h // 2, :],
                   start=True, stop=True).then_inc(moba_s, 1)

            pe.wait_ge(y2_ms, 1)
            moba_scores(0)
            for h in range(MH):
                if h + 1 < MH:
                    moba_scores(h + 1)
                pe.wait_ge(moba_e, h + 1)
                if h >= 1:
                    pe.wait_ge(moba_T_out, h)
                transposes(pe, bank[7], [soft[:, k * P:(k + 1) * P] for k in range(3)]).then_inc(moba_T, 1)
                pe.wait_ge(moba_T_out, h + 1)
                cols = slice(h * MD, (h + 1) * MD)
                mm(bank[1][:, cols], softT[:, 0:P], mv[:, 0, cols], start=True, stop=True)
                for k in range(2):
                    ins = mm(bank[2][:, cols], softT[:, (1 + k) * P:(2 + k) * P], mv[:, k, cols],
                             start=k == 0, stop=k == 1)
                ins.then_inc(moba_y, 1)
            pe.wait_ge(mix2_ready, 1)
            for g in range(4):
                if g >= 2:
                    pe.wait_ge(mixT_out, 4 + g - 1)
                transposes(pe, bank[5 + g % 2], [Y2[:, t, (2 * g + b) * P:(2 * g + b + 1) * P]
                                                 for b in range(2) for t in range(NT)]).then_inc(mixT_done, 1)
            pe.wait_ge(mixT_out, 8)
            project_fm(pe, C_OUT2, N_OUT, mix2T)
            sums_over_features(pe, sq4, 3)
            pe.wait_ge(h4_ready, 1)
            pe.wait_ge(route_here, 16)
            for t in range(NT):
                for k in range(KD):
                    ins = mm(bank[4][:, t * (NG + NE):(t + 1) * (NG + NE)], h4T[:, k, t * P:(t + 1) * P],
                             routeW[:, k, :], start=k == 0, stop=k == KD - 1)
            ins.then_inc(route_done, 1)
            for b in range(4):
                mm(bank[b][:, :], zero4[:, 0:P], zero4, start=True, stop=False, skip_group_check=True)
            pe.wait_ge(comb_ready, 1)
            for i in range(NE // 2):
                if i >= 2:
                    pe.wait_ge((cb_even_out, cb_odd_out)[i % 2], i // 2)
                for j in range(2):
                    e = 2 * i + j
                    for t in range(NT):
                        ins = mm(bank[4 + 2 * (i % 2)][:, j * T + t * P:j * T + (t + 1) * P],
                                 bc(comb[:, t, e // EG, e % EG], 1, P), ident, start=True, stop=True)
                ins.then_inc(cb_done, 1)

            def gate_up(b, turn):
                pe.wait_ge(gu_here[b], turn * 16 + 16)
                pe.wait_ge(gu_free, turn * 2 + (b + 1))
                w = wring[:, 2 * b * CHUNK:(2 * b + 2) * CHUNK].rearrange("p (a k f) -> p a k f", a=2, k=KD)
                for a in range(2):
                    for f in range(2):
                        for k in range(KD):
                            ins = mm(bank[4 + 2 * b + a][:, f * T:(f + 1) * T], w[:, a, k, f * P:(f + 1) * P],
                                     h4T[:, k, :], start=k == 0, stop=k == KD - 1)
                ins.then_inc(gu_done, 1)

            def down(b, turn):
                pe.wait_ge(down_here[b], turn * 16 + 16)
                pe.wait_ge(hid_ready, turn * 2 + (b + 1))
                w = wring[:, (4 + b) * CHUNK:(5 + b) * CHUNK].rearrange("p (f c) -> p f c", f=2)
                for m in range(KD):
                    for f in range(2):
                        ins = mm(bank[m // 2][:, (m % 2) * T:(m % 2 + 1) * T], w[:, f, m * P:(m + 1) * P],
                                 hid[:, b, f, :], start=False, stop=False, skip_group_check=True)
                ins.then_inc(down_used, 1)

            gate_up(0, 0)
            with pe.Fori(0, NE // 2 - 1) as turn:
                gate_up(1, turn)
                down(0, turn)
                gate_up(0, turn + 1)
                down(1, turn)
            gate_up(1, NE // 2 - 1)
            down(0, NE // 2 - 1)
            down(1, NE // 2 - 1)
            sums_over_features(pe, sq4, 4)


CTX_CHUNKS = (1, 2, 3, 8, 9, 10, 11)


def turned_views(rqT, rkT, dqT, dkT):
    out = [rqT, rkT[:, :, T:2 * T], rkT[:, :, 0:T]]
    out += [dqT[:, 2 * i:2 * i + 2, :] for i in range(2)]
    out += [dkT[:, 2 * i:2 * i + 2, T:2 * T] for i in range(2)]
    out += [dkT[:, 2 * i:2 * i + 2, 0:T] for i in range(2)]
    return out


def constants():
    c = np.zeros((P, CN_N), np.float32)
    p = np.arange(P)
    c[:, CN["ident"]] = np.eye(P)
    c[:, CN["ones"]] = 1.0
    c[:, CN["eps"]] = EPS
    quarter = RK // 4
    freqs = (10000.0 ** (-np.arange(quarter, dtype=np.float32) / quarter)).astype(np.float32)
    t = np.arange(T)
    ar = (t // 64).astype(np.float32)[:, None] * freqs
    ac = (t % 64).astype(np.float32)[:, None] * freqs
    ang = np.concatenate([ar, ar, ac, ac], axis=1).astype(np.float64)
    sign = np.tile(np.repeat([-1.0, 1.0], quarter), 2)
    c[:, CN["cos"]] = np.cos(ang).reshape(NT, P, RK).transpose(1, 0, 2).reshape(P, -1)
    c[:, CN["sin"]] = (np.sin(ang) * sign).reshape(NT, P, RK).transpose(1, 0, 2).reshape(P, -1)
    dist = t[None, None, :] - (np.arange(NT)[None, :, None] * P + p[:, None, None])
    c[:, CN["dist"]] = dist.reshape(P, -1)
    c[:, CN["iota"]] = np.arange(TOPK)
    c[:, CN["upper"]] = p[:, None] <= p[None, :]
    c[:, CN["lower"]] = p[:, None] >= p[None, :]
    c[:, CN["causal"]] = np.where(p[:, None] >= p[None, :], 0.0, -1e30)
    masks = np.zeros((2, LEVELS, P, P), np.float32)
    for s in range(LEVELS):
        w = 1 << s
        low = (p[:, None] // w == p[None, :] // w + 1) & (p[:, None] // (2 * w) == p[None, :] // (2 * w))
        masks[0, s], masks[1, s] = low, low.T
    return c, np.ascontiguousarray(masks.transpose(2, 0, 1, 3)).reshape(P, -1)


def pack(w):
    n = w.shape[1] // COLS
    return w.reshape(KD, P, n, COLS).transpose(2, 1, 0, 3).reshape(n, P, CHUNK)


def fm(a, n):
    return a.reshape(n, P).T


def kernel(**inputs):
    import concourse.bacc as bacc
    from concourse.bass_utils import run_bass_kernel_spmd

    g = {k: np.asarray(a) for k, a in inputs.items()}
    cond = np.stack([g["c"][0], g["c_ctx"]], axis=-1).reshape(KD, P, 2).transpose(1, 0, 2).reshape(P, -1)
    conv = g["conv_w_2"][0].reshape(CONV, 12, P).transpose(2, 1, 0).reshape(P, -1)
    small = np.concatenate([cond, fm(g["b_mod"], 6 * KD), fm(g["norm1_g"], KD), fm(g["norm2_g"], KD),
                            fm(g["attn_norm_2"], KD), fm(g["ffn_norm_2"], KD), fm(g["final_norm_2"], KD),
                            conv], axis=1)
    row = np.concatenate([g[k].reshape(-1) for k in
                          ("ret_norm_g", "diff_norm_g", "diff_qk_norm_g", "diff_lambda", "ret_decay_logit",
                           "gdn_norm_2", "A_log_2", "dt_bias_2")])
    const, masks = constants()
    keys = g["peer_sub_keys"][0].reshape(2 * PH, NK, P).transpose(2, 0, 1).reshape(1, P, CHUNK)
    w2 = g["w_in_2"][0]
    stream = np.concatenate([pack(g["w_mod"][0]), pack(g["w_in"][0]), pack(g["w_out"][0]),
                             pack(g["peer_w_query"][0]), keys, pack(w2[:, :3584]), pack(g["w_out_2"][0])])
    fold = lambda w: w.reshape(KD, P, -1).transpose(1, 0, 2)
    gate_up = np.stack([g["w_gate_2"][0].reshape(NE, KD, P, FF), g["w_up_2"][0].reshape(NE, KD, P, FF)], axis=1)
    gate_up = gate_up.transpose(0, 3, 1, 2, 4).reshape(NE, P, 2 * CHUNK)
    down = g["w_down_2"][0].reshape(NE, FF // P, P, D).transpose(0, 2, 1, 3).reshape(NE, P, CHUNK)
    tokens = lambda x: fold(x[0].T)
    arrays = {
        "xT": tokens(g["x"]), "ctxT": tokens(g["ctx"]), "small": small,
        "rows": np.broadcast_to(row, (P, RW_N)), "const": const, "masks": masks, "stream": stream,
        "gate2": fold(w2[:, 3584:]).reshape(P, -1),
        "uv": np.concatenate([g["peer_u"][0], g["peer_v"][0]], axis=1),
        "route": fold(np.concatenate([g["w_group_2"][0], g["w_router_2"][0]], axis=1)).reshape(P, -1),
        "moe": np.concatenate([gate_up, down], axis=2),
    }
    arrays = {k: np.ascontiguousarray(a) for k, a in arrays.items()}
    nc = bacc.Bacc("TRN2", target_bir_lowering=False, num_devices=1)
    args = [nc.dram_tensor(f"{k}_in", a.shape, fp32, kind="ExternalInput").ap() for k, a in arrays.items()]
    out = nc.dram_tensor("out_dram", (P, KD, T), fp32, kind="ExternalOutput").ap()
    two_blocks(nc, *args, out)
    r = run_bass_kernel_spmd(nc, [{f"{k}_in": a for k, a in arrays.items()}], core_ids=[0])
    return r.results[0]["out_dram"].transpose(2, 1, 0).reshape(1, T, D)
```

```python
from contextlib import ExitStack

import numpy as np
import concourse.bass as bass
from concourse import mybir

P = 128
D = 1024
T = 256
NT = T // P
KD = D // P
EPS = 1e-6
RH, RK, RV = 4, 64, 128
DH, DD = 4, 64
IN1 = 3072
PH, NK, TOPK = 8, 128, 16
SLOTS = PH * TOPK
MH, MD = 8, 64
GH, GD = 4, 128
CONV = 4
NG, EG, FF = 4, 8, 256
NE = NG * EG
LAM_INIT = 0.2

CHUNK = 2048
COLS = CHUNK // KD
N_MOD = 6 * D // COLS
N_IN1 = IN1 // COLS
N_OUT = D // COLS
N_Q = 2 * PH * NK // COLS
N_SK = 1
N_IN2 = 3584 // COLS
C_MOD = 0
C_IN1 = C_MOD + N_MOD
C_OUT1 = C_IN1 + N_IN1
C_Q = C_OUT1 + N_OUT
C_SK = C_Q + N_Q
C_IN2 = C_SK + N_SK
C_OUT2 = C_IN2 + N_IN2
N_CHUNKS = C_OUT2 + N_OUT
WSLOTS = 8

SM = {}
_at = 0
for _name, _n in [("cond", 16), ("b_mod", 48), ("g1", 8), ("g2", 8), ("g3", 8), ("g4", 8), ("g5", 8),
                  ("conv", 48)]:
    SM[_name] = slice(_at, _at + _n)
    _at += _n
SM_N = _at
RW = {}
_at = 0
for _name, _n in [("ret_g", 512), ("diff_g", 512), ("qk_g", 128), ("lam", 256), ("decay", 8),
                  ("gdn_g", 128), ("A_log", 4), ("dt", 4)]:
    RW[_name] = slice(_at, _at + _n)
    _at += _n
RW_N = _at
CN = {}
_at = 0
for _name, _n in [("ident", 128), ("ones", 128), ("cos", NT * 64), ("sin", NT * 64), ("dist", NT * T),
                  ("iota", 16), ("eps", 1), ("upper", 128), ("lower", 128), ("causal", 128)]:
    CN[_name] = slice(_at, _at + _n)
    _at += _n
CN_N = _at
ARENA = 28928
WINDOWS = T // P
PAIRS = NE // 2
NONE = 4096
LEVELS = 7

fp32 = mybir.dt.float32
bf16 = mybir.dt.bfloat16
u32 = mybir.dt.uint32
ALU = mybir.AluOpType
ACT = mybir.ActivationFunctionType
AX = mybir.AxisListType.X


class Carve:

    def __init__(self, tensor, at=0):
        self.tensor, self.at = tensor, at

    def take(self, *dims, dt=fp32):
        n = int(np.prod(dims))
        ap = self.tensor[:, self.at:self.at + n]
        self.at += n
        if dt is not fp32:
            ap = ap.bitcast(dt)
        if len(dims) > 1:
            names = "abcd"[:len(dims)]
            ap = ap.rearrange(f"p ({' '.join(names)}) -> p {' '.join(names)}",
                              **dict(zip(names, dims)))
        return ap


def bc(ap, axis, n):
    shape = list(ap.shape)
    shape.insert(axis, n)
    return ap.unsqueeze(axis).to_broadcast(shape)


def last_chunk_in(slot, before):
    return max(n for n in range(before) if n % WSLOTS == slot)


def two_blocks(nc, xT_d, ctxT_d, small_d, rows_d, const_d, masks_d, wstream_d, gate2_d, uv_d, route_d,
               moe_d, final_g_d, out_d, h4_d, y4_d):
    ctx = ExitStack()
    with ctx:
        def sb(name, n, dt=fp32):
            return ctx.enter_context(nc.sbuf_tensor(name, [P, n], dt))

        def sem(name):
            return ctx.enter_context(nc.semaphore(name))

        wring = sb("wring", WSLOTS * CHUNK)
        arena = sb("arena", ARENA)
        xT = sb("xT", KD * T)[:, :].rearrange("p (k t) -> p k t", k=KD)
        small = sb("small", SM_N)
        rows = sb("rows", RW_N)
        const = sb("const", CN_N)
        tiny = Carve(sb("tiny", 1024))
        bank = [ctx.enter_context(nc.psum_tensor(f"bank{i}", [P, 512], fp32)) for i in range(8)]

        ident, ones, epsc = const[:, CN["ident"]], const[:, CN["ones"]], const[:, CN["eps"]]

        def wchunk(n):
            s = n % WSLOTS
            return wring[:, s * CHUNK:(s + 1) * CHUNK].rearrange("p (k c) -> p k c", k=KD)

        condS = tiny.take(KD, 2)
        modv = tiny.take(6 * KD, 2)
        scale1 = tiny.take(2, KD)
        scale2 = tiny.take(KD)
        lg = tiny.take(8)
        lgL = tiny.take(8)
        nlg = tiny.take(8)
        lt = tiny.take(6, 8)
        lamt = tiny.take(2, 64)
        lam2 = tiny.take(4)
        ss = tiny.take(48)
        sr = tiny.take(48)
        zm = tiny.take(2, 2)
        zz = tiny.take(2, 2)
        zr = tiny.take(2, 2)

        m1 = Carve(arena)
        proj = m1.take(NT, IN1)
        cproj = m1.take(NT, 1792)
        hT = m1.take(KD, T)
        chT = m1.take(KD, T)
        tmp = m1.take(2, 1024)
        rqT = m1.take(2, T)
        rkT = m1.take(2, 2 * T)
        dqT = m1.take(4, T)
        dkT = m1.take(4, 2 * T)
        SD = m1.take(2, 4, T)
        DC = m1.take(2, 4, T)
        prob = m1.take(2, 2 * T)
        aT = m1.take(2, 4, P)
        Y = m1.take(NT, D)
        mixT = chT
        assert m1.at <= ARENA
        sq = tmp.rearrange("p a b -> p (a b)").rearrange("p (k t) -> p k t", k=KD)
        csq = Y.rearrange("p a b -> p (a b)").rearrange("p (k t) -> p k t", k=KD)
        rstd = prob[:, 0, :].rearrange("p (a t) -> p a t", a=2)

        GS = 8
        m2 = Carve(arena)
        G = m2.take(GS, 2 * D)
        early = Carve(arena)
        h2T = early.take(KD, T)
        sq2 = early.take(KD, T)
        qT = early.take(2 * PH, T)
        rstd2 = early.take(T)
        h2 = m2.take(NT, D)
        keyS = m2.take(NT, 2 * PH, NK)
        cand = m2.take(PH, TOPK * TOPK)
        hot = m2.take(SLOTS, TOPK)
        topv = m2.take(PH, 2, TOPK)
        topi = m2.take(PH, 2, TOPK, dt=u32)
        topf = m2.take(PH, 2, TOPK)
        pos = m2.take(SLOTS, dt=u32)
        posu = m2.take(2, SLOTS, dt=u32)
        posf = m2.take(2, SLOTS)
        chosen = m2.take(2, SLOTS)
        expert = m2.take(NT, SLOTS, dt=u32)
        gates = m2.take(NT, SLOTS)
        gsum = m2.take(PH)
        stage = m2.take(GS, dt=u32)
        dots = m2.take(2, 4)
        gelu = m2.take(2, 4)
        weight = m2.take(2, 4)
        assert m2.at <= ARENA
        diag = keyS[:, 0, 0:GS, :]
        zeros = hot.rearrange("p a b -> p (a b)")[:, 0:512]
        junk = cand.rearrange("p (c a) b -> p c (a b)", c=2)
        ffn = junk[:, 0, :]

        m3 = Carve(arena)
        h3T = m3.take(KD, T)
        sq3 = m3.take(KD, T)
        cvin = m3.take(12, CONV - 1 + T)
        rstd3 = m3.take(T)
        assert m3.at <= 8192
        late = Carve(arena)
        gD, gDT, gA, gAT, gT_, gTT, gM, gMT = (late.take(8, P) for _ in range(8))
        m3 = Carve(arena, late.at)
        mqT = m3.take(4, T)
        mkT = m3.take(4, T)
        mv = m3.take(NT, 512)
        gz = m3.take(NT, 512)
        cvT = m3.take(12, T)
        masks = m3.take(2, LEVELS, P)
        gate2 = m3.take(KD, 8)
        kTM = m3.take(8, P)
        vTM = m3.take(8, P)
        gW = m3.take(8, P)
        gR = m3.take(8, P)
        gU = m3.take(8, P)
        gS = m3.take(4, P)
        gwT = m3.take(4, P)
        soft = m3.take(384)
        softT = m3.take(384)
        Y2 = m3.take(NT, D)
        ab = m3.take(2, NT, 4)
        spt = m3.take(5, 8)
        g8 = m3.take(8)
        beta = m3.take(8)
        bg = m3.take(8)
        kd = m3.take(8)
        gc = m3.take(8)
        egc = m3.take(8)
        rz = m3.take(NT, MH)
        mx = m3.take(2, 2)
        ms2 = m3.take(8)
        assert m3.at <= ARENA
        nsq = Carve(arena, 6 * 1024).take(8, T)
        nrm = Carve(arena, 2 * 1024).take(8, T)
        mix2T = cvT[:, 0:KD, :]

        m4 = Carve(arena)
        h4T = m4.take(KD, T)
        sq4 = m4.take(KD, T)
        rstd4 = m4.take(T)
        routeW = m4.take(KD, NG + NE)
        h4 = m4.take(NT, D)
        x3 = m4.take(NT, D)
        X = m4.take(2, D)
        XT = m4.take(2, KD, P)
        hid = m4.take(2, FF)
        hidT = m4.take(2, 2, P)
        sg = m4.take(2, FF)
        Yx = m4.take(2, D)
        hot4 = m4.take(NT + 1, NE * P // 2).bitcast(bf16)\
                 .rearrange("p a (e s) -> p a e s", e=NE)
        final_g = m4.take(D)
        slot_no = m4.take(WINDOWS, P)
        token_no = m4.take(NT)
        rank_in = m4.take(NT, NE)
        rank = m4.take(NT, NE)
        tags = m4.take(NT, NE)
        tags = tags.bitcast(bf16).rearrange("p t (e a) -> p t e a", a=2)
        slotv = m4.take(WINDOWS * NE, 2)
        absent = m4.take(WINDOWS * NE)
        from_row = m4.take(WINDOWS * NE + 2, dt=u32)
        to_row = m4.take(WINDOWS * NE + 2, dt=u32)
        stage4 = m4.take(4, dt=u32)
        most = m4.take(2)
        pairs = m4.take(1, dt=u32)
        ms4 = m4.take(NT)
        logit = m4.take(NT, NG + NE)
        pad8 = m4.take(NT, 8)
        gm8 = m4.take(NT, 8)
        gi8 = m4.take(NT, 8, dt=u32)
        gif = m4.take(NT, 8)
        ghot = m4.take(NT, NG)
        gex = m4.take(NT, NG)
        gsel = m4.take(NT, 8, NG)
        ing = m4.take(NT, 8)
        im8 = m4.take(NT, 8)
        ii8 = m4.take(NT, 8, dt=u32)
        iif = m4.take(NT, 8)
        pw = m4.take(NT, 4)
        within = m4.take(2, NT, 8)
        assert m4.at <= ARENA
        back = Carve(arena).take(NT, 2, D)

        chunk_here = [sem(f"chunk_here{i}") for i in range(WSLOTS)]
        chunk_used = sem("chunk_used")
        x_here = sem("x_here")
        small_here = sem("small_here")
        const_here = sem("const_here")
        act_step = sem("act_step")
        dve_step = sem("dve_step")
        cond_ready = sem("cond_ready")
        squares1 = sem("squares1")
        sums1 = sem("sums1")
        root1 = sem("root1")
        h_ready = sem("h_ready")
        proj_x_out = sem("proj_x_out")
        proj_c_out = sem("proj_c_out")
        qk_sq = sem("qk_sq")
        qk_root = sem("qk_root")
        roped = sem("roped")
        turned = sem("turned")
        turned_out = sem("turned_out")
        gam_e = sem("gam_e")
        gam_ready = sem("gam_ready")
        decay_args = sem("decay_args")
        decay_ready = sem("decay_ready")
        ret_scores = sem("ret_scores")
        ret_masked = sem("ret_masked")
        ret_y = sem("ret_y")
        ret_y_out = sem("ret_y_out")
        lam_dots = sem("lam_dots")
        lam_exp = sem("lam_exp")
        diff_scores = sem("diff_scores")
        diff_max = sem("diff_max")
        diff_exp = sem("diff_exp")
        diff_a = sem("diff_a")
        diff_aT = sem("diff_aT")
        diff_aT_out = sem("diff_aT_out")
        diff_y = sem("diff_y")
        y_ms = sem("y_ms")
        y_root = sem("y_root")
        mix_ready = sem("mix_ready")
        mixT_done = sem("mixT_done")
        mixT_out = sem("mixT_out")

        rms_sq = sem("rms_sq")
        rms_sum = sem("rms_sum")
        rms_root = sem("rms_root")
        h2_ready = sem("h2_ready")
        q_out = sem("q_out")
        keys_done = sem("keys_done")
        keys_out = sem("keys_out")
        tokens_turned = sem("tokens_turned")
        tokens_out = sem("tokens_out")
        top_exp = sem("top_exp")
        top_expd = sem("top_expd")
        top_ready = sem("top_ready")
        idx_staged = sem("idx_staged")
        dot_done = sem("dot_done")
        gelu_step = sem("gelu_step")
        diag_ready = sem("diag_ready")
        slot_used = sem("slot_used")
        zero_set = sem("zero_set")
        ffn_out = sem("ffn_out")
        ffnT_done = sem("ffnT_done")
        x2_ready = sem("x2_ready")
        h3_ready = sem("h3_ready")
        masks_here = sem("masks_here")
        in2_out = sem("in2_out")
        ab_done = sem("ab_done")
        ab_exp = sem("ab_exp")
        ab_expd = sem("ab_expd")
        conv_ready = sem("conv_ready")
        conv_silu = sem("conv_silu")
        lnorm_sq = sem("lnorm_sq")
        lnorm_sum = sem("lnorm_sum")
        lnorm_root = sem("lnorm_root")
        lnorm_done = sem("lnorm_done")
        tm_done = sem("tm_done")
        tm_out = sem("tm_out")
        g_ready = sem("g_ready")
        g_done = sem("g_done")
        gx_ready = sem("gx_ready")
        gx_exp = sem("gx_exp")
        kk_done = sem("kk_done")
        a_ready = sem("a_ready")
        at_done = sem("at_done")
        at_out = sem("at_out")
        level_ready = sem("level_ready")
        w_done = sem("w_done")
        w_out = sem("w_out")
        t_done = sem("t_done")
        uv_ready = sem("uv_ready")
        uv_done = sem("uv_done")
        uv_out = sem("uv_out")
        s_done = sem("s_done")
        s_out = sem("s_out")
        pt_done = sem("pt_done")
        pt_ready = sem("pt_ready")
        u1_done = sem("u1_done")
        u1_ready = sem("u1_ready")
        o_done = sem("o_done")
        moba_s = sem("moba_s")
        moba_m = sem("moba_m")
        moba_e = sem("moba_e")
        moba_T = sem("moba_T")
        moba_T_out = sem("moba_T_out")
        moba_y = sem("moba_y")
        y2_ms = sem("y2_ms")
        y2_root = sem("y2_root")
        mix2_ready = sem("mix2_ready")
        x3_ready = sem("x3_ready")
        h4_ready = sem("h4_ready")
        route_here = sem("route_here")
        route_done = sem("route_done")
        route_exp = sem("route_exp")
        route_expd = sem("route_expd")
        numbers_ready = sem("numbers_ready")
        chosen_ready = sem("chosen_ready")
        rank_ready = sem("rank_ready")
        hot_ready = sem("hot_ready")
        slots_ready = sem("slots_ready")
        rows_saved = sem("rows_saved")
        x_turned = sem("x_turned")
        xt_left = sem("xt_left")
        xt_right = sem("xt_right")
        hid_turned = sem("hid_turned")
        hidT_ready = sem("hidT_ready")
        y_left = sem("y_left")
        from_staged = sem("from_staged")
        to_staged = sem("to_staged")
        y_right = sem("y_right")
        scattered = [sem(f"scattered{b}") for b in range(2)]
        y_back = sem("y_back")
        x4_ready = sem("x4_ready")
        gu_done = sem("gu_done")
        silu_ready = sem("silu_ready")
        hid_ready = sem("hid_ready")
        down_used = sem("down_used")
        out_ready = sem("out_ready")
        out_gone = sem("out_gone")
        gathered = [sem(f"gathered{j}") for j in range(GS)]
        gu_here = [sem(f"gu_here{b}") for b in range(2)]
        down_here = [sem(f"down_here{b}") for b in range(2)]

        GATHERED = 16 * NT * SLOTS // GS

        block = ctx.enter_context(nc.Block())

        def chunk_ready(eng, n):
            eng.wait_ge(chunk_here[n % WSLOTS], 16 * (n // WSLOTS + 1))

        def chunk_done(eng, n):
            eng.wait_ge(chunk_used, n + 1)

        def project_fm(pe, c0, count, act_T, at=0):
            for n in range(count):
                chunk_ready(pe, c0 + n)
                w = wchunk(c0 + n)
                for j in range(2):
                    for k in range(KD):
                        ins = nc.tensor.matmul(bank[1 + (at + n) % 4][:, j * T:(j + 1) * T],
                                               w[:, k, j * P:(j + 1) * P], act_T[:, k, :],
                                               start=k == 0, stop=k == KD - 1)
                ins.then_inc(chunk_used, 1)

        def sums_over_features(pe, squares, nth):
            pe.wait_ge(rms_sq, nth)
            for k in range(KD):
                ins = nc.tensor.matmul(bank[7][:, 0:T], ones, squares[:, k, :], start=k == 0, stop=k == KD - 1)
            ins.then_inc(rms_sum, 1)

        def transposes(pe, out, blocks):
            for i, b in enumerate(blocks):
                ins = nc.tensor.transpose(out[:, i * P:(i + 1) * P], b, ident)
            return ins

        @block.sync
        def _(sp):
            for n in range(WSLOTS):
                sp.dma_start(wring[:, n * CHUNK:(n + 1) * CHUNK], wstream_d[n]).then_inc(chunk_here[n], 16)
            full = N_CHUNKS // WSLOTS
            with sp.Fori(1, full) as turn:
                for s in range(WSLOTS):
                    sp.wait_ge(chunk_used, turn * WSLOTS + (s + 1 - WSLOTS))
                    sp.dma_start(wring[:, s * CHUNK:(s + 1) * CHUNK],
                                 wstream_d[bass.ds(turn * WSLOTS + s, 1)].rearrange("a p c -> (a p) c"))\
                      .then_inc(chunk_here[s], 16)
            for n in range(full * WSLOTS, N_CHUNKS):
                sp.wait_ge(chunk_used, n + 1 - WSLOTS)
                s = n % WSLOTS
                sp.dma_start(wring[:, s * CHUNK:(s + 1) * CHUNK], wstream_d[n]).then_inc(chunk_here[s], 16)

            def gu_buf(b):
                return wring[:, 2 * b * CHUNK:(2 * b + 2) * CHUNK]

            def down_buf(b):
                return wring[:, (4 + b) * CHUNK:(5 + b) * CHUNK]

            for b in range(2):
                sp.wait_ge(chunk_used, last_chunk_in(2 * b, N_CHUNKS) + 1)
                sp.wait_ge(chunk_used, last_chunk_in(2 * b + 1, N_CHUNKS) + 1)
                sp.dma_start(gu_buf(b), moe_d[b, :, 0:2 * CHUNK]).then_inc(gu_here[b], 16)
                sp.wait_ge(chunk_used, last_chunk_in(4 + b, N_CHUNKS) + 1)
                sp.dma_start(down_buf(b), moe_d[b, :, 2 * CHUNK:3 * CHUNK]).then_inc(down_here[b], 16)
            sp.wait_ge(slots_ready, 1)
            n_pairs = sp.value_load(pairs[0:1, 0:1], min_val=PAIRS, max_val=WINDOWS * PAIRS)
            with sp.Fori(1, n_pairs) as i:
                for b in range(2):
                    src = moe_d[bass.ds((2 * i + b) % NE, 1)].rearrange("a p c -> (a p) c")
                    sp.wait_ge(gu_done, 2 * i + (b - 1))
                    sp.dma_start(gu_buf(b), src[:, 0:2 * CHUNK]).then_inc(gu_here[b], 16)
                    sp.wait_ge(down_used, 2 * i + (b - 1))
                    sp.dma_start(down_buf(b), src[:, 2 * CHUNK:3 * CHUNK]).then_inc(down_here[b], 16)
            for b in range(2):
                sp.wait_ge(scattered[b], n_pairs * 16 + 16)
            for t in range(NT):
                sp.dma_start(back[:, t].rearrange("p r d -> p (r d)"), y4_d[t * P * 2:(t + 1) * P * 2]
                             .rearrange("(p r) d -> p (r d)", r=2)).then_inc(y_back, 16)
            for t in range(NT):
                sp.wait_ge(out_ready, t + 1)
                sp.dma_start(out_d[t * P:(t + 1) * P], x3[:, t]).then_inc(out_gone, 16)
            sp.wait_ge(out_gone, 16 * NT)

        @block.gpsimd
        def _(pool):
            def gather(t, j, column):
                src = bass.IndirectOffsetOnAxis(ap=column, axis=0)
                pool.indirect_dma_start(G[:, j, :], None, uv_d, src).then_inc(gathered[j], 16)

            for t in range(NT):
                pool.wait_ge(top_ready, t + 1)
                if t == 0:
                    chunk_done(pool, C_SK)
                    pool.wait_ge(tokens_turned, 4)
                    for j in range(GS):
                        gather(0, j, expert[:, 0, j:j + 1])
                with pool.Fori(1 if t == 0 else 0, SLOTS // GS) as turn:
                    for j in range(GS):
                        pool.wait_ge(slot_used, turn * GS + (t * SLOTS + j + 1 - GS))
                        nc.gpsimd.tensor_copy(stage[:, j:j + 1], expert[:, t, bass.ds(turn * GS + j, 1)])\
                          .then_inc(idx_staged, 1)
                        pool.wait_ge(top_ready, t + 1)
                        pool.wait_ge(idx_staged, turn * GS + (t * SLOTS + j + 1 - GS))
                        gather(t, j, stage[:, j:j + 1])

            pool.wait_ge(x3_ready, 1)
            nc.gpsimd.iota(slot_no, [[P, WINDOWS], [1, P]], base=1, channel_multiplier=0,
                           allow_small_or_imprecise_dtypes=True)
            nc.gpsimd.iota(token_no, [[P, NT]], base=1, channel_multiplier=1,
                           allow_small_or_imprecise_dtypes=True).then_inc(numbers_ready, 1)
            nc.gpsimd.memset(X, 0.0)
            nc.gpsimd.memset(Yx, 0.0).then_inc(to_staged, 2)
            pool.wait_ge(to_staged, 2)
            pool.wait_ge(rows_saved, 16 * NT)
            pool.wait_ge(slots_ready, 1)
            n_pairs = pool.value_load(pairs[0:1, 0:1], min_val=PAIRS, max_val=WINDOWS * PAIRS)

            last_from, last_to = pool.to_reg(T - 1), pool.to_reg(2 * T - 1)

            def gather4(b, column):
                src = bass.IndirectOffsetOnAxis(ap=column, axis=0)
                pool.indirect_dma_start(X[:, b], None, h4_d, src, bounds_check=last_from, oob_is_err=False)\
                    .then_inc(gathered[b], 16)

            def scatter4(b, column):
                dst = bass.IndirectOffsetOnAxis(ap=column, axis=0)
                pool.indirect_dma_start(y4_d, dst, Yx[:, b], None, bounds_check=last_to, oob_is_err=False)\
                    .then_inc(scattered[b], 16)

            for b in range(2):
                gather4(b, from_row[:, b:b + 1])
            for b in range(2):
                scatter4(b, to_row[:, WINDOWS * NE + b:WINDOWS * NE + b + 1])
            with pool.Fori(0, n_pairs) as i:
                for b in range(2):
                    pool.wait_ge(x_turned, 2 * i + (b + 1))
                    nc.gpsimd.tensor_copy(stage4[:, b:b + 1], from_row[:, bass.ds(2 * i + (b + 2), 1)])\
                      .then_inc(from_staged, 1)
                    pool.wait_ge(slots_ready, 1)
                    pool.wait_ge(from_staged, 2 * i + (b + 1))
                    gather4(b, stage4[:, b:b + 1])
                for b in range(2):
                    pool.wait_ge(y_left, 2 * i + (b + 3))
                    pool.wait_ge(y_right, 2 * i + (b + 3))
                    pool.wait_ge(scattered[b], 16 * i + 16)
                    nc.gpsimd.tensor_copy(stage4[:, 2 + b:3 + b], to_row[:, bass.ds(2 * i + b, 1)])\
                      .then_inc(to_staged, 1)
                    pool.wait_ge(slots_ready, 1)
                    pool.wait_ge(to_staged, 2 * i + (b + 3))
                    scatter4(b, stage4[:, 2 + b:3 + b])
            for b in range(2):
                pool.wait_ge(gathered[b], n_pairs * 16 + (GATHERED + 16))

        @block.scalar
        def _(act):
            steps = [0]

            def own(ins):
                steps[0] += 1
                ins.then_inc(act_step, 1)
                act.wait_ge(act_step, steps[0])

            act.dma_start(small[:, :], small_d).then_inc(small_here, 16)
            act.dma_start(xT, xT_d).then_inc(x_here, 16)
            act.dma_start(chT, ctxT_d).then_inc(x_here, 16)
            act.dma_start(const[:, :], const_d).then_inc(const_here, 16)
            act.dma_start(rows[:, :], rows_d).then_inc(const_here, 16)
            act.wait_ge(small_here, 16)
            nc.scalar.activation(condS.rearrange("p k c -> p (k c)"), small[:, SM["cond"]], ACT.Silu)\
              .then_inc(cond_ready, 1)
            act.wait_ge(x_here, 32)
            act.wait_ge(const_here, 32)
            nc.scalar.activation(sq, xT, ACT.Square).then_inc(squares1, 1)
            nc.scalar.activation(csq, chT, ACT.Square).then_inc(squares1, 1)
            act.wait_ge(sums1, 1)
            nc.scalar.activation(rstd.rearrange("p a t -> p (a t)"), bank[7][:, :], ACT.Sqrt,
                                 bias=epsc, scale=1.0 / D).then_inc(root1, 1)
            for n in range(N_IN1):
                chunk_done(act, C_IN1 + n)
                func = ACT.Silu if n in (4, 5) else ACT.Copy
                nc.scalar.activation(proj[:, :, n * COLS:(n + 1) * COLS],
                                     bank[1 + 2 * (n % 2)][:, :].rearrange("p (t c) -> p t c", t=NT),
                                     func).then_inc(proj_x_out, 1)
            act.wait_ge(qk_sq, 1)
            nc.scalar.activation(sr, ss, ACT.Sqrt, bias=epsc, scale=1.0 / DD).then_inc(qk_root, 1)
            act.wait_ge(gam_e, 1)
            nc.scalar.activation(lt[:, 1, :], lt[:, 0, :], ACT.Exp).then_inc(gam_e, 1)
            act.wait_ge(lam_dots, 1)
            nc.scalar.activation(lam2[:, 0:2], lam2[:, 0:2], ACT.Exp).then_inc(lam_exp, 1)
            act.wait_ge(gam_ready, 1)
            for h in range(RH):
                act.wait_ge(decay_args, h + 1)
                d = DC[:, h % 2]
                dist = const[:, CN["dist"]].rearrange("p (k t) -> p k t", k=NT)
                if h >= 2:
                    act.wait_ge(ret_masked, h - 1)
                nc.scalar.activation(d[:, 0:2, :], dist, ACT.Exp, bias=lgL[:, h:h + 1],
                                     scale=lg[:, h:h + 1])
                nc.scalar.activation(tmp[:, h % 2, 0:512].rearrange("p (k t) -> p k t", k=NT), dist,
                                     ACT.Exp, bias=lgL[:, 4 + h:5 + h], scale=nlg[:, 4 + h:5 + h])
                nc.scalar.activation(d[:, 2:4, :].rearrange("p k t -> p (k t)"),
                                     tmp[:, h % 2, 512:1024], ACT.Exp).then_inc(decay_ready, 1)
            for i in range(DH * NT):
                for c in range(2):
                    act.wait_ge(diff_max, 2 * i + c + 1)
                    if i >= 1:
                        act.wait_ge(diff_a, i)
                    nc.scalar.activation(prob[:, c, :], bank[1 + 2 * (i % 2) + c][:, :], ACT.Exp,
                                         bias=zm[:, 1, c:c + 1], scale=DD ** -0.5,
                                         accum_out=zz[:, 0, c:c + 1]).then_inc(diff_exp, 1)
                act.wait_ge(diff_aT, i + 1)
                if i >= 2:
                    act.wait_ge(diff_y, i - 1)
                nc.scalar.activation(aT[:, i % 2].rearrange("p k t -> p (k t)"), bank[5 + i % 2][:, :],
                                     ACT.Copy).then_inc(diff_aT_out, 1)
            act.wait_ge(y_ms, 1)
            nc.scalar.activation(sr[:, 0:16], ss[:, 0:16], ACT.Sqrt, bias=epsc, scale=1.0 / RV)\
              .then_inc(y_root, 1)
            for g in range(4):
                act.wait_ge(mixT_done, g + 1)
                nc.scalar.activation(mixT[:, 2 * g:2 * g + 2, :].rearrange("p k t -> p (k t)"),
                                     bank[5 + g % 2][:, :], ACT.Copy).then_inc(mixT_out, 1)

            chunk_done(act, C_OUT1 + N_OUT - 1)
            act.wait_ge(x2_ready, 1)
            nc.scalar.activation(sq2, xT, ACT.Square).then_inc(rms_sq, 1)
            act.wait_ge(rms_sum, 1)
            nc.scalar.activation(rstd2, bank[7][:, 0:T], ACT.Sqrt, bias=epsc, scale=1.0 / D)\
              .then_inc(rms_root, 1)
            for n in range(N_Q):
                chunk_done(act, C_Q + n)
                nc.scalar.activation(qT[:, 2 * n:2 * n + 2, :].rearrange("p k t -> p (k t)"),
                                     bank[1 + n % 4][:, :], ACT.Copy).then_inc(q_out, 1)
            for g in range(4):
                act.wait_ge(tokens_turned, g + 1)
                nc.scalar.activation(h2[:, g // 2, (g % 2) * 512:(g % 2 + 1) * 512], bank[5 + g % 2][:, :],
                                     ACT.Copy).then_inc(tokens_out, 1)
            for i in range(2 * NT):
                if i < 2 * NT - 1:
                    act.wait_ge(keys_done, i + 1)
                else:
                    chunk_done(act, C_SK)
                for b in range(2):
                    ins = nc.scalar.activation(
                        keyS[:, i // 2, 8 * (i % 2) + 4 * b:8 * (i % 2) + 4 * b + 4, :]
                        .rearrange("p h n -> p (h n)"), bank[(1, 3)[i % 2] + b][:, :], ACT.Copy)
                ins.then_inc(keys_out, 1)
            for t in range(NT):
                act.wait_ge(top_exp, t + 1)
                nc.scalar.activation(gates[:, t, :], gates[:, t, :], ACT.Exp).then_inc(top_expd, 1)
            n_step = 5
            for t in range(NT):
                with act.Fori(0, SLOTS // GS) as turn:
                    for g in range(2):
                        act.wait_ge(dot_done, turn * GS + (t * SLOTS + 4 * g + 4 + 2))
                        nc.scalar.activation(gelu[:, g, :], dots[:, g, :], ACT.Gelu).then_inc(gelu_step, 1)
                        done = turn * (2 * n_step) + (t * 2 * n_step * SLOTS // GS + g * n_step)
                        act.wait_ge(gelu_step, done + 1)
                        for q in range(4):
                            nc.scalar.activation(weight[:, g, q:q + 1], gelu[:, g, q:q + 1], ACT.Copy,
                                                 scale=gates[:, t, bass.ds(turn * GS + (4 * g + q), 1)])\
                              .then_inc(gelu_step, 1)
                        for q in range(4):
                            act.wait_ge(gelu_step, done + (q + 2))
                            nc.scalar.activation(diag[:, 4 * g + q, :], ident, ACT.Copy,
                                                 scale=weight[:, g, q:q + 1]).then_inc(diag_ready, 1)
                act.wait_ge(slot_used, (t + 1) * SLOTS)
                if t == 1:
                    act.wait_ge(ffnT_done, 2)
                for c in range(2):
                    ins = nc.scalar.activation(ffn[:, c * 512:(c + 1) * 512], bank[1 + 2 * t + c][:, :], ACT.Copy)
                ins.then_inc(ffn_out, 1)
            act.wait_ge(x2_ready, 2)
            act.dma_start(masks.rearrange("p w s n -> p (w s n)"), masks_d).then_inc(masks_here, 16)
            act.dma_start(gate2.rearrange("p k c -> p (k c)"), gate2_d).then_inc(masks_here, 16)
            nc.scalar.activation(sq3, xT, ACT.Square).then_inc(rms_sq, 1)
            act.wait_ge(rms_sum, 2)
            nc.scalar.activation(rstd3, bank[7][:, 0:T], ACT.Sqrt, bias=epsc, scale=1.0 / D)\
              .then_inc(rms_root, 1)
            for n in range(N_IN2):
                chunk_done(act, C_IN2 + n)
                b = bank[1 + n % 4]
                two = b[:, :].rearrange("p (k t) -> p k t", k=2)
                if n < 4:
                    dst, src = (mqT, mkT)[n // 2][:, 2 * (n % 2):2 * (n % 2) + 2, :], two
                elif n < 6:
                    dst, src = mv[:, :, (n - 4) * COLS:(n - 3) * COLS], two
                elif n < 12:
                    dst, src = cvin[:, 2 * (n - 6):2 * (n - 6) + 2, CONV - 1:], two
                else:
                    dst, src = gz[:, :, (n - 12) * COLS:(n - 11) * COLS], two
                nc.scalar.activation(dst, src, ACT.Silu if n >= 12 else ACT.Copy).then_inc(in2_out, 1)
            act.wait_ge(ab_exp, 1)
            nc.scalar.activation(spt[:, 1, :], spt[:, 0, :], ACT.Exp)
            nc.scalar.activation(beta, beta, ACT.Exp, scale=-1.0)
            nc.scalar.activation(kd[:, 0:4], rows[:, RW["A_log"]], ACT.Exp).then_inc(ab_expd, 1)
            act.wait_ge(conv_ready, 1)
            nc.scalar.activation(cvT, cvT, ACT.Silu).then_inc(conv_silu, 1)
            act.wait_ge(lnorm_sum, 1)
            for i in range(4):
                ins = nc.scalar.activation(nrm[:, 2 * i:2 * i + 2, :].rearrange("p a b -> p (a b)"),
                                           bank[1 + i][:, :], ACT.Sqrt, bias=epsc)
            ins.then_inc(lnorm_root, 1)
            act.wait_ge(g_done, 1)
            nc.scalar.activation(gc, bank[7][:, 0:8], ACT.Copy)
            for i in range(2):
                ins = nc.scalar.activation(gR[:, 4 * i:4 * i + 4, :].rearrange("p a b -> p (a b)"),
                                           bank[5 + i][:, :], ACT.Copy)
            ins.then_inc(g_done, 1)
            for i, dst in enumerate((kTM, vTM)):
                for c in range(2):
                    act.wait_ge(tm_done, 2 * i + c + 1)
                    nc.scalar.activation(dst[:, 4 * c:4 * c + 4, :].rearrange("p a b -> p (a b)"),
                                         bank[5 + c][:, :], ACT.Copy).then_inc(tm_out, 1)
            act.wait_ge(gx_ready, 1)
            nc.scalar.activation(gD, gD, ACT.Exp)
            nc.scalar.activation(gDT, gDT, ACT.Exp)
            nc.scalar.activation(egc, gc, ACT.Exp)
            nc.scalar.activation(kd, kd, ACT.Exp)
            nc.scalar.activation(gR, gR, ACT.Exp).then_inc(gx_exp, 1)
            act.wait_ge(at_done, 1)
            for i in range(2):
                ins = nc.scalar.activation(gAT[:, 4 * i:4 * i + 4, :].rearrange("p a b -> p (a b)"),
                                           bank[5 + i][:, :], ACT.Copy)
            ins.then_inc(at_out, 1)
            for s in range(1, LEVELS):
                act.wait_ge(w_done, s)
                for i in range(2):
                    ins = nc.scalar.activation(gW[:, 4 * i:4 * i + 4, :].rearrange("p a b -> p (a b)"),
                                               bank[1 + i][:, :], ACT.Copy)
                ins.then_inc(w_out, 1)
            act.wait_ge(uv_done, 1)
            for i in range(2):
                nc.scalar.activation(gU[:, 4 * i:4 * i + 4, :].rearrange("p a b -> p (a b)"),
                                     bank[1 + i][:, :], ACT.Copy)
            nc.scalar.activation(gwT.rearrange("p a b -> p (a b)"), bank[3][:, :], ACT.Copy).then_inc(uv_out, 1)
            act.wait_ge(s_done, 1)
            nc.scalar.activation(gS.rearrange("p a b -> p (a b)"), bank[4][:, :], ACT.Copy).then_inc(s_out, 1)
            for h in range(MH):
                act.wait_ge(moba_m, h + 1)
                if h >= 1:
                    act.wait_ge(moba_T, h)
                nc.scalar.activation(soft[:, 0:P], soft[:, 0:P], ACT.Exp, bias=mx[:, 1, 0:1],
                                     accum_out=rz[:, 0, h:h + 1])
                nc.scalar.activation(soft[:, P:3 * P], soft[:, P:3 * P], ACT.Exp, bias=mx[:, 1, 1:2],
                                     accum_out=rz[:, 1, h:h + 1]).then_inc(moba_e, 1)
                act.wait_ge(moba_T, h + 1)
                if h >= 1:
                    act.wait_ge(moba_y, h)
                nc.scalar.activation(softT, bank[7][:, 0:3 * P], ACT.Copy).then_inc(moba_T_out, 1)
            act.wait_ge(y2_ms, 1)
            nc.scalar.activation(ms2, ms2, ACT.Sqrt, bias=epsc, scale=1.0 / GD).then_inc(y2_root, 1)
            for g in range(4):
                act.wait_ge(mixT_done, 4 + g + 1)
                nc.scalar.activation(mix2T[:, 2 * g:2 * g + 2, :].rearrange("p k t -> p (k t)"),
                                     bank[5 + g % 2][:, :], ACT.Copy).then_inc(mixT_out, 1)
            act.wait_ge(x3_ready, 1)
            act.dma_start(routeW.rearrange("p k e -> p (k e)"), route_d).then_inc(route_here, 16)
            nc.scalar.activation(sq4, xT, ACT.Square).then_inc(rms_sq, 1)
            act.wait_ge(rms_sum, 3)
            nc.scalar.activation(rstd4, bank[7][:, 0:T], ACT.Sqrt, bias=epsc, scale=1.0 / D)\
              .then_inc(rms_root, 1)
            act.dma_start(final_g, final_g_d).then_inc(route_here, 16)
            for g in range(8):
                act.wait_ge(tokens_turned, 4 + g + 1)
                to = h4 if g < 4 else x3
                nc.scalar.activation(to[:, (g // 2) % 2, (g % 2) * 512:(g % 2 + 1) * 512],
                                     bank[g % 4][:, :], ACT.Copy).then_inc(tokens_out, 1)
                if g == 3:
                    for t in range(NT):
                        act.wait_ge(tokens_out, 4 + 2 * t + 2)
                        act.dma_start(h4_d[t * P:(t + 1) * P], h4[:, t]).then_inc(rows_saved, 16)
            act.wait_ge(route_exp, 1)
            nc.scalar.activation(gex, gex, ACT.Exp)
            nc.scalar.activation(pw[:, :, 1:2], pw[:, :, 0:1], ACT.Exp).then_inc(route_expd, 1)
            nc.scalar.activation(zr[:, 0], ones[:, 0:2], ACT.Copy).then_inc(y_left, 2)

            def turned_rows(b, wait_n):
                act.wait_ge(x_turned, wait_n)
                nc.scalar.activation(XT[:, b, 0:4].rearrange("p k t -> p (k t)"), bank[0][:, :],
                                     ACT.Copy).then_inc(xt_left, 1)

            for b in range(2):
                turned_rows(b, b + 1)
            act.wait_ge(slots_ready, 1)
            n_pairs = act.value_load(pairs[0:1, 0:1], min_val=PAIRS, max_val=WINDOWS * PAIRS)
            with act.Fori(0, n_pairs) as i:
                for b in range(2):
                    act.wait_ge(gu_done, 2 * i + (b + 1))
                    nc.scalar.activation(sg[:, b], bank[2 + b][:, 0:FF], ACT.Silu).then_inc(silu_ready, 1)
                for b in range(2):
                    turned_rows(b, 2 * i + (b + 3))
                    act.wait_ge(scattered[b], 16 * i + 16)
                    act.wait_ge(down_used, 2 * i + (b + 1))
                    nc.scalar.activation(Yx[:, b, 0:512], bank[4 + 2 * b][:, :], ACT.Copy).then_inc(y_left, 1)
            for t in range(NT):
                act.wait_ge(x4_ready, t + 1)
                nc.scalar.activation(h4[:, t], x3[:, t], ACT.Square, accum_out=ms4[:, t:t + 1])\
                  .then_inc(act_step, 1)
                steps[0] += 1
                act.wait_ge(act_step, steps[0])
                nc.scalar.activation(ms4[:, t:t + 1], ms4[:, t:t + 1], ACT.Sqrt, bias=epsc, scale=1.0 / D)\
                  .then_inc(rms_root, 1)

        @block.vector
        def _(dve):
            v = nc.vector
            steps = [0]

            def link(ins):
                steps[0] += 1
                ins.then_inc(dve_step, 1)
                dve.wait_ge(dve_step, steps[0])

            dve.wait_ge(const_here, 32)
            x = rows[:, RW["decay"]]
            link(v.tensor_scalar(lt[:, 2, :], x, -1.0, None, ALU.mult))
            link(v.tensor_tensor(lt[:, 0, :], x, lt[:, 2, :], ALU.min))
            v.memset(ss, 0.0).then_inc(gam_e, 1)
            lam = rows[:, RW["lam"]].rearrange("p (a c) -> p a c", a=4)
            link(v.tensor_tensor(lamt[:, 0, :], lam[:, 0, :], lam[:, 1, :], ALU.mult))
            link(v.tensor_tensor(lamt[:, 1, :], lam[:, 2, :], lam[:, 3, :], ALU.mult))
            v.tensor_reduce(lam2[:, 0:2], lamt, AX, ALU.add).then_inc(lam_dots, 1)

            dve.wait_ge(root1, 1)
            link(v.reciprocal(rstd, rstd))
            link(v.tensor_tensor(hT, xT, bc(rstd[:, 0, :], 1, KD), ALU.mult))
            link(v.tensor_tensor(chT, chT, bc(rstd[:, 1, :], 1, KD), ALU.mult))
            chunk_done(dve, C_MOD + N_MOD - 1)
            link(v.tensor_tensor(modv, bank[0][:, 0:96].rearrange("p (m c) -> p m c", c=2),
                                 bc(small[:, SM["b_mod"]], 2, 2), ALU.add))
            for c in range(2):
                link(v.scalar_tensor_tensor(scale1[:, c, :], modv[:, KD:2 * KD, c], 1.0,
                                            small[:, SM["g1"]], ALU.add, ALU.mult))
            link(v.scalar_tensor_tensor(scale2, modv[:, 4 * KD:5 * KD, 0], 1.0,
                                        small[:, SM["g2"]], ALU.add, ALU.mult))
            for k in range(KD):
                for c, h in enumerate((hT, chT)):
                    ins = v.tensor_scalar(h[:, k, :], h[:, k, :], scale1[:, c, k:k + 1],
                                          modv[:, k, c:c + 1], ALU.mult, ALU.add)
            ins.then_inc(h_ready, 1)
            at = 0
            for n in range(N_IN1):
                if n in CTX_CHUNKS:
                    chunk_done(dve, C_IN1 + n)
                    v.tensor_copy(cproj[:, :, at:at + COLS],
                                  bank[2 + 2 * (n % 2)][:, :].rearrange("p (t c) -> p t c", t=NT))\
                     .then_inc(proj_c_out, 1)
                    at += COLS
            dve.wait_ge(proj_c_out, 7)
            dve.wait_ge(proj_x_out, N_IN1)
            qk = [(proj[:, t, 1536:2560], 16, 16 * t) for t in range(NT)]
            qk += [(cproj[:, t, 768:1280], 8, 32 + 8 * t) for t in range(NT)]
            for ap, n, at in qk:
                flat = tmp[:, 0, 0:n * DD]
                link(v.tensor_tensor(flat, ap, ap, ALU.mult))
                ins = v.tensor_reduce(ss[:, at:at + n], flat.rearrange("p (h c) -> p h c", h=n), AX, ALU.add)
                if at == 40:
                    ins.then_inc(qk_sq, 1)
                else:
                    link(ins)
            dve.wait_ge(qk_root, 1)
            link(v.reciprocal(sr, sr))
            gq, gk = rows[:, RW["qk_g"]][:, 0:DD], rows[:, RW["qk_g"]][:, DD:2 * DD]
            for ap, n, at in qk:
                a3 = ap.rearrange("p (h c) -> p h c", h=n)
                link(v.tensor_tensor(a3, a3, bc(sr[:, at:at + n], 2, DD), ALU.mult))
                if n == 16:
                    link(v.tensor_tensor(a3[:, 0:8], a3[:, 0:8], bc(gq, 1, 8), ALU.mult))
                    link(v.tensor_tensor(a3[:, 8:16], a3[:, 8:16], bc(gk, 1, 8), ALU.mult))
                else:
                    link(v.tensor_tensor(a3, a3, bc(gk, 1, 8), ALU.mult))
            for t in range(NT):
                cos = const[:, CN["cos"]][:, t * 64:(t + 1) * 64]
                sin = const[:, CN["sin"]][:, t * 64:(t + 1) * 64]
                for lo, n in ((0, 8), (1536, 16)):
                    a = proj[:, t, lo:lo + n * 64]
                    t0, t1 = tmp[:, 0, 0:n * 64], tmp[:, 1, 0:n * 64]

                    def parts(ap):
                        return ap.rearrange("p (h r c) -> p h r c", r=2, c=16)
                    link(v.tensor_tensor(t0.rearrange("p (h c) -> p h c", h=n),
                                         a.rearrange("p (h c) -> p h c", h=n), bc(cos, 1, n), ALU.mult))
                    for half in range(2):
                        x4 = a.rearrange("p (h r s c) -> p h r s c", r=2, s=2, c=16)
                        o4 = t1.rearrange("p (h r s c) -> p h r s c", r=2, s=2, c=16)
                        s4 = sin.rearrange("p (r s c) -> p r s c", r=2, s=2)
                        link(v.tensor_tensor(o4[:, :, :, half, :], x4[:, :, :, 1 - half, :],
                                             bc(s4[:, :, half, :], 1, n), ALU.mult))
                    link(v.tensor_tensor(a, t0, t1, ALU.add))
            v.memset(lamt, 0.0).then_inc(roped, 1)
            dve.wait_ge(gam_e, 2)
            e = lt[:, 1, :]
            link(v.tensor_scalar(lt[:, 2, :], e, 2.0, None, ALU.add))
            link(v.reciprocal(lt[:, 2, :], lt[:, 2, :]))
            link(v.tensor_tensor(lt[:, 3, :], e, lt[:, 2, :], ALU.mult))
            link(v.tensor_tensor(lt[:, 4, :], lt[:, 3, :], lt[:, 3, :], ALU.mult))
            link(v.tensor_scalar(lt[:, 5, :], lt[:, 4, :], 2.0 / 17, 2.0 / 15, ALU.mult, ALU.add))
            for k in (13, 11, 9, 7, 5, 3, 1):
                link(v.tensor_tensor(lt[:, 5, :], lt[:, 5, :], lt[:, 4, :], ALU.mult))
                link(v.tensor_scalar(lt[:, 5, :], lt[:, 5, :], 2.0 / k, None, ALU.add))
            link(v.tensor_tensor(lt[:, 5, :], lt[:, 5, :], lt[:, 3, :], ALU.mult))
            link(v.scalar_tensor_tensor(lg, x, 0.0, lt[:, 5, :], ALU.min, ALU.subtract))
            link(v.tensor_scalar(nlg, lg, -1.0, None, ALU.mult))
            v.tensor_scalar(lgL, lg, float(T), None, ALU.mult).then_inc(gam_ready, 1)
            dve.wait_ge(lam_exp, 1)
            link(v.tensor_tensor(lam2[:, 2:3], lam2[:, 1:2], lam2[:, 0:1], ALU.subtract))
            link(v.tensor_scalar(lam2[:, 3:4], lam2[:, 2:3], -LAM_INIT, None, ALU.add))
            dve.wait_ge(gam_ready, 1)

            for i, dst in enumerate(turned_views(rqT, rkT, dqT, dkT)):
                dve.wait_ge(turned, i + 1)
                v.tensor_copy(dst, bank[5 + i % 2][:, :].rearrange("p (b t) -> p b t", b=2))\
                 .then_inc(turned_out, 1)
            dist = const[:, CN["dist"]].rearrange("p (k t) -> p k t", k=NT)

            def decay_arg(h):
                w = tmp[:, h % 2, 512:1024].rearrange("p (k t) -> p k t", k=NT)
                u = prob[:, h % 2, :].rearrange("p (k t) -> p k t", k=NT)
                link(v.tensor_scalar(w, dist, 0.0, lg[:, h:h + 1], ALU.max, ALU.mult))
                link(v.tensor_scalar(u, dist, 0.0, nlg[:, 4 + h:5 + h], ALU.min, ALU.mult))
                v.tensor_tensor(w, w, u, ALU.add).then_inc(decay_args, 1)

            decay_arg(0)
            for h in range(RH):
                if h + 1 < RH:
                    decay_arg(h + 1)
                dve.wait_ge(decay_ready, h + 1)
                d = DC[:, h % 2]
                link(v.tensor_tensor(d[:, 0:2, :].rearrange("p k t -> p (k t)"),
                                     d[:, 0:2, :].rearrange("p k t -> p (k t)"),
                                     tmp[:, h % 2, 0:512], ALU.add))
                dve.wait_ge(ret_scores, h + 1)
                if h >= 2:
                    dve.wait_ge(ret_y, h - 1)
                for half in range(2):
                    ins = v.scalar_tensor_tensor(
                        SD[:, h % 2, 2 * half:2 * half + 2].rearrange("p k t -> p (k t)"),
                        bank[1 + 2 * (h % 2) + half][:, :], RK ** -0.5,
                        d[:, 2 * half:2 * half + 2].rearrange("p k t -> p (k t)"), ALU.mult, ALU.mult)
                ins.then_inc(ret_masked, 1)
            for j in range(2):
                dve.wait_ge(ret_y, 2 * j + 2)
                v.tensor_copy(Y[:, :, 256 * j:256 * j + 256].rearrange("p t (h e) -> p h t e", h=2),
                              bank[(0, 7)[j]][:, :].rearrange("p (h t e) -> p h t e", h=2, t=NT))\
                 .then_inc(ret_y_out, 1)
            for i in range(DH * NT):
                for c in range(2):
                    dve.wait_ge(diff_scores, 2 * i + c + 1)
                    link(v.reduce_max(zm[:, 0, c:c + 1], bank[1 + 2 * (i % 2) + c][:, :], AX))
                    v.tensor_scalar(zm[:, 1, c:c + 1], zm[:, 0, c:c + 1], -DD ** -0.5, None, ALU.mult)\
                     .then_inc(diff_max, 1)
                dve.wait_ge(diff_exp, 2 * i + 2)
                link(v.reciprocal(zr[:, 0, :], zz[:, 0, :]))
                link(v.tensor_tensor(zr[:, 1, 0:1], zr[:, 0, 1:2], lam2[:, 3:4], ALU.mult))
                link(v.tensor_scalar(prob[:, 0, :], prob[:, 0, :], zr[:, 0, 0:1], None, ALU.mult))
                if i >= 1:
                    dve.wait_ge(diff_aT, i)
                v.scalar_tensor_tensor(tmp[:, 0, 0:512], prob[:, 1, :], zr[:, 1, 0:1], prob[:, 0, :],
                                       ALU.mult, ALU.add).then_inc(diff_a, 1)
            for j in range(2):
                dve.wait_ge(diff_y, 4 * j + 4)
                link(v.tensor_copy(
                    Y[:, :, 512 + 256 * j:768 + 256 * j].rearrange("p t (h e) -> p h t e", h=2),
                    bank[(0, 7)[j]][:, :].rearrange("p (h t e) -> p h t e", h=2, t=NT)))
            for t in range(NT):
                dve.wait_ge(diff_aT, DH * NT)
                link(v.tensor_tensor(tmp[:, t, :], Y[:, t, :], Y[:, t, :], ALU.mult))
                ins = v.tensor_reduce(ss[:, 8 * t:8 * t + 8], tmp[:, t, :].rearrange("p (h e) -> p h e", h=8),
                                      AX, ALU.add)
                if t == NT - 1:
                    ins.then_inc(y_ms, 1)
                else:
                    link(ins)
            dve.wait_ge(y_root, 1)
            link(v.reciprocal(sr[:, 0:16], sr[:, 0:16]))
            for t in range(NT):
                y = Y[:, t, :]
                y3 = y.rearrange("p (h e) -> p h e", h=8)
                link(v.tensor_tensor(y3, y3, bc(sr[:, 8 * t:8 * t + 8], 2, RV), ALU.mult))
                link(v.tensor_tensor(y[:, 0:512], y[:, 0:512], proj[:, t, 1024:1536], ALU.mult))
                link(v.tensor_tensor(y[:, 0:512], y[:, 0:512], rows[:, RW["ret_g"]], ALU.mult))
                v.scalar_tensor_tensor(y[:, 512:1024], y[:, 512:1024], 1.0 - LAM_INIT,
                                       rows[:, RW["diff_g"]], ALU.mult, ALU.mult).then_inc(mix_ready, 1)
            for n in range(N_OUT):
                chunk_done(dve, C_OUT1 + n)
                for m in (2 * n, 2 * n + 1):
                    link(v.scalar_tensor_tensor(xT[:, m, :], bank[1 + n][:, (m % 2) * T:(m % 2 + 1) * T],
                                                modv[:, 2 * KD + m, 0:1], xT[:, m, :], ALU.mult, ALU.add))
            v.memset(zr, 0.0).then_inc(x2_ready, 1)
            dve.wait_ge(rms_root, 1)
            link(v.reciprocal(rstd2, rstd2))
            link(v.tensor_tensor(h2T, xT, bc(rstd2, 1, KD), ALU.mult))
            for k in range(KD):
                ins = v.tensor_scalar(h2T[:, k, :], h2T[:, k, :], scale2[:, k:k + 1],
                                      modv[:, 3 * KD + k, 0:1], ALU.mult, ALU.add)
            ins.then_inc(h2_ready, 1)
            low = -3.0e38
            for t in range(NT):
                dve.wait_ge(keys_out, 2 * t + 2)
                halves = [(h, p) for h in range(PH) for p in range(2)]
                for first in (True, False):
                    r = slice(0, 8) if first else slice(8, 16)
                    for h, p in halves:
                        ins = v.max(topv[:, h, p, r], keyS[:, t, 2 * h + p, :])
                    link(ins)
                    for h, p in halves:
                        ins = v.max_index(topi[:, h, p, r], topv[:, h, p, r], keyS[:, t, 2 * h + p, :])
                    link(ins)
                    if first:
                        for h, p in halves:
                            s_ = keyS[:, t, 2 * h + p, :]
                            ins = v.match_replace(s_, topv[:, h, p, r], s_, low)
                        link(ins)
                link(v.tensor_copy(topf, topi))
                c4 = cand.rearrange("p h (a b) -> p h a b", a=TOPK)
                link(v.tensor_tensor(c4, bc(topv[:, :, 0, :], 3, TOPK), bc(topv[:, :, 1, :], 2, TOPK), ALU.add))
                best = gates[:, t, :].rearrange("p (h k) -> p h k", h=PH)
                pos3 = pos.rearrange("p (h k) -> p h k", h=PH)
                for first in (True, False):
                    r = slice(0, 8) if first else slice(8, 16)
                    for h in range(PH):
                        ins = v.max(best[:, h, r], cand[:, h, :])
                    link(ins)
                    for h in range(PH):
                        ins = v.max_index(pos3[:, h, r], best[:, h, r], cand[:, h, :])
                    link(ins)
                    if first:
                        for h in range(PH):
                            ins = v.match_replace(cand[:, h, :], best[:, h, r], cand[:, h, :], low)
                        link(ins)
                link(v.tensor_copy(gsum, best[:, :, 0]))
                v.tensor_tensor(best, best, bc(gsum, 2, TOPK), ALU.subtract).then_inc(top_exp, 1)
                link(v.tensor_scalar(posu[:, 0, :], pos, 4, None, ALU.logical_shift_right))
                link(v.tensor_scalar(posu[:, 1, :], pos, TOPK - 1, None, ALU.bitwise_and))
                link(v.tensor_copy(posf, posu))
                for p in range(2):
                    link(v.tensor_tensor(hot, bc(posf[:, p, :], 2, TOPK), bc(const[:, CN["iota"]], 1, SLOTS),
                                         ALU.is_equal))
                    h4 = hot.rearrange("p (h k) a -> p h k a", h=PH)
                    link(v.tensor_tensor(h4, h4, bc(topf[:, :, p, :], 2, TOPK), ALU.mult))
                    link(v.tensor_reduce(chosen[:, p, :], hot, AX, ALU.add))
                link(v.scalar_tensor_tensor(posf[:, 0, :], chosen[:, 0, :], float(NK), chosen[:, 1, :],
                                            ALU.mult, ALU.add))
                link(v.tensor_copy(expert[:, t, :], posf[:, 0, :]))
                dve.wait_ge(top_expd, t + 1)
                link(v.tensor_reduce(gsum, best, AX, ALU.add))
                link(v.reciprocal(gsum, gsum))
                v.tensor_tensor(best, best, bc(gsum, 2, TOPK), ALU.mult).then_inc(top_ready, 1)
            dve.wait_ge(top_ready, NT)
            v.memset(zeros, 0.0).then_inc(zero_set, 1)
            v.memset(zr, 0.0).then_inc(dot_done, 2)
            dve.wait_ge(tokens_out, 4)
            for t in range(NT):
                with dve.Fori(0, SLOTS // GS) as turn:
                    for j in range(GS):
                        dve.wait_ge(gathered[j], turn * 16 + 16 * (t * SLOTS // GS + 1))
                        dve.wait_ge(dot_done, turn * GS + (t * SLOTS + j + 1))
                        v.tensor_tensor_reduce(out=junk[:, j % 2], in0=G[:, j, 0:D], in1=h2[:, t, :], scale=1.0,
                                               scalar=0.0, op0=ALU.mult, op1=ALU.add,
                                               accum_out=dots[:, j // 4, j % 4:j % 4 + 1])\
                         .then_inc(dot_done, 1)
                for i in range(2):
                    dve.wait_ge(ffnT_done, 2 * t + i + 1)
                    for m in range(4 * i, 4 * i + 4):
                        x_ = xT[:, m, t * P:(t + 1) * P]
                        ins = v.scalar_tensor_tensor(x_, bank[5 + i][:, (m % 4) * P:(m % 4 + 1) * P],
                                                     modv[:, 5 * KD + m, 0:1], x_, ALU.mult, ALU.add)
            ins.then_inc(x2_ready, 1)
            dve.wait_ge(rms_root, 2)
            v.memset(cvin[:, :, 0:CONV - 1], 0.0)
            link(v.reciprocal(rstd3, rstd3))
            link(v.tensor_tensor(h3T, xT, bc(rstd3, 1, KD), ALU.mult))
            v.tensor_tensor(h3T, h3T, bc(small[:, SM["g3"]], 2, T), ALU.mult).then_inc(h3_ready, 1)
            dve.wait_ge(ab_done, 1)
            both = bank[5][:, 0:NT * 8].rearrange("p (t c) -> p t c", t=NT)
            flat = lambda a: a.rearrange("p t h -> p (t h)")
            link(v.tensor_tensor(ab[:, 0], both[:, :, 0:4], bc(rows[:, RW["dt"]], 1, NT), ALU.add))
            link(v.tensor_copy(beta.rearrange("p (t h) -> p t h", t=NT), both[:, :, 4:8]))
            link(v.tensor_scalar(spt[:, 2, :], flat(ab[:, 0]), -1.0, None, ALU.mult))
            v.tensor_tensor(spt[:, 0, :], flat(ab[:, 0]), spt[:, 2, :], ALU.min).then_inc(ab_exp, 1)
            dve.wait_ge(ab_expd, 1)
            e = spt[:, 1, :]
            link(v.tensor_scalar(spt[:, 2, :], e, 2.0, None, ALU.add))
            link(v.reciprocal(spt[:, 2, :], spt[:, 2, :]))
            link(v.tensor_tensor(spt[:, 3, :], e, spt[:, 2, :], ALU.mult))
            link(v.tensor_tensor(spt[:, 4, :], spt[:, 3, :], spt[:, 3, :], ALU.mult))
            link(v.tensor_scalar(spt[:, 2, :], spt[:, 4, :], 2.0 / 17, 2.0 / 15, ALU.mult, ALU.add))
            for k in (13, 11, 9, 7, 5, 3, 1):
                link(v.tensor_tensor(spt[:, 2, :], spt[:, 2, :], spt[:, 4, :], ALU.mult))
                link(v.tensor_scalar(spt[:, 2, :], spt[:, 2, :], 2.0 / k, None, ALU.add))
            link(v.tensor_tensor(spt[:, 2, :], spt[:, 2, :], spt[:, 3, :], ALU.mult))
            link(v.scalar_tensor_tensor(spt[:, 3, :], flat(ab[:, 0]), 0.0, spt[:, 2, :], ALU.max, ALU.add))
            link(v.tensor_tensor(g8.rearrange("p (t h) -> p t h", t=NT),
                                 spt[:, 3, :].rearrange("p (t h) -> p t h", t=NT), bc(kd[:, 0:4], 1, NT),
                                 ALU.mult))
            link(v.tensor_scalar(g8, g8, -1.0, None, ALU.mult))
            link(v.tensor_scalar(beta, beta, 1.0, None, ALU.add))
            v.reciprocal(beta, beta).then_inc(g_ready, 1)
            dve.wait_ge(in2_out, 12)
            cw = small[:, SM["conv"]].rearrange("p (b i) -> p b i", i=CONV)
            for i in range(CONV):
                for b in range(12):
                    src = cvin[:, b, i:i + T]
                    if i == 0:
                        ins = v.tensor_scalar(cvT[:, b, :], src, cw[:, b, 0:1], None, ALU.mult)
                    else:
                        ins = v.scalar_tensor_tensor(cvT[:, b, :], src, cw[:, b, i:i + 1], cvT[:, b, :],
                                                     ALU.mult, ALU.add)
                if i < CONV - 1:
                    link(ins)
            ins.then_inc(conv_ready, 1)
            dve.wait_ge(conv_silu, 1)
            qk = cvT[:, 0:8, :]
            v.tensor_tensor(nsq, qk, qk, ALU.mult).then_inc(lnorm_sq, 1)
            dve.wait_ge(lnorm_root, 1)
            link(v.reciprocal(nrm, nrm))
            link(v.tensor_tensor(qk, qk, nrm, ALU.mult))
            v.tensor_scalar(cvT[:, 0:4, :], cvT[:, 0:4, :], GD ** -0.5, None, ALU.mult)\
             .then_inc(lnorm_done, 1)
            dve.wait_ge(g_done, 2)
            last = gR[:, :, P - 1]
            link(v.tensor_tensor(gM, gR, bc(gc, 2, P), ALU.subtract))
            link(v.tensor_scalar(gD, gM, 0.0, -1.0, ALU.max, ALU.mult))
            link(v.tensor_scalar(gDT, gM, 0.0, None, ALU.min))
            v.tensor_tensor(kd, last, gc, ALU.subtract).then_inc(gx_ready, 1)
            dve.wait_ge(gx_exp, 1)
            link(v.tensor_tensor(gDT, gDT, bc(const[:, CN["upper"]], 1, 8), ALU.mult))
            dve.wait_ge(kk_done, 1)
            for p in range(8):
                ins = v.scalar_tensor_tensor(gA[:, p, :], bank[3 + p // 4][:, (p % 4) * P:(p % 4 + 1) * P],
                                             beta[:, p:p + 1], gD[:, p, :], ALU.mult, ALU.mult)
            ins.then_inc(a_ready, 1)
            link(v.tensor_tensor(bg, beta, egc, ALU.mult))
            dve.wait_ge(tm_out, 4)
            link(v.tensor_tensor(vTM, vTM, bc(beta, 2, P), ALU.mult))
            dve.wait_ge(a_ready, 1)
            link(v.tensor_tensor(gD[:, 4:8, :], kTM[:, 4:8, :], bc(bg[:, 4:8], 2, P), ALU.mult))
            link(v.tensor_tensor(gD[:, 0:4, :], kTM[:, 0:4, :], bc(kd[:, 0:4], 2, P), ALU.mult))
            link(v.tensor_tensor(gR[:, 4:8, :], cvT[:, 0:4, P:2 * P], gR[:, 4:8, :], ALU.mult))
            dve.wait_ge(at_out, 1)
            dve.wait_ge(masks_here, 32)

            def masked(out, a, which, s):
                link(v.tensor_tensor(out, a, bc(masks[:, which, s, :], 1, 8), ALU.mult))

            masked(gM, gA, 0, 0)
            masked(gMT, gAT, 1, 0)
            link(v.tensor_tensor(gT_, bc(ident, 1, 8), gM, ALU.subtract))
            link(v.tensor_tensor(gTT, bc(ident, 1, 8), gMT, ALU.subtract))
            for s in range(1, LEVELS):
                masked(gM, gA, 0, s)
                link(v.tensor_tensor(gMT, gAT, bc(masks[:, 1, s, :], 1, 8), ALU.mult))
                v.memset(zr, 0.0).then_inc(level_ready, 1)
                dve.wait_ge(t_done, s)
                for i in range(2):
                    q4 = slice(4 * i, 4 * i + 4)
                    link(v.tensor_tensor(gT_[:, q4, :], gT_[:, q4, :],
                                         bank[3 + i][:, :].rearrange("p (a b) -> p a b", a=4), ALU.subtract))
                    link(v.tensor_tensor(gTT[:, q4, :], gTT[:, q4, :],
                                         bank[5 + i][:, :].rearrange("p (a b) -> p a b", a=4), ALU.subtract))
            v.memset(zr, 0.0).then_inc(uv_ready, 1)
            dve.wait_ge(pt_done, 1)
            for i in range(2):
                q4 = slice(4 * i, 4 * i + 4)
                ins = v.tensor_tensor(gM[:, q4, :], gDT[:, q4, :],
                                      bank[5 + i][:, :].rearrange("p (a b) -> p a b", a=4), ALU.mult)
            ins.then_inc(pt_ready, 1)
            dve.wait_ge(u1_done, 1)
            v.tensor_tensor(gU[:, 4:8, :], gU[:, 4:8, :],
                            bank[3][:, :].rearrange("p (a b) -> p a b", a=4), ALU.subtract).then_inc(u1_ready, 1)
            dve.wait_ge(o_done, 1)
            for c in range(2):
                link(v.tensor_copy(Y2[:, c, 512:1024], bank[1 + c][:, :]))
                link(v.tensor_tensor(vTM[:, 4 * c:4 * c + 4, :].rearrange("p a b -> p (a b)"),
                                     Y2[:, c, 512:1024], Y2[:, c, 512:1024], ALU.mult))
            link(v.tensor_reduce(ms2, vTM, AX, ALU.add))
            v.memset(zr, 0.0).then_inc(y2_ms, 1)
            for h in range(MH):
                b = bank[3 + h % 2]
                dve.wait_ge(moba_s, h + 1)
                if h >= 1:
                    dve.wait_ge(moba_T, h)
                causal = const[:, CN["causal"]]
                link(v.scalar_tensor_tensor(soft[:, 0:P], b[:, 0:P], MD ** -0.5, causal, ALU.mult, ALU.add))
                link(v.tensor_scalar(soft[:, P:2 * P], b[:, P:2 * P], MD ** -0.5, None, ALU.mult))
                link(v.scalar_tensor_tensor(soft[:, 2 * P:3 * P], b[:, 2 * P:3 * P], MD ** -0.5, causal,
                                            ALU.mult, ALU.add))
                link(v.reduce_max(mx[:, 0, 0:1], soft[:, 0:P], AX))
                link(v.reduce_max(mx[:, 0, 1:2], soft[:, P:3 * P], AX))
                v.tensor_scalar(mx[:, 1, :], mx[:, 0, :], -1.0, None, ALU.mult).then_inc(moba_m, 1)
            dve.wait_ge(y2_root, 1)
            link(v.reciprocal(ms2, ms2))
            for c in range(2):
                y = Y2[:, c, 512:1024]
                y3 = y.rearrange("p (h e) -> p h e", h=GH)
                link(v.tensor_tensor(y3, y3, bc(ms2[:, 4 * c:4 * c + 4], 2, GD), ALU.mult))
                link(v.tensor_tensor(y3, y3, bc(rows[:, RW["gdn_g"]], 1, GH), ALU.mult))
                link(v.tensor_tensor(y, y, gz[:, c, :], ALU.mult))
            dve.wait_ge(moba_e, MH)
            link(v.reciprocal(rz, rz))
            dve.wait_ge(moba_y, MH)
            for t in range(NT):
                ins = v.tensor_tensor(Y2[:, t, 0:512].rearrange("p (h e) -> p h e", h=MH),
                                      bank[1 + t][:, :].rearrange("p (h e) -> p h e", h=MH),
                                      bc(rz[:, t, :], 2, MD), ALU.mult)
            ins.then_inc(mix2_ready, 1)
            for n in range(N_OUT):
                chunk_done(dve, C_OUT2 + n)
                x_ = xT[:, 2 * n:2 * n + 2, :]
                ins = v.tensor_tensor(x_, x_, bank[1 + n][:, :].rearrange("p (k t) -> p k t", k=2), ALU.add)
            ins.then_inc(x3_ready, 1)
            dve.wait_ge(rms_root, 3)
            link(v.reciprocal(rstd4, rstd4))
            link(v.tensor_tensor(h4T, xT, bc(rstd4, 1, KD), ALU.mult))
            v.tensor_tensor(h4T, h4T, bc(small[:, SM["g4"]], 2, T), ALU.mult).then_inc(h4_ready, 1)
            dve.wait_ge(route_done, 1)
            link(v.tensor_copy(logit, bank[4][:, 0:NT * (NG + NE)].rearrange("p (t e) -> p t e", t=NT)))
            link(v.memset(pad8, low))
            link(v.tensor_copy(pad8[:, :, 0:NG], logit[:, :, 0:NG]))
            for t in range(NT):
                link(v.max(gm8[:, t, :], pad8[:, t, :]))
                link(v.max_index(gi8[:, t, :], gm8[:, t, :], pad8[:, t, :]))
            link(v.tensor_copy(gif, gi8))
            iota = const[:, CN["iota"]]
            link(v.tensor_tensor(ghot, bc(iota[:, 0:NG], 1, NT), bc(gif[:, :, 0], 2, NG), ALU.is_equal))
            for t in range(NT):
                link(v.tensor_tensor(gsel[:, t], logit[:, t, NG:].rearrange("p (g e) -> p e g", g=NG),
                                     bc(ghot[:, t, :], 1, EG), ALU.mult))
            link(v.tensor_reduce(ing, gsel, AX, ALU.add))
            for t in range(NT):
                link(v.max(im8[:, t, :], ing[:, t, :]))
                link(v.max_index(ii8[:, t, :], im8[:, t, :], ing[:, t, :]))
            link(v.tensor_copy(iif, ii8))
            link(v.tensor_tensor(pw[:, :, 0], im8[:, :, 1], im8[:, :, 0], ALU.subtract))
            v.tensor_tensor(gex, logit[:, :, 0:NG], bc(gm8[:, :, 0], 2, NG), ALU.subtract).then_inc(route_exp, 1)
            for r in range(2):
                link(v.tensor_tensor(within[:, r], bc(iota[:, 0:EG], 1, NT), bc(iif[:, :, r], 2, EG),
                                     ALU.is_equal))
            dve.wait_ge(numbers_ready, 1)
            for t in range(NT):
                by_group = lambda a: a.rearrange("p (g e) -> p g e", g=NG)
                link(v.tensor_tensor(by_group(tags[:, t, :, 1]), bc(ghot[:, t, :], 2, EG),
                                     bc(within[:, 1, t, :], 1, NG), ALU.mult))
                link(v.tensor_tensor(by_group(rank_in[:, t]), bc(ghot[:, t, :], 2, EG),
                                     bc(within[:, 0, t, :], 1, NG), ALU.mult))
            link(v.tensor_copy(tags[:, :, :, 0], bc(token_no, 2, NE)))
            v.tensor_tensor(rank_in, rank_in, tags[:, :, :, 1], ALU.add).then_inc(chosen_ready, 1)
            dve.wait_ge(route_done, 2)
            v.tensor_tensor(rank, rank_in, bank[4][:, P:P + NT * NE].rearrange("p (t e) -> p t e", t=NT),
                            ALU.mult).then_inc(rank_ready, 1)
            dve.wait_ge(rank_ready, 1)
            for t in range(NT):
                v.tensor_tensor(hot4[:, t], bc(slot_no[:, 0], 1, NE), bc(rank[:, t], 2, P),
                                ALU.is_equal).then_inc(hot_ready, 1)
            v.tensor_tensor(hot4[:, 2], bc(slot_no[:, 1], 1, NE), bc(rank[:, 1], 2, P),
                            ALU.is_equal).then_inc(hot_ready, 1)
            link(v.tensor_reduce(most[:, 0:1], bank[4][:, P + NT * NE:P + (NT + 1) * NE], AX, ALU.max))
            link(v.tensor_scalar(most[:, 1:2], most[:, 0:1], float(P), float(PAIRS), ALU.is_gt, ALU.mult))
            link(v.tensor_scalar(pairs, most[:, 1:2], float(PAIRS), None, ALU.add))
            link(v.memset(from_row, NONE))
            link(v.memset(to_row, NONE))
            dve.wait_ge(route_expd, 1)
            link(v.tensor_reduce(pw[:, :, 3], gex, AX, ALU.add))
            link(v.reciprocal(pw[:, :, 3], pw[:, :, 3]))
            link(v.tensor_scalar(pw[:, :, 2], pw[:, :, 1], 1.0, None, ALU.add))
            link(v.reciprocal(pw[:, :, 2], pw[:, :, 2]))
            link(v.tensor_tensor(pw[:, :, 2], pw[:, :, 2], pw[:, :, 3], ALU.mult))
            link(v.tensor_tensor(pw[:, :, 3], pw[:, :, 2], pw[:, :, 1], ALU.mult))
            dve.wait_ge(route_done, 3)
            link(v.tensor_copy(slotv, bank[5][:, 0:2 * WINDOWS * NE]
                               .rearrange("p (n a) -> p n a", a=2)))
            link(v.tensor_scalar(absent, slotv[:, :, 0], 0.0, float(NONE), ALU.is_equal, ALU.mult))
            link(v.tensor_tensor(absent, absent, slotv[:, :, 0], ALU.add))
            n_ = WINDOWS * NE
            link(v.tensor_scalar(from_row[:, 0:n_], absent, -1.0, None, ALU.add))
            link(v.tensor_scalar(absent, absent, 2.0, -2.0, ALU.mult, ALU.add))
            v.tensor_tensor(to_row[:, 0:n_], absent, slotv[:, :, 1], ALU.add).then_inc(slots_ready, 1)
            v.memset(zz, 0.0).then_inc(y_right, 2)

            def turned_rows(b, wait_n):
                dve.wait_ge(x_turned, wait_n)
                v.tensor_copy(XT[:, b, 4:8].rearrange("p k t -> p (k t)"), bank[1][:, :]).then_inc(xt_right, 1)

            for b in range(2):
                turned_rows(b, b + 1)
            dve.wait_ge(slots_ready, 1)
            n_pairs = dve.value_load(pairs[0:1, 0:1], min_val=PAIRS, max_val=WINDOWS * PAIRS)
            with dve.Fori(0, n_pairs) as i:
                for b in range(2):
                    dve.wait_ge(silu_ready, 2 * i + (b + 1))
                    v.tensor_tensor(hid[:, b], bank[2 + b][:, FF:2 * FF], sg[:, b], ALU.mult).then_inc(hid_ready, 1)
                for b in range(2):
                    dve.wait_ge(hid_turned, 2 * i + (b + 1))
                    v.tensor_copy(hidT[:, b].rearrange("p k t -> p (k t)"), bank[2 + b][:, 0:FF])\
                     .then_inc(hidT_ready, 1)
                    turned_rows(b, 2 * i + (b + 3))
                    dve.wait_ge(scattered[b], 16 * i + 16)
                    dve.wait_ge(down_used, 2 * i + (b + 1))
                    v.tensor_copy(Yx[:, b, 512:1024], bank[5 + 2 * b][:, :]).then_inc(y_right, 1)
            for t in range(NT):
                dve.wait_ge(y_back, 16 * NT)
                for r in range(2):
                    ins = v.scalar_tensor_tensor(x3[:, t], back[:, t, r], pw[:, t, 2 + r:3 + r], x3[:, t],
                                                 ALU.mult, ALU.add)
                    if r == 0:
                        link(ins)
                ins.then_inc(x4_ready, 1)
            for t in range(NT):
                dve.wait_ge(rms_root, 4 + t)
                link(v.reciprocal(ms4[:, t:t + 1], ms4[:, t:t + 1]))
                v.scalar_tensor_tensor(x3[:, t], x3[:, t], ms4[:, t:t + 1], final_g,
                                       ALU.mult, ALU.mult).then_inc(out_ready, 1)

        @block.tensor
        def _(pe):
            mm = nc.tensor.matmul
            pe.wait_ge(const_here, 32)
            for i, s in enumerate((sq, csq)):
                pe.wait_ge(squares1, i + 1)
                for k in range(KD):
                    ins = mm(bank[7][:, i * T:(i + 1) * T], ones, s[:, k, :], start=k == 0, stop=k == KD - 1)
            ins.then_inc(sums1, 1)
            pe.wait_ge(cond_ready, 1)
            with pe.Fori(0, N_MOD // WSLOTS) as turn:
                for s in range(WSLOTS):
                    pe.wait_ge(chunk_here[s], turn * 16 + 16)
                    w = wchunk(s)
                    for j in range(2):
                        at = turn * (4 * WSLOTS) + (4 * s + 2 * j)
                        for k in range(KD):
                            ins = mm(bank[0][:, bass.ds(at, 2)], w[:, k, j * P:(j + 1) * P], condS[:, k, :],
                                     start=k == 0, stop=k == KD - 1)
                    ins.then_inc(chunk_used, 1)
            pe.wait_ge(h_ready, 1)
            n_c = 0
            for n in range(N_IN1):
                chunk_ready(pe, C_IN1 + n)
                w = wchunk(C_IN1 + n)
                if n >= 2:
                    pe.wait_ge(proj_x_out, n - 1)
                groups = [(bank[1 + 2 * (n % 2)], hT)]
                if n in CTX_CHUNKS:
                    n_c += 1
                    if n_c >= 2:
                        pe.wait_ge(proj_c_out, n_c - 1)
                    groups.append((bank[2 + 2 * (n % 2)], chT))
                for out, h in groups:
                    for t in range(NT):
                        for k in range(KD):
                            ins = mm(out[:, t * COLS:(t + 1) * COLS], h[:, k, t * P:(t + 1) * P],
                                     w[:, k, :], start=k == 0, stop=k == KD - 1)
                ins.then_inc(chunk_used, 1)
            pe.wait_ge(roped, 1)
            sources = [(proj, 0), (proj, 256), (cproj, 0)]
            sources += [(proj, 1536 + 256 * i) for i in range(4)] + [(cproj, 768 + 256 * i) for i in range(2)]
            for i, (src, at) in enumerate(sources):
                if i >= 2:
                    pe.wait_ge(turned_out, i - 1)
                for b in range(2):
                    for t in range(NT):
                        ins = nc.tensor.transpose(bank[5 + i % 2][:, b * T + t * P:b * T + (t + 1) * P],
                                                  src[:, t, at + b * P:at + (b + 1) * P], ident)
                ins.then_inc(turned, 1)
            pe.wait_ge(turned_out, len(sources))

            def scores(h):
                r = slice(RK * (h % 2), RK * (h % 2) + RK)
                if h >= 2:
                    pe.wait_ge(ret_masked, h - 1)
                for k in range(4):
                    ins = mm(bank[1 + 2 * (h % 2) + k // 2][:, (k % 2) * T:(k % 2 + 1) * T],
                             rkT[r, h // 2, k * P:(k + 1) * P], rqT[r, h // 2, :], start=True, stop=True)
                ins.then_inc(ret_scores, 1)

            def outputs(h):
                pe.wait_ge(ret_masked, h + 1)
                for t in range(NT):
                    for k in range(4):
                        val = cproj[:, k, 256 + h * RV:256 + (h + 1) * RV] if k < 2 else \
                            proj[:, k - 2, 512 + h * RV:512 + (h + 1) * RV]
                        ins = mm(bank[(0, 7)[h // 2]][:, (h % 2) * 256 + t * P:(h % 2) * 256 + (t + 1) * P],
                                 SD[:, h % 2, k, t * P:(t + 1) * P], val, start=k == 0, stop=k == 3)
                ins.then_inc(ret_y, 1)

            scores(0)
            for h in range(RH):
                if h + 1 < RH:
                    scores(h + 1)
                outputs(h)

            def diff_scores_of(i):
                h, t = i // NT, i % NT
                if i >= 2:
                    pe.wait_ge(diff_exp, 2 * i - 2)
                for c in range(2):
                    r = slice(DD * c, DD * (c + 1))
                    mm(bank[1 + 2 * (i % 2) + c][:, :], dqT[r, h, t * P:(t + 1) * P], dkT[r, h, :],
                       start=True, stop=True).then_inc(diff_scores, 1)

            def diff_outputs_of(i):
                h, t = i // NT, i % NT
                pe.wait_ge(diff_a, i + 1)
                if i >= 2:
                    pe.wait_ge(diff_aT_out, i - 1)
                for k in range(4):
                    ins = nc.tensor.transpose(bank[5 + i % 2][:, k * P:(k + 1) * P],
                                              tmp[:, 0, k * P:(k + 1) * P], ident)
                ins.then_inc(diff_aT, 1)
                pe.wait_ge(diff_aT_out, i + 1)
                if h % 2 == 0 and t == 0:
                    pe.wait_ge(ret_y_out, h // 2 + 1)
                for k in range(4):
                    val = cproj[:, k, 1280 + h * RV:1280 + (h + 1) * RV] if k < 2 else \
                        proj[:, k - 2, 2560 + h * RV:2560 + (h + 1) * RV]
                    ins = mm(bank[(0, 7)[h // 2]][:, (h % 2) * 256 + t * P:(h % 2) * 256 + (t + 1) * P],
                             aT[:, i % 2, k, :], val, start=k == 0, stop=k == 3)
                ins.then_inc(diff_y, 1)

            pe.wait_ge(ret_masked, RH)
            diff_scores_of(0)
            for i in range(DH * NT):
                if i + 1 < DH * NT:
                    diff_scores_of(i + 1)
                diff_outputs_of(i)
            pe.wait_ge(mix_ready, NT)
            for g in range(4):
                if g >= 2:
                    pe.wait_ge(mixT_out, g - 1)
                for b in range(2):
                    for t in range(NT):
                        ins = nc.tensor.transpose(bank[5 + g % 2][:, b * T + t * P:b * T + (t + 1) * P],
                                                  Y[:, t, (2 * g + b) * P:(2 * g + b + 1) * P], ident)
                ins.then_inc(mixT_done, 1)
            pe.wait_ge(mixT_out, 4)
            project_fm(pe, C_OUT1, N_OUT, mixT)
            sums_over_features(pe, sq2, 1)
            pe.wait_ge(h2_ready, 1)
            for n in range(N_Q):
                if n >= 4:
                    pe.wait_ge(q_out, n - 3)
                project_fm(pe, C_Q + n, 1, h2T, at=n)
            for g in range(4):
                if g >= 2:
                    pe.wait_ge(tokens_out, g - 1)
                t = g // 2
                transposes(pe, bank[5 + g % 2], [h2T[:, 4 * (g % 2) + k, t * P:(t + 1) * P] for k in range(4)])\
                    .then_inc(tokens_turned, 1)
            pe.wait_ge(q_out, N_Q)
            chunk_ready(pe, C_SK)
            s_ = C_SK % WSLOTS
            keys = wring[:, s_ * CHUNK:(s_ + 1) * CHUNK].rearrange("p (h n) -> p h n", h=2 * PH)
            for i in range(2 * NT):
                t = i // 2
                if i >= 2:
                    pe.wait_ge(keys_out, i - 1)
                for q in range(8):
                    hp = 8 * (i % 2) + q
                    ins = mm(bank[(1, 3)[i % 2] + q // 4][:, (q % 4) * P:(q % 4 + 1) * P],
                             qT[:, hp, t * P:(t + 1) * P], keys[:, hp, :], start=True, stop=True)
                ins.then_inc(keys_done if i < 2 * NT - 1 else chunk_used, 1)
            pe.wait_ge(keys_out, 2 * NT)
            pe.wait_ge(zero_set, 1)
            for b in range(1, 5):
                mm(bank[b][:, :], zeros[:, 0:P], zeros, start=True, stop=False, skip_group_check=True)
            for t in range(NT):
                with pe.Fori(0, SLOTS // GS) as turn:
                    for j in range(GS):
                        pe.wait_ge(diag_ready, turn * GS + (t * SLOTS + j + 1))
                        for c in range(2):
                            ins = mm(bank[1 + 2 * t + c][:, :], diag[:, j, :],
                                     G[:, j, D + c * 512:D + (c + 1) * 512], start=False, stop=False,
                                     skip_group_check=True)
                        ins.then_inc(slot_used, 1)
                pe.wait_ge(ffn_out, t + 1)
                for i in range(2):
                    transposes(pe, bank[5 + i], [ffn[:, (4 * i + k) * P:(4 * i + k + 1) * P] for k in range(4)])\
                        .then_inc(ffnT_done, 1)
            sums_over_features(pe, sq3, 2)
            pe.wait_ge(h3_ready, 1)
            pe.wait_ge(masks_here, 32)
            for t in range(NT):
                for k in range(KD):
                    ins = mm(bank[5][:, t * 8:(t + 1) * 8], h3T[:, k, t * P:(t + 1) * P], gate2[:, k, :],
                             start=k == 0, stop=k == KD - 1)
            ins.then_inc(ab_done, 1)
            for n in range(N_IN2):
                if n >= 4:
                    pe.wait_ge(in2_out, n - 3)
                if n in (4, 5, 12, 13):
                    chunk_ready(pe, C_IN2 + n)
                    for t in range(NT):
                        for k in range(KD):
                            ins = mm(bank[1 + n % 4][:, t * COLS:(t + 1) * COLS], h3T[:, k, t * P:(t + 1) * P],
                                     wchunk(C_IN2 + n)[:, k, :], start=k == 0, stop=k == KD - 1)
                    ins.then_inc(chunk_used, 1)
                else:
                    project_fm(pe, C_IN2 + n, 1, h3T, at=n)
            pe.wait_ge(lnorm_sq, 1)
            pe.wait_ge(in2_out, N_IN2)
            for i in range(4):
                ins = mm(bank[1 + i][:, :], ones, nsq[:, 2 * i:2 * i + 2, :].rearrange("p a b -> p (a b)"),
                         start=True, stop=True)
            ins.then_inc(lnorm_sum, 1)
            pe.wait_ge(g_ready, 1)
            mm(bank[7][:, 0:8], const[:, CN["upper"]], g8, start=True, stop=True)
            for p in range(8):
                ins = mm(bank[5 + p // 4][:, (p % 4) * P:(p % 4 + 1) * P], bc(g8[:, p], 1, P),
                         const[:, CN["upper"]], start=True, stop=True)
            ins.then_inc(g_done, 1)
            pe.wait_ge(lnorm_done, 1)
            for p in range(8):
                c, h = p // 4, p % 4
                kT = cvT[:, 4 + h, c * P:(c + 1) * P]
                ins = mm(bank[3 + p // 4][:, (p % 4) * P:(p % 4 + 1) * P], kT, kT, start=True, stop=True)
            ins.then_inc(kk_done, 1)
            pe.wait_ge(g_done, 2)
            for i in range(2):
                for c in range(2):
                    if i:
                        pe.wait_ge(tm_out, c + 1)
                    transposes(pe, bank[5 + c], [cvT[:, 4 + 4 * i + h, c * P:(c + 1) * P] for h in range(4)])\
                        .then_inc(tm_done, 1)
            pe.wait_ge(a_ready, 1)
            pe.wait_ge(tm_out, 4)
            for i in range(2):
                ins = transposes(pe, bank[5 + i], [gA[:, 4 * i + k, :] for k in range(4)])
            ins.then_inc(at_done, 1)
            pe.wait_ge(at_out, 1)
            for s in range(1, LEVELS):
                pe.wait_ge(level_ready, s)
                for p in range(8):
                    ins = mm(bank[1 + p // 4][:, (p % 4) * P:(p % 4 + 1) * P], gMT[:, p, :], gT_[:, p, :],
                             start=True, stop=True)
                ins.then_inc(w_done, 1)
                pe.wait_ge(w_out, s)
                for p in range(8):
                    mm(bank[3 + p // 4][:, (p % 4) * P:(p % 4 + 1) * P], gTT[:, p, :], gW[:, p, :],
                       start=True, stop=True)
                    ins = mm(bank[5 + p // 4][:, (p % 4) * P:(p % 4 + 1) * P], gW[:, p, :], gTT[:, p, :],
                             start=True, stop=True)
                ins.then_inc(t_done, 1)
            pe.wait_ge(uv_ready, 1)
            for p in range(8):
                mm(bank[1 + p // 4][:, (p % 4) * P:(p % 4 + 1) * P], gTT[:, p, :], vTM[:, p, :],
                   start=True, stop=True)
            for h in range(GH):
                ins = mm(bank[3][:, h * P:(h + 1) * P], gD[:, 4 + h, :], gTT[:, 4 + h, :], start=True, stop=True)
            ins.then_inc(uv_done, 1)
            for p in range(8):
                c, h = p // 4, p % 4
                ins = mm(bank[5 + p // 4][:, (p % 4) * P:(p % 4 + 1) * P], cvT[:, 4 + h, c * P:(c + 1) * P],
                         cvT[:, h, c * P:(c + 1) * P], start=True, stop=True)
            ins.then_inc(pt_done, 1)
            pe.wait_ge(uv_out, 1)
            for h in range(GH):
                ins = mm(bank[4][:, h * P:(h + 1) * P], gD[:, h, :], gU[:, h, :], start=True, stop=True)
            ins.then_inc(s_done, 1)
            pe.wait_ge(s_out, 1)
            for h in range(GH):
                ins = mm(bank[3][:, h * P:(h + 1) * P], gwT[:, h, :], gS[:, h, :], start=True, stop=True)
            ins.then_inc(u1_done, 1)
            pe.wait_ge(pt_ready, 1)
            pe.wait_ge(u1_ready, 1)
            for p in range(8):
                out = bank[1 + p // 4][:, (p % 4) * P:(p % 4 + 1) * P]
                ins = mm(out, gM[:, p, :], gU[:, p, :], start=True, stop=p < 4)
                if p >= 4:
                    ins = mm(out, gR[:, p, :], gS[:, p - 4, :], start=False, stop=True)
            ins.then_inc(o_done, 1)

            def moba_scores(h):
                r = slice(MD * (h % 2), MD * (h % 2) + MD)
                if h >= 2:
                    pe.wait_ge(moba_m, h - 1)
                mm(bank[3 + h % 2][:, 0:P], mqT[r, h // 2, 0:P], mkT[r, h // 2, 0:P], start=True, stop=True)
                mm(bank[3 + h % 2][:, P:3 * P], mqT[r, h // 2, P:2 * P], mkT[r, h // 2, :],
                   start=True, stop=True).then_inc(moba_s, 1)

            pe.wait_ge(y2_ms, 1)
            moba_scores(0)
            for h in range(MH):
                if h + 1 < MH:
                    moba_scores(h + 1)
                pe.wait_ge(moba_e, h + 1)
                if h >= 1:
                    pe.wait_ge(moba_T_out, h)
                transposes(pe, bank[7], [soft[:, k * P:(k + 1) * P] for k in range(3)]).then_inc(moba_T, 1)
                pe.wait_ge(moba_T_out, h + 1)
                cols = slice(h * MD, (h + 1) * MD)
                mm(bank[1][:, cols], softT[:, 0:P], mv[:, 0, cols], start=True, stop=True)
                for k in range(2):
                    ins = mm(bank[2][:, cols], softT[:, (1 + k) * P:(2 + k) * P], mv[:, k, cols],
                             start=k == 0, stop=k == 1)
                ins.then_inc(moba_y, 1)
            pe.wait_ge(mix2_ready, 1)
            for g in range(4):
                if g >= 2:
                    pe.wait_ge(mixT_out, 4 + g - 1)
                transposes(pe, bank[5 + g % 2], [Y2[:, t, (2 * g + b) * P:(2 * g + b + 1) * P]
                                                 for b in range(2) for t in range(NT)]).then_inc(mixT_done, 1)
            pe.wait_ge(mixT_out, 8)
            project_fm(pe, C_OUT2, N_OUT, mix2T)
            sums_over_features(pe, sq4, 3)
            pe.wait_ge(h4_ready, 1)
            pe.wait_ge(route_here, 32)
            for t in range(NT):
                for k in range(KD):
                    ins = mm(bank[4][:, t * (NG + NE):(t + 1) * (NG + NE)], h4T[:, k, t * P:(t + 1) * P],
                             routeW[:, k, :], start=k == 0, stop=k == KD - 1)
            ins.then_inc(route_done, 1)
            for g in range(8):
                if g >= 4:
                    pe.wait_ge(tokens_out, 4 + g - 3)
                src, t = (h4T if g < 4 else xT), (g // 2) % 2
                transposes(pe, bank[g % 4], [src[:, 4 * (g % 2) + k, t * P:(t + 1) * P] for k in range(4)])\
                    .then_inc(tokens_turned, 1)
            pe.wait_ge(chosen_ready, 1)
            upper = const[:, CN["upper"]]
            places = lambda n: bank[4][:, P + n * NE:P + (n + 1) * NE]
            mm(places(0), upper, rank_in[:, 0], start=True, stop=True)
            mm(places(1), upper, rank_in[:, 1], start=True, stop=False)
            mm(places(1), ones, rank_in[:, 0], start=False, stop=True)
            mm(places(2), ones, rank_in[:, 0], start=True, stop=False)
            mm(places(2), ones, rank_in[:, 1], start=False, stop=True).then_inc(route_done, 1)
            slot_tags = lambda w, e: bank[5][:, 2 * (w * NE + e):2 * (w * NE + e + 1)]
            pe.wait_ge(hot_ready, NT)
            for e in range(NE):
                for t in range(NT):
                    mm(slot_tags(0, e), hot4[:, t, e], tags[:, t, e], start=t == 0, stop=t == NT - 1)
            pe.wait_ge(hot_ready, NT + 1)
            for e in range(NE):
                ins = mm(slot_tags(1, e), hot4[:, 2, e], tags[:, 1, e], start=True, stop=True)
            ins.then_inc(route_done, 1)

            def turn_rows(b, wait_gather, nth):
                pe.wait_ge(gathered[b], wait_gather)
                if nth is not None:
                    pe.wait_ge(xt_left, nth)
                    pe.wait_ge(xt_right, nth)
                for h in range(2):
                    ins = transposes(pe, bank[h], [X[:, b, (4 * h + k) * P:(4 * h + k + 1) * P] for k in range(4)])
                ins.then_inc(x_turned, 1)

            pe.wait_ge(tokens_out, 12)
            turn_rows(0, GATHERED + 16, None)
            turn_rows(1, GATHERED + 16, 1)
            n_pairs = pe.value_load(pairs[0:1, 0:1], min_val=PAIRS, max_val=WINDOWS * PAIRS)
            with pe.Fori(0, n_pairs) as i:
                for b in range(2):
                    pe.wait_ge(gu_here[b], i * 16 + 16)
                    pe.wait_ge(xt_left, 2 * i + (b + 1))
                    pe.wait_ge(xt_right, 2 * i + (b + 1))
                    w = wring[:, 2 * b * CHUNK:(2 * b + 2) * CHUNK].rearrange("p (k c) -> p k c", k=KD)
                    for k in range(KD):
                        ins = mm(bank[2 + b][:, :], XT[:, b, k], w[:, k, :], start=k == 0, stop=k == KD - 1)
                    ins.then_inc(gu_done, 1)
                for b in range(2):
                    pe.wait_ge(hid_ready, 2 * i + (b + 1))
                    transposes(pe, bank[2 + b], [hid[:, b, f * P:(f + 1) * P] for f in range(2)])\
                        .then_inc(hid_turned, 1)
                    turn_rows(b, i * 16 + (GATHERED + 32), 2 * i + (b + 2))
                    pe.wait_ge(down_here[b], i * 16 + 16)
                    pe.wait_ge(hidT_ready, 2 * i + (b + 1))
                    pe.wait_ge(y_left, 2 * i + (b + 1))
                    pe.wait_ge(y_right, 2 * i + (b + 1))
                    w = wring[:, (4 + b) * CHUNK:(5 + b) * CHUNK].rearrange("p (f c) -> p f c", f=2)
                    for h in range(2):
                        for f in range(2):
                            ins = mm(bank[4 + 2 * b + h][:, :], hidT[:, b, f], w[:, f, h * 512:(h + 1) * 512],
                                     start=f == 0, stop=f == 1)
                    ins.then_inc(down_used, 1)


CTX_CHUNKS = (1, 2, 3, 8, 9, 10, 11)


def turned_views(rqT, rkT, dqT, dkT):
    out = [rqT, rkT[:, :, T:2 * T], rkT[:, :, 0:T]]
    out += [dqT[:, 2 * i:2 * i + 2, :] for i in range(2)]
    out += [dkT[:, 2 * i:2 * i + 2, T:2 * T] for i in range(2)]
    out += [dkT[:, 2 * i:2 * i + 2, 0:T] for i in range(2)]
    return out


def constants():
    c = np.zeros((P, CN_N), np.float32)
    p = np.arange(P)
    c[:, CN["ident"]] = np.eye(P)
    c[:, CN["ones"]] = 1.0
    c[:, CN["eps"]] = EPS
    quarter = RK // 4
    freqs = (10000.0 ** (-np.arange(quarter, dtype=np.float32) / quarter)).astype(np.float32)
    t = np.arange(T)
    ar = (t // 64).astype(np.float32)[:, None] * freqs
    ac = (t % 64).astype(np.float32)[:, None] * freqs
    ang = np.concatenate([ar, ar, ac, ac], axis=1).astype(np.float64)
    sign = np.tile(np.repeat([-1.0, 1.0], quarter), 2)
    c[:, CN["cos"]] = np.cos(ang).reshape(NT, P, RK).transpose(1, 0, 2).reshape(P, -1)
    c[:, CN["sin"]] = (np.sin(ang) * sign).reshape(NT, P, RK).transpose(1, 0, 2).reshape(P, -1)
    dist = t[None, None, :] - (np.arange(NT)[None, :, None] * P + p[:, None, None])
    c[:, CN["dist"]] = dist.reshape(P, -1)
    c[:, CN["iota"]] = np.arange(TOPK)
    c[:, CN["upper"]] = p[:, None] <= p[None, :]
    c[:, CN["lower"]] = p[:, None] >= p[None, :]
    c[:, CN["causal"]] = np.where(p[:, None] >= p[None, :], 0.0, -1e30)
    masks = np.zeros((2, LEVELS, P, P), np.float32)
    for s in range(LEVELS):
        w = 1 << s
        low = (p[:, None] // w == p[None, :] // w + 1) & (p[:, None] // (2 * w) == p[None, :] // (2 * w))
        masks[0, s], masks[1, s] = low, low.T
    return c, np.ascontiguousarray(masks.transpose(2, 0, 1, 3)).reshape(P, -1)


def pack(w):
    n = w.shape[1] // COLS
    return w.reshape(KD, P, n, COLS).transpose(2, 1, 0, 3).reshape(n, P, CHUNK)


def fm(a, n):
    return a.reshape(n, P).T


def kernel(**inputs):
    import concourse.bacc as bacc
    from concourse.bass_utils import run_bass_kernel_spmd

    g = {k: np.asarray(a) for k, a in inputs.items()}
    cond = np.stack([g["c"][0], g["c_ctx"]], axis=-1).reshape(KD, P, 2).transpose(1, 0, 2).reshape(P, -1)
    conv = g["conv_w_2"][0].reshape(CONV, 12, P).transpose(2, 1, 0).reshape(P, -1)
    small = np.concatenate([cond, fm(g["b_mod"], 6 * KD), fm(g["norm1_g"], KD), fm(g["norm2_g"], KD),
                            fm(g["attn_norm_2"], KD), fm(g["ffn_norm_2"], KD), fm(g["final_norm_2"], KD),
                            conv], axis=1)
    row = np.concatenate([g[k].reshape(-1) for k in
                          ("ret_norm_g", "diff_norm_g", "diff_qk_norm_g", "diff_lambda", "ret_decay_logit",
                           "gdn_norm_2", "A_log_2", "dt_bias_2")])
    const, masks = constants()
    keys = g["peer_sub_keys"][0].reshape(2 * PH, NK, P).transpose(2, 0, 1).reshape(1, P, CHUNK)
    w2 = g["w_in_2"][0]
    stream = np.concatenate([pack(g["w_mod"][0]), pack(g["w_in"][0]), pack(g["w_out"][0]),
                             pack(g["peer_w_query"][0]), keys, pack(w2[:, :3584]), pack(g["w_out_2"][0])])
    fold = lambda w: w.reshape(KD, P, -1).transpose(1, 0, 2)
    gate_up = np.stack([g["w_gate_2"][0].reshape(NE, KD, P, FF), g["w_up_2"][0].reshape(NE, KD, P, FF)], axis=3)
    gate_up = gate_up.transpose(0, 2, 1, 3, 4).reshape(NE, P, 2 * CHUNK)
    down = g["w_down_2"][0].reshape(NE, FF // P, P, D).transpose(0, 2, 1, 3).reshape(NE, P, CHUNK)
    tokens = lambda x: fold(x[0].T)
    arrays = {
        "xT": tokens(g["x"]), "ctxT": tokens(g["ctx"]), "small": small,
        "rows": np.broadcast_to(row, (P, RW_N)), "const": const, "masks": masks, "stream": stream,
        "gate2": fold(w2[:, 3584:]).reshape(P, -1),
        "uv": np.concatenate([g["peer_u"][0], g["peer_v"][0]], axis=1),
        "route": fold(np.concatenate([g["w_group_2"][0], g["w_router_2"][0]], axis=1)).reshape(P, -1),
        "moe": np.concatenate([gate_up, down], axis=2),
        "final_g": np.broadcast_to(g["final_norm_2"], (P, D)),
    }
    arrays = {k: np.ascontiguousarray(a) for k, a in arrays.items()}
    nc = bacc.Bacc("TRN2", target_bir_lowering=False, num_devices=1)
    args = [nc.dram_tensor(f"{k}_in", a.shape, fp32, kind="ExternalInput").ap() for k, a in arrays.items()]
    out = nc.dram_tensor("out_dram", (T, D), fp32, kind="ExternalOutput").ap()
    h4_rows = nc.dram_tensor("h4_rows", (T, D), fp32, kind="Internal").ap()
    expert_rows = nc.dram_tensor("expert_rows", (2 * T, D), fp32, kind="Internal").ap()
    two_blocks(nc, *args, out, h4_rows, expert_rows)
    r = run_bass_kernel_spmd(nc, [{f"{k}_in": a for k, a in arrays.items()}], core_ids=[0])
    return r.results[0]["out_dram"].reshape(1, T, D)
```

```python
from contextlib import ExitStack

import numpy as np
import concourse.bass as bass
from concourse import mybir

P = 128
D = 1024
T = 256
NT = T // P
KD = D // P
EPS = 1e-6
RH, RK, RV = 4, 64, 128
DH, DD = 4, 64
IN1 = 3072
PH, NK, TOPK = 8, 128, 16
SLOTS = PH * TOPK
MH, MD = 8, 64
GH, GD = 4, 128
CONV = 4
NG, EG, FF = 4, 8, 256
NE = NG * EG
LAM_INIT = 0.2

CHUNK = 2048
COLS = CHUNK // KD
N_IN1 = IN1 // COLS
N_OUT = D // COLS
N_Q = 2 * PH * NK // COLS
N_SK = 1
N_IN2 = 3584 // COLS
MOD_GROUP = D // COLS
C_IN1 = 2 * MOD_GROUP
C_OUT1 = C_IN1 + N_IN1 + 3 * MOD_GROUP
C_Q = C_OUT1 + N_OUT
C_SK = C_Q + 1
C_IN2 = C_Q + N_Q + N_SK + MOD_GROUP
C_MOD = [0, MOD_GROUP] + [C_IN1 + N_IN1 + i * MOD_GROUP for i in range(3)] + [C_Q + N_Q + N_SK]
C_OUT2 = C_IN2 + N_IN2
N_CHUNKS = C_OUT2 + N_OUT
WSLOTS = 8

SM = {}
_at = 0
for _name, _n in [("cond", 16), ("b_mod", 48), ("g1", 8), ("g2", 8), ("g3", 8), ("g4", 8), ("g5", 8),
                  ("conv", 48)]:
    SM[_name] = slice(_at, _at + _n)
    _at += _n
SM_N = _at
RW = {}
_at = 0
for _name, _n in [("ret_g", 512), ("diff_g", 512), ("qk_g", 128), ("lam", 256), ("decay", 8),
                  ("gdn_g", 128), ("A_log", 4), ("dt", 4)]:
    RW[_name] = slice(_at, _at + _n)
    _at += _n
RW_N = _at
CN = {}
_at = 0
for _name, _n in [("ident", 128), ("ones", 128), ("cos", NT * 64), ("sin", NT * 64), ("dist", NT * T),
                  ("iota", 16), ("eps", 1), ("upper", 128), ("lower", 128), ("causal", 128), ("zero", 128)]:
    CN[_name] = slice(_at, _at + _n)
    _at += _n
CN_N = _at
ARENA = 28928
WINDOWS = T // P
PAIRS = NE // 2
NONE = 4096
IN2_ORDER = [6, 7, 8, 9, 10, 11, 0, 1, 2, 3, 4, 5, 12, 13]
N_GDN = 6
LEVELS = 7

fp32 = mybir.dt.float32
bf16 = mybir.dt.bfloat16
u32 = mybir.dt.uint32
ALU = mybir.AluOpType
ACT = mybir.ActivationFunctionType
AX = mybir.AxisListType.X


class Carve:

    def __init__(self, tensor, at=0):
        self.tensor, self.at = tensor, at

    def take(self, *dims, dt=fp32):
        n = int(np.prod(dims))
        ap = self.tensor[:, self.at:self.at + n]
        self.at += n
        if dt is not fp32:
            ap = ap.bitcast(dt)
        if len(dims) > 1:
            names = "abcd"[:len(dims)]
            ap = ap.rearrange(f"p ({' '.join(names)}) -> p {' '.join(names)}",
                              **dict(zip(names, dims)))
        return ap


def bc(ap, axis, n):
    shape = list(ap.shape)
    shape.insert(axis, n)
    return ap.unsqueeze(axis).to_broadcast(shape)


def last_chunk_in(slot, before):
    return max(n for n in range(before) if n % WSLOTS == slot)


def two_blocks(nc, xT_d, ctxT_d, small_d, rows_d, const_d, masks_d, wstream_d, gate2_d, uv_d, route_d,
               moe_d, final_g_d, out_d, h4_d, y4_d):
    ctx = ExitStack()
    with ctx:
        def sb(name, n, dt=fp32):
            return ctx.enter_context(nc.sbuf_tensor(name, [P, n], dt))

        def sem(name):
            return ctx.enter_context(nc.semaphore(name))

        wring = sb("wring", WSLOTS * CHUNK)
        arena = sb("arena", ARENA)
        xT = sb("xT", KD * T)[:, :].rearrange("p (k t) -> p k t", k=KD)
        small = sb("small", SM_N)
        mod_rows = sb("mod_rows", D)
        rows = sb("rows", RW_N)
        const = sb("const", CN_N)
        tiny = Carve(sb("tiny", 1024))
        bank = [ctx.enter_context(nc.psum_tensor(f"bank{i}", [P, 512], fp32)) for i in range(8)]

        ident, ones, epsc = const[:, CN["ident"]], const[:, CN["ones"]], const[:, CN["eps"]]

        def wchunk(n):
            s = n % WSLOTS
            return wring[:, s * CHUNK:(s + 1) * CHUNK].rearrange("p (k c) -> p k c", k=KD)

        condS = tiny.take(KD, 2)
        modv = tiny.take(6 * KD, 2)
        scale1 = tiny.take(2, KD)
        scale2 = tiny.take(KD)
        lg = tiny.take(8)
        lgL = tiny.take(8)
        nlg = tiny.take(8)
        lt = tiny.take(6, 8)
        lamt = tiny.take(2, 64)
        lam2 = tiny.take(4)
        ss = tiny.take(48)
        sr = tiny.take(48)
        zm = tiny.take(2, 2, 2)
        zz = tiny.take(2, 2)
        zr = tiny.take(2, 2)

        m1 = Carve(arena)
        proj = m1.take(NT, IN1)
        cproj = m1.take(NT, 1792)
        hT = m1.take(KD, T)
        chT = m1.take(KD, T)
        tmp = m1.take(2, 1024)
        rqT = m1.take(2, T)
        rkT = m1.take(2, 2 * T)
        dqT = m1.take(4, T)
        dkT = m1.take(4, 2 * T)
        SD = m1.take(2, 4, T)
        DC = m1.take(2, 4, T)
        prob = m1.take(2, 2 * T)
        aT = m1.take(2, 4, P)
        Y = m1.take(NT, D)
        probs = [prob, DC[:, 0].rearrange("p a t -> p (a t)").rearrange("p (c k) -> p c k", c=2)]
        mixT = chT
        assert m1.at <= ARENA
        sq = tmp.rearrange("p a b -> p (a b)").rearrange("p (k t) -> p k t", k=KD)
        csq = Y.rearrange("p a b -> p (a b)").rearrange("p (k t) -> p k t", k=KD)
        rstd = prob[:, 0, :].rearrange("p (a t) -> p a t", a=2)

        GS = 8
        m2 = Carve(arena)
        G = m2.take(GS, 2 * D)
        h2T = m2.take(KD, T)
        h2 = m2.take(NT, D)
        qT = m2.take(2, 2, T)
        keyS0 = m2.take(2, 2, NK)
        keyS1 = m2.take(PH, 2, NK)
        diag = m2.take(GS, P)
        junk = m2.take(D)
        rstd2 = m2.take(T)
        cand = m2.take(TOPK * TOPK)
        hot = m2.take(TOPK, TOPK)
        topv = m2.take(2, TOPK)
        topi = m2.take(2, TOPK, dt=u32)
        topf = m2.take(2, TOPK)
        pos = m2.take(TOPK, dt=u32)
        posu = m2.take(2, TOPK, dt=u32)
        posf = m2.take(2, TOPK)
        chosen = m2.take(2, TOPK)
        expert = m2.take(NT * SLOTS, dt=u32)
        gates = m2.take(NT * SLOTS)
        gsum = m2.take(1)
        stage = m2.take(GS, dt=u32)
        dots = m2.take(2, 4)
        gelu = m2.take(2, 4)
        weight = m2.take(2, 4)
        assert m2.at <= ARENA
        sq2 = Carve(arena).take(KD, T)
        ffn = mod_rows
        zero = const[:, CN["zero"]]
        UNITS = NT * PH

        m3 = Carve(arena)
        N_ROUTE = KD * (NG + NE)
        routeW = Carve(arena, ARENA - N_ROUTE).take(KD, NG + NE)
        h3T = m3.take(KD, T)
        sq3 = m3.take(KD, T)
        cvin = m3.take(12, CONV - 1 + T)
        rstd3 = m3.take(T)
        assert m3.at <= 8192
        late = Carve(arena)
        late.take(KD, T)
        gA, gAT, gT_, gTT, gM, gMT = (late.take(8, P) for _ in range(6))
        m3 = Carve(arena, late.at)
        gD = m3.take(8, P)
        gDT = m3.take(8, P)
        mqT = m3.take(4, T)
        mkT = m3.take(4, T)
        mv = m3.take(NT, 512)
        gz = m3.take(NT, 512)
        cvT = m3.take(12, T)
        masks = m3.take(2, LEVELS, P)
        gate2 = m3.take(KD, 8)
        kTM = m3.take(8, P)
        vTM = m3.take(8, P)
        gW = m3.take(8, P)
        gR = m3.take(8, P)
        gU = m3.take(8, P)
        gS = m3.take(4, P)
        gwT = m3.take(4, P)
        Y2 = m3.take(NT, D)
        ab = m3.take(2, NT, 4)
        spt = m3.take(5, 8)
        g8 = m3.take(8)
        beta = m3.take(8)
        bg = m3.take(8)
        kd = m3.take(8)
        gc = m3.take(8)
        egc = m3.take(8)
        rz = m3.take(NT, MH)
        mx = m3.take(2, 2, 2)
        qk_norm = m3.take(NT * 8)
        ms2 = m3.take(8)
        assert m3.at <= ARENA - N_ROUTE
        nsq = Carve(arena, KD * T).take(8, T)
        over_h3 = Carve(arena)
        soft = over_h3.take(2, 3 * P)
        softT = over_h3.take(2, 3 * P)
        mix2T = cvT[:, 0:KD, :]

        m4 = Carve(arena)
        h4T = m4.take(KD, T)
        sq4 = m4.take(KD, T)
        rstd4 = m4.take(T)
        h4 = m4.take(NT, D)
        x3 = m4.take(NT, D)
        X = m4.take(2, D)
        XT = m4.take(2, KD, P)
        hid = m4.take(2, FF)
        hidT = m4.take(2, 2, P)
        sg = m4.take(2, FF)
        Yx = m4.take(2, D)
        hot4 = m4.take(NT + 1, NE * P // 2).bitcast(bf16)\
                 .rearrange("p a (e s) -> p a e s", e=NE)
        final_g = m4.take(D)
        slot_no = m4.take(WINDOWS, P // 2).bitcast(bf16)
        token_no = m4.take(NT)
        rank_in = m4.take(NT, NE)
        rank = m4.take(NT, NE // 2).bitcast(bf16)
        tags = m4.take(NT, NE)
        tags = tags.bitcast(bf16).rearrange("p t (e a) -> p t e a", a=2)
        slotv = m4.take(WINDOWS * NE, 2)
        absent = m4.take(WINDOWS * NE)
        from_row = m4.take(WINDOWS * NE + 2, dt=u32)
        to_row = m4.take(WINDOWS * NE + 2, dt=u32)
        stage4 = m4.take(4, dt=u32)
        most = m4.take(2)
        pairs = m4.take(1, dt=u32)
        ms4 = m4.take(NT)
        logit = m4.take(NT, NG + NE)
        pad8 = m4.take(NT, 8)
        gm8 = m4.take(NT, 8)
        gi8 = m4.take(NT, 8, dt=u32)
        gif = m4.take(NT, 8)
        ghot = m4.take(NT, NG)
        gex = m4.take(NT, NG)
        gsel = m4.take(NT, 8, NG)
        ing = m4.take(NT, 8)
        im8 = m4.take(NT, 8)
        ii8 = m4.take(NT, 8, dt=u32)
        iif = m4.take(NT, 8)
        pw = m4.take(NT, 4)
        within = m4.take(2, NT, 8)
        assert m4.at <= ARENA - N_ROUTE
        back = Carve(arena).take(NT, 2, D)

        chunk_here = [sem(f"chunk_here{i}") for i in range(WSLOTS)]
        chunk_used = sem("chunk_used")
        x_here = sem("x_here")
        small_here = sem("small_here")
        const_here = sem("const_here")
        act_step = sem("act_step")
        dve_step = sem("dve_step")
        mod_out = sem("mod_out")
        mod_turned = sem("mod_turned")
        inputs_ready = sem("inputs_ready")
        sums1 = sem("sums1")
        root1 = sem("root1")
        h_ready = sem("h_ready")
        proj_x_out = sem("proj_x_out")
        proj_c_out = sem("proj_c_out")
        qk_sq = sem("qk_sq")
        qk_root = sem("qk_root")
        roped = sem("roped")
        turned = sem("turned")
        turned_out = sem("turned_out")
        gam_e = sem("gam_e")
        gam_ready = sem("gam_ready")
        decay_args = sem("decay_args")
        decay_ready = sem("decay_ready")
        ret_scores = sem("ret_scores")
        ret_masked = sem("ret_masked")
        ret_y = sem("ret_y")
        ret_y_out = sem("ret_y_out")
        lam_dots = sem("lam_dots")
        lam_exp = sem("lam_exp")
        diff_scores = sem("diff_scores")
        diff_max = sem("diff_max")
        diff_exp = sem("diff_exp")
        diff_a = sem("diff_a")
        diff_aT = sem("diff_aT")
        diff_aT_out = sem("diff_aT_out")
        diff_y = sem("diff_y")
        y_ms = sem("y_ms")
        y_root = sem("y_root")
        mix_ready = sem("mix_ready")
        mixT_done = sem("mixT_done")
        mixT_out = sem("mixT_out")

        rms_sq = sem("rms_sq")
        rms_sum = sem("rms_sum")
        rms_root = sem("rms_root")
        h2_ready = sem("h2_ready")
        q_done = sem("q_done")
        q_out = sem("q_out")
        keys_done = sem("keys_done")
        keys_out = sem("keys_out")
        tokens_turned = sem("tokens_turned")
        tokens_out = sem("tokens_out")
        top_exp = sem("top_exp")
        top_expd = sem("top_expd")
        top_ready = sem("top_ready")
        idx_staged = sem("idx_staged")
        dot_done = sem("dot_done")
        gelu_step = sem("gelu_step")
        diag_ready = sem("diag_ready")
        slot_used = sem("slot_used")
        ffn_out = sem("ffn_out")
        ffnT_done = sem("ffnT_done")
        x2_ready = sem("x2_ready")
        h3_ready = sem("h3_ready")
        masks_here = sem("masks_here")
        in2_out = sem("in2_out")
        ab_done = sem("ab_done")
        ab_exp = sem("ab_exp")
        ab_expd = sem("ab_expd")
        conv_ready = sem("conv_ready")
        conv_silu = sem("conv_silu")
        lnorm_sq = sem("lnorm_sq")
        lnorm_sum = sem("lnorm_sum")
        lnorm_root = sem("lnorm_root")
        lnorm_done = sem("lnorm_done")
        tm_done = sem("tm_done")
        tm_out = sem("tm_out")
        g_ready = sem("g_ready")
        g_done = sem("g_done")
        gx_ready = sem("gx_ready")
        g_copied = sem("g_copied")
        gx_exp = sem("gx_exp")
        kk_done = sem("kk_done")
        a_ready = sem("a_ready")
        at_done = sem("at_done")
        at_out = sem("at_out")
        t_in = sem("t_in")
        mask_ready = sem("mask_ready")
        w_done = sem("w_done")
        w_out = sem("w_out")
        t_done = sem("t_done")
        prepared = sem("prepared")
        uv_done = sem("uv_done")
        uv_out = sem("uv_out")
        s_done = sem("s_done")
        s_out = sem("s_out")
        pt_done = sem("pt_done")
        pt_ready = sem("pt_ready")
        u1_done = sem("u1_done")
        norms_spread = sem("norms_spread")
        moba_s = sem("moba_s")
        moba_m = sem("moba_m")
        moba_e = sem("moba_e")
        moba_T = sem("moba_T")
        moba_T_out = sem("moba_T_out")
        moba_y = sem("moba_y")
        x3_ready = sem("x3_ready")
        h4_ready = sem("h4_ready")
        final_g_here = sem("final_g_here")
        route_done = sem("route_done")
        route_exp = sem("route_exp")
        route_expd = sem("route_expd")
        numbers_ready = sem("numbers_ready")
        chosen_ready = sem("chosen_ready")
        rank_ready = sem("rank_ready")
        hot_ready = sem("hot_ready")
        slots_ready = sem("slots_ready")
        rows_saved = sem("rows_saved")
        x_turned = sem("x_turned")
        xt_left = sem("xt_left")
        xt_right = sem("xt_right")
        hid_turned = sem("hid_turned")
        hidT_ready = sem("hidT_ready")
        y_left = sem("y_left")
        from_staged = sem("from_staged")
        to_staged = sem("to_staged")
        y_right = sem("y_right")
        scattered = [sem(f"scattered{b}") for b in range(2)]
        y_back = sem("y_back")
        y_back1 = sem("y_back1")
        x4_ready = sem("x4_ready")
        gu_done = sem("gu_done")
        silu_ready = sem("silu_ready")
        hid_ready = sem("hid_ready")
        down_used = sem("down_used")
        out_ready = sem("out_ready")
        out_gone = sem("out_gone")
        gathered = [sem(f"gathered{j}") for j in range(GS)]
        gu_here = [sem(f"gu_here{b}") for b in range(2)]
        down_here = [sem(f"down_here{b}") for b in range(2)]

        GATHERED = 16 * NT * SLOTS // GS

        block = ctx.enter_context(nc.Block())

        def chunk_ready(eng, n):
            eng.wait_ge(chunk_here[n % WSLOTS], 16 * (n // WSLOTS + 1))

        def chunk_done(eng, n):
            eng.wait_ge(chunk_used, n + 1)

        def project_fm(pe, c0, count, act_T, at=0):
            for n in range(count):
                chunk_ready(pe, c0 + n)
                w = wchunk(c0 + n)
                for j in range(2):
                    for k in range(KD):
                        ins = nc.tensor.matmul(bank[1 + (at + n) % 4][:, j * T:(j + 1) * T],
                                               w[:, k, j * P:(j + 1) * P], act_T[:, k, :],
                                               start=k == 0, stop=k == KD - 1)
                ins.then_inc(chunk_used, 1)

        def sums_over_features(pe, squares, nth):
            pe.wait_ge(rms_sq, nth)
            for k in range(KD):
                ins = nc.tensor.matmul(bank[7][:, 0:T], ones, squares[:, k, :], start=k == 0, stop=k == KD - 1)
            ins.then_inc(rms_sum, 1)

        MOD_BANK = (0, 7, 0, 7, 0, 0)

        def mod_products(pe, g, banks, chunks=range(MOD_GROUP)):
            for n in chunks:
                chunk_ready(pe, C_MOD[g] + n)
                w = wchunk(C_MOD[g] + n)
                for k in range(KD):
                    ins = nc.tensor.matmul(bank[banks[n // 2]][0:2, (n % 2) * COLS:(n % 2 + 1) * COLS],
                                           condS[:, k, :], w[:, k, :], start=k == 0, stop=k == KD - 1)
                ins.then_inc(chunk_used, 1)

        def mod_turn(pe, g):
            pe.wait_ge(mod_out, 2 * g + 2)
            for k in range(KD):
                ins = nc.tensor.transpose(bank[MOD_BANK[g]][:, 2 * k:2 * k + 2],
                                          mod_rows[0:2, k * P:(k + 1) * P], ident[0:2, 0:2])
            ins.then_inc(mod_turned, 1)

        def transposes(pe, out, blocks):
            for i, b in enumerate(blocks):
                ins = nc.tensor.transpose(out[:, i * P:(i + 1) * P], b, ident)
            return ins

        @block.sync
        def _(sp):
            for n in range(WSLOTS):
                sp.dma_start(wring[:, n * CHUNK:(n + 1) * CHUNK], wstream_d[n]).then_inc(chunk_here[n], 16)
            behind = C_IN2 + 2
            full = behind // WSLOTS
            with sp.Fori(1, full) as turn:
                for s in range(WSLOTS):
                    sp.wait_ge(chunk_used, turn * WSLOTS + (s + 1 - WSLOTS))
                    sp.dma_start(wring[:, s * CHUNK:(s + 1) * CHUNK],
                                 wstream_d[bass.ds(turn * WSLOTS + s, 1)].rearrange("a p c -> (a p) c"))\
                      .then_inc(chunk_here[s], 16)
            for n in range(full * WSLOTS, N_CHUNKS):
                if n == behind:
                    sp.wait_ge(slot_used, NT * SLOTS)
                    sp.dma_start(gate2.rearrange("p k c -> p (k c)"), gate2_d).then_inc(masks_here, 16)
                    sp.dma_start(masks.rearrange("p w s n -> p (w s n)"), masks_d).then_inc(masks_here, 16)
                    sp.dma_start(routeW.rearrange("p k e -> p (k e)"), route_d).then_inc(masks_here, 16)
                sp.wait_ge(chunk_used, n + 1 - WSLOTS)
                s = n % WSLOTS
                sp.dma_start(wring[:, s * CHUNK:(s + 1) * CHUNK], wstream_d[n]).then_inc(chunk_here[s], 16)

            def gu_buf(b):
                return wring[:, 2 * b * CHUNK:(2 * b + 2) * CHUNK]

            def down_buf(b):
                return wring[:, (4 + b) * CHUNK:(5 + b) * CHUNK]

            for b in range(2):
                sp.wait_ge(chunk_used, last_chunk_in(2 * b, N_CHUNKS) + 1)
                sp.wait_ge(chunk_used, last_chunk_in(2 * b + 1, N_CHUNKS) + 1)
                sp.dma_start(gu_buf(b), moe_d[b, :, 0:2 * CHUNK]).then_inc(gu_here[b], 16)
                sp.wait_ge(chunk_used, last_chunk_in(4 + b, N_CHUNKS) + 1)
                sp.dma_start(down_buf(b), moe_d[b, :, 2 * CHUNK:3 * CHUNK]).then_inc(down_here[b], 16)
            sp.wait_ge(slots_ready, 1)
            n_pairs = sp.value_load(pairs[0:1, 0:1], min_val=PAIRS, max_val=WINDOWS * PAIRS)
            with sp.Fori(1, n_pairs) as i:
                for b in range(2):
                    src = moe_d[bass.ds((2 * i + b) % NE, 1)].rearrange("a p c -> (a p) c")
                    sp.wait_ge(gu_done, 2 * i + (b - 1))
                    sp.dma_start(gu_buf(b), src[:, 0:2 * CHUNK]).then_inc(gu_here[b], 16)
                    sp.wait_ge(down_used, 2 * i + (b - 1))
                    sp.dma_start(down_buf(b), src[:, 2 * CHUNK:3 * CHUNK]).then_inc(down_here[b], 16)
            for b in range(2):
                sp.wait_ge(scattered[b], n_pairs * 16 + 16)
            for t in range(NT):
                sp.dma_start(back[:, t].rearrange("p r d -> p (r d)"), y4_d[t * P * 2:(t + 1) * P * 2]
                             .rearrange("(p r) d -> p (r d)", r=2)).then_inc((y_back, y_back1)[t], 16)
            for t in range(NT):
                sp.wait_ge(out_ready, t + 1)
                sp.dma_start(out_d[t * P:(t + 1) * P], x3[:, t]).then_inc(out_gone, 16)
            sp.wait_ge(out_gone, 16 * NT)

        @block.gpsimd
        def _(pool):
            def gather(j, column):
                src = bass.IndirectOffsetOnAxis(ap=column, axis=0)
                pool.indirect_dma_start(G[:, j, :], None, uv_d, src).then_inc(gathered[j], 16)

            def gather_turn(unit, half):
                for j in range(GS):
                    n = unit * TOPK + (half * GS + j)
                    pool.wait_ge(slot_used, n + (1 - GS))
                    nc.gpsimd.tensor_copy(stage[:, j:j + 1], expert[:, bass.ds(n, 1)]).then_inc(idx_staged, 1)
                    pool.wait_ge(top_ready, 1)
                    pool.wait_ge(idx_staged, n + (1 - GS))
                    gather(j, stage[:, j:j + 1])

            pool.wait_ge(top_ready, 1)
            for j in range(GS):
                gather(j, expert[:, j:j + 1])
            gather_turn(0, 1)
            with pool.Fori(1, UNITS) as unit:
                pool.wait_ge(top_ready, unit + 1)
                for half in range(2):
                    gather_turn(unit, half)

            def mask_level(lv):
                if lv >= 3:
                    pool.wait_ge(w_done, 2 * (lv - 2))
                nc.gpsimd.tensor_tensor((gMT, gM)[lv % 2], gAT, bc(masks[:, 1, lv, :], 1, 8), ALU.mult)\
                  .then_inc(mask_ready, 1)

            pool.wait_ge(masks_here, 48)
            pool.wait_ge(at_out, 1)
            mask_level(1)
            pool.wait_ge(tm_out, 4)
            pool.wait_ge(lnorm_done, 2)
            pool.wait_ge(a_ready, 1)
            pool.wait_ge(gx_ready, 3)
            nc.gpsimd.tensor_tensor(vTM, vTM, bc(beta, 2, P), ALU.mult).then_inc(prepared, 1)
            mask_level(2)
            nc.gpsimd.tensor_tensor(gD[:, 4:8, :], kTM[:, 4:8, :], bc(bg[:, 4:8], 2, P), ALU.mult)\
              .then_inc(prepared, 1)
            nc.gpsimd.tensor_tensor(gD[:, 0:4, :], kTM[:, 0:4, :], bc(kd[:, 0:4], 2, P), ALU.mult)\
              .then_inc(prepared, 1)
            mask_level(3)
            nc.gpsimd.tensor_tensor(gR[:, 4:8, :], cvT[:, 0:4, P:2 * P], gR[:, 4:8, :], ALU.mult)\
              .then_inc(prepared, 1)
            for lv in range(4, LEVELS):
                mask_level(lv)

            pool.wait_ge(x3_ready, 1)
            nc.gpsimd.iota(slot_no, [[P, WINDOWS], [1, P]], base=1, channel_multiplier=0,
                           allow_small_or_imprecise_dtypes=True)
            nc.gpsimd.iota(token_no, [[P, NT]], base=1, channel_multiplier=1,
                           allow_small_or_imprecise_dtypes=True).then_inc(numbers_ready, 1)
            nc.gpsimd.memset(X, 0.0)
            nc.gpsimd.memset(Yx, 0.0).then_inc(to_staged, 2)
            pool.wait_ge(to_staged, 2)
            pool.wait_ge(rows_saved, 16 * NT)
            pool.wait_ge(slots_ready, 1)
            n_pairs = pool.value_load(pairs[0:1, 0:1], min_val=PAIRS, max_val=WINDOWS * PAIRS)

            last_from, last_to = pool.to_reg(T - 1), pool.to_reg(2 * T - 1)

            def gather4(b, column):
                src = bass.IndirectOffsetOnAxis(ap=column, axis=0)
                pool.indirect_dma_start(X[:, b], None, h4_d, src, bounds_check=last_from, oob_is_err=False)\
                    .then_inc(gathered[b], 16)

            def scatter4(b, column):
                dst = bass.IndirectOffsetOnAxis(ap=column, axis=0)
                pool.indirect_dma_start(y4_d, dst, Yx[:, b], None, bounds_check=last_to, oob_is_err=False)\
                    .then_inc(scattered[b], 16)

            for b in range(2):
                gather4(b, from_row[:, b:b + 1])
            for b in range(2):
                scatter4(b, to_row[:, WINDOWS * NE + b:WINDOWS * NE + b + 1])
            pool.wait_ge(slots_ready, WINDOWS)
            with pool.Fori(0, n_pairs) as i:
                for b in range(2):
                    pool.wait_ge(x_turned, 2 * i + (b + 1))
                    nc.gpsimd.tensor_copy(stage4[:, b:b + 1], from_row[:, bass.ds(2 * i + (b + 2), 1)])\
                      .then_inc(from_staged, 1)
                    pool.wait_ge(slots_ready, WINDOWS)
                    pool.wait_ge(from_staged, 2 * i + (b + 1))
                    gather4(b, stage4[:, b:b + 1])
                for b in range(2):
                    pool.wait_ge(y_left, 2 * i + (b + 3))
                    pool.wait_ge(y_right, 2 * i + (b + 3))
                    pool.wait_ge(scattered[b], 16 * i + 16)
                    nc.gpsimd.tensor_copy(stage4[:, 2 + b:3 + b], to_row[:, bass.ds(2 * i + b, 1)])\
                      .then_inc(to_staged, 1)
                    pool.wait_ge(slots_ready, WINDOWS)
                    pool.wait_ge(to_staged, 2 * i + (b + 3))
                    scatter4(b, stage4[:, 2 + b:3 + b])
            for b in range(2):
                pool.wait_ge(gathered[b], n_pairs * 16 + (GATHERED + 16))

        @block.scalar
        def _(act):
            steps = [0]

            def own(ins):
                steps[0] += 1
                ins.then_inc(act_step, 1)
                act.wait_ge(act_step, steps[0])

            act.dma_start(small[:, :], small_d).then_inc(small_here, 16)
            act.dma_start(xT, xT_d).then_inc(x_here, 16)
            act.dma_start(chT, ctxT_d).then_inc(x_here, 16)
            act.dma_start(const[:, :], const_d).then_inc(const_here, 16)
            act.dma_start(rows[:, :], rows_d).then_inc(const_here, 16)
            act.wait_ge(small_here, 16)
            nc.scalar.activation(condS.rearrange("p k c -> p (k c)"), small[:, SM["cond"]], ACT.Silu)\
              .then_inc(inputs_ready, 1)
            act.wait_ge(x_here, 32)
            act.wait_ge(const_here, 32)
            nc.scalar.activation(sq, xT, ACT.Square).then_inc(inputs_ready, 1)
            nc.scalar.activation(csq, chT, ACT.Square).then_inc(inputs_ready, 1)
            act.wait_ge(sums1, 1)
            nc.scalar.activation(rstd.rearrange("p a t -> p (a t)"), bank[7][:, :], ACT.Sqrt,
                                 bias=epsc, scale=1.0 / D).then_inc(root1, 1)

            def modulation_out(g, banks, halves=(0, 1)):
                if g >= 1:
                    act.wait_ge(mod_turned, g)
                for i in halves:
                    b = banks[i]
                    chunk_done(act, C_MOD[g] + 2 * i + 1)
                    nc.scalar.activation(mod_rows[0:2, i * 512:(i + 1) * 512], bank[b][0:2, :], ACT.Copy)\
                      .then_inc(mod_out, 1)

            modulation_out(0, (1, 2))
            modulation_out(1, (3, 4))
            at = 0
            for n in range(N_IN1):
                if n == N_IN1 - 1:
                    act.wait_ge(qk_sq, 1)
                    nc.scalar.activation(sr, ss, ACT.Sqrt, bias=epsc, scale=1.0 / DD).then_inc(qk_root, 1)
                    act.wait_ge(gam_e, 1)
                    nc.scalar.activation(lt[:, 1, :], lt[:, 0, :], ACT.Exp).then_inc(gam_e, 1)
                    act.wait_ge(lam_dots, 1)
                    nc.scalar.activation(lam2[:, 0:2], lam2[:, 0:2], ACT.Exp).then_inc(lam_exp, 1)
                chunk_done(act, C_IN1 + n)
                func = ACT.Silu if n in (4, 5) else ACT.Copy
                nc.scalar.activation(proj[:, :, n * COLS:(n + 1) * COLS],
                                     bank[1 + 2 * (n % 2)][:, :].rearrange("p (t c) -> p t c", t=NT),
                                     func).then_inc(proj_x_out, 1)
                if n in CTX_CHUNKS:
                    nc.scalar.activation(cproj[:, :, at:at + COLS],
                                         bank[2 + 2 * (n % 2)][:, :].rearrange("p (t c) -> p t c", t=NT),
                                         ACT.Copy).then_inc(proj_c_out, 1)
                    at += COLS
            modulation_out(2, (5, 6))
            modulation_out(3, (1, 2))
            act.wait_ge(gam_ready, 1)
            for h in range(RH):
                act.wait_ge(decay_args, h + 1)
                d = DC[:, h % 2]
                dist = const[:, CN["dist"]].rearrange("p (k t) -> p k t", k=NT)
                if h >= 2:
                    act.wait_ge(ret_masked, h - 1)
                nc.scalar.activation(d[:, 0:2, :], dist, ACT.Exp, bias=lgL[:, h:h + 1],
                                     scale=lg[:, h:h + 1])
                nc.scalar.activation(tmp[:, h % 2, 0:512].rearrange("p (k t) -> p k t", k=NT), dist,
                                     ACT.Exp, bias=lgL[:, 4 + h:5 + h], scale=nlg[:, 4 + h:5 + h])
                nc.scalar.activation(d[:, 2:4, :].rearrange("p k t -> p (k t)"),
                                     tmp[:, h % 2, 512:1024], ACT.Exp).then_inc(decay_ready, 1)
            def diff_exps(i):
                for c in range(2):
                    act.wait_ge(diff_max, 2 * i + c + 1)
                    if i == 1:
                        act.wait_ge(ret_masked, RH)
                    if i >= 2:
                        act.wait_ge(diff_a, i - 1)
                    nc.scalar.activation(probs[i % 2][:, c, :], bank[1 + 2 * (i % 2) + c][:, :], ACT.Exp,
                                         bias=zm[:, i % 2, 1, c:c + 1], scale=DD ** -0.5,
                                         accum_out=zz[:, i % 2, c:c + 1]).then_inc(diff_exp, 1)

            diff_exps(0)
            diff_exps(1)
            for i in range(DH * NT):
                act.wait_ge(diff_aT, i + 1)
                if i >= 2:
                    act.wait_ge(diff_y, i - 1)
                nc.scalar.activation(aT[:, i % 2].rearrange("p k t -> p (k t)"), bank[5 + i % 2][:, :],
                                     ACT.Copy).then_inc(diff_aT_out, 1)
                if i == 0:
                    modulation_out(4, (6, 1), (0,))
                if i + 2 < DH * NT:
                    diff_exps(i + 2)
            act.wait_ge(y_ms, 1)
            nc.scalar.activation(sr[:, 0:16], ss[:, 0:16], ACT.Sqrt, bias=epsc, scale=1.0 / RV)\
              .then_inc(y_root, 1)
            modulation_out(4, (6, 1), (1,))
            for g in range(4):
                act.wait_ge(mixT_done, g + 1)
                nc.scalar.activation(mixT[:, 2 * g:2 * g + 2, :].rearrange("p k t -> p (k t)"),
                                     bank[5 + g % 2][:, :], ACT.Copy).then_inc(mixT_out, 1)

            chunk_done(act, C_OUT1 + N_OUT - 1)
            act.wait_ge(x2_ready, 1)
            nc.scalar.activation(sq2, xT, ACT.Square).then_inc(rms_sq, 1)
            act.wait_ge(rms_sum, 1)
            nc.scalar.activation(rstd2, bank[7][:, 0:T], ACT.Sqrt, bias=epsc, scale=1.0 / D)\
              .then_inc(rms_root, 1)

            def queries_out(h):
                if h == 0:
                    chunk_done(act, C_Q)
                else:
                    act.wait_ge(q_done, h)
                nc.scalar.activation(qT[:, h % 2].rearrange("p k t -> p (k t)"), bank[5][:, :], ACT.Copy)\
                  .then_inc(q_out, 1)

            def scores_out(h):
                if h >= 2:
                    act.wait_ge(top_ready, h - 1)
                if h == PH - 1:
                    chunk_done(act, C_Q + N_Q)
                else:
                    act.wait_ge(keys_done, h + 1)
                for keyS, at in ((keyS0[:, h % 2], 0), (keyS1[:, h], 2 * NK)):
                    ins = nc.scalar.activation(keyS.rearrange("p h n -> p (h n)"),
                                               bank[6][:, at:at + 2 * NK], ACT.Copy)
                ins.then_inc(keys_out, 1)

            def gate_exp(unit):
                act.wait_ge(top_exp, unit + 1)
                g = gates[:, unit * TOPK:(unit + 1) * TOPK]
                nc.scalar.activation(g, g, ACT.Exp).then_inc(top_expd, 1)

            queries_out(0)
            scores_out(0)
            for g in range(4):
                act.wait_ge(tokens_turned, g + 1)
                nc.scalar.activation(h2[:, g // 2, (g % 2) * 512:(g % 2 + 1) * 512],
                                     bank[(7, 0)[g % 2]][:, :], ACT.Copy).then_inc(tokens_out, 1)
            queries_out(1)
            scores_out(1)
            gate_exp(0)
            queries_out(2)
            scores_out(2)
            gate_exp(1)
            n_step = 5

            def weights(unit, half):
                for g in range(2):
                    first = unit * TOPK + half * GS + 4 * g
                    act.wait_ge(dot_done, first + 5)
                    nc.scalar.activation(gelu[:, g, :], dots[:, g, :], ACT.Gelu).then_inc(gelu_step, 1)
                    done = n_step * (first // 4)
                    act.wait_ge(gelu_step, done + 1)
                    for q in range(4):
                        nc.scalar.activation(weight[:, g, q:q + 1], gelu[:, g, q:q + 1], ACT.Copy,
                                             scale=gates[:, first + q:first + q + 1]).then_inc(gelu_step, 1)
                    for q in range(4):
                        act.wait_ge(gelu_step, done + (q + 2))
                        nc.scalar.activation(diag[:, 4 * g + q, :], ident, ACT.Copy,
                                             scale=weight[:, g, q:q + 1]).then_inc(diag_ready, 1)

            for unit in range(UNITS):
                weights(unit, 0)
                if unit + 3 < PH:
                    queries_out(unit + 3)
                if unit == PH - 1:
                    modulation_out(5, (5, 6))
                weights(unit, 1)
                if unit + 3 < PH:
                    scores_out(unit + 3)
                if unit % PH == PH - 1:
                    t = unit // PH
                    act.wait_ge(slot_used, (t + 1) * SLOTS)
                    act.wait_ge(mod_turned, 6)
                    if t == 1:
                        act.wait_ge(ffnT_done, 2)
                    for c in range(2):
                        ins = nc.scalar.activation(ffn[:, c * 512:(c + 1) * 512], bank[1 + 2 * t + c][:, :], ACT.Copy)
                    ins.then_inc(ffn_out, 1)
                if unit + 2 < UNITS:
                    gate_exp(unit + 2)
            act.wait_ge(x2_ready, 2)
            nc.scalar.activation(sq3, xT, ACT.Square).then_inc(rms_sq, 1)
            act.wait_ge(rms_sum, 2)
            nc.scalar.activation(rstd3, bank[7][:, 0:T], ACT.Sqrt, bias=epsc, scale=1.0 / D)\
              .then_inc(rms_root, 1)
            in2_at = [0]

            def in2_evac():
                i = in2_at[0]
                in2_at[0] += 1
                n = IN2_ORDER[i]
                chunk_done(act, C_IN2 + i)
                two = bank[(0, 7)[i % 2]][:, :].rearrange("p (k t) -> p k t", k=2)
                if n < 4:
                    dst = (mqT, mkT)[n // 2][:, 2 * (n % 2):2 * (n % 2) + 2, :]
                elif n < 6:
                    dst = mv[:, :, (n - 4) * COLS:(n - 3) * COLS]
                elif n < 12:
                    dst = cvin[:, 2 * (n - 6):2 * (n - 6) + 2, CONV - 1:]
                else:
                    dst = gz[:, :, (n - 12) * COLS:(n - 11) * COLS]
                nc.scalar.activation(dst, two, ACT.Silu if n >= 12 else ACT.Copy).then_inc(in2_out, 1)

            def conv_out(i):
                act.wait_ge(conv_ready, i + 1)
                c = cvT[:, 2 * i:2 * i + 2, :]
                nc.scalar.activation(c, c, ACT.Silu).then_inc(conv_silu, 1)
                if i < 4:
                    act.wait_ge(conv_silu, i + 1)
                    nc.scalar.activation(nsq[:, 2 * i:2 * i + 2, :], c, ACT.Square).then_inc(lnorm_sq, 1)

            in2_evac()
            act.wait_ge(ab_exp, 1)
            nc.scalar.activation(spt[:, 1, :], spt[:, 0, :], ACT.Exp)
            nc.scalar.activation(beta, beta, ACT.Exp, scale=-1.0)
            nc.scalar.activation(kd[:, 0:4], rows[:, RW["A_log"]], ACT.Exp).then_inc(ab_expd, 1)
            in2_evac()
            conv_out(0)
            act.wait_ge(g_done, 1)
            nc.scalar.activation(gc, bank[2][:, 0:8], ACT.Copy)
            for i in range(2):
                ins = nc.scalar.activation(gR[:, 4 * i:4 * i + 4, :].rearrange("p a b -> p (a b)"),
                                           bank[5 + i][:, :], ACT.Copy)
            ins.then_inc(g_copied, 1)
            in2_evac()
            conv_out(1)
            in2_evac()
            act.wait_ge(gx_ready, 1)
            nc.scalar.activation(gD, gD, ACT.Exp)
            nc.scalar.activation(gDT, gDT, ACT.Exp)
            nc.scalar.activation(egc, gc, ACT.Exp)
            nc.scalar.activation(kd, kd, ACT.Exp)
            nc.scalar.activation(gR, gR, ACT.Exp).then_inc(gx_exp, 1)
            conv_out(2)
            in2_evac()
            conv_out(3)
            in2_evac()
            act.wait_ge(lnorm_sum, 1)
            nc.scalar.activation(qk_norm, bank[1][:, 0:NT * 8], ACT.Sqrt, bias=epsc).then_inc(lnorm_root, 1)
            conv_out(4)
            conv_out(5)
            in2_evac()
            for c in range(2):
                act.wait_ge(tm_done, c + 1)
                nc.scalar.activation(kTM[:, 4 * c:4 * c + 4, :].rearrange("p a b -> p (a b)"),
                                     bank[5 + c][:, :], ACT.Copy).then_inc(tm_out, 1)
            act.wait_ge(at_done, 1)
            for i in range(2):
                ins = nc.scalar.activation(gAT[:, 4 * i:4 * i + 4, :].rearrange("p a b -> p (a b)"),
                                           bank[5 + i][:, :], ACT.Copy)
            ins.then_inc(at_out, 1)
            in2_evac()
            for c in range(2):
                act.wait_ge(tm_done, 2 + c + 1)
                nc.scalar.activation(vTM[:, 4 * c:4 * c + 4, :].rearrange("p a b -> p (a b)"),
                                     bank[3 + c][:, :], ACT.Copy).then_inc(tm_out, 1)
            for s in range(1, LEVELS):
                for i in range(2):
                    act.wait_ge(w_done, 2 * (s - 1) + i + 1)
                    nc.scalar.activation(gW[:, 4 * i:4 * i + 4, :].rearrange("p a b -> p (a b)"),
                                         bank[1 + i][:, :], ACT.Copy).then_inc(w_out, 1)
                if s % 2 == 0:
                    in2_evac()
            act.wait_ge(uv_done, 1)
            nc.scalar.activation(gwT.rearrange("p a b -> p (a b)"), bank[3][:, :], ACT.Copy)
            for i in range(2):
                ins = nc.scalar.activation(gU[:, 4 * i:4 * i + 4, :].rearrange("p a b -> p (a b)"),
                                           bank[1 + i][:, :], ACT.Copy)
            ins.then_inc(uv_out, 1)
            act.wait_ge(s_done, 1)
            nc.scalar.activation(gS.rearrange("p a b -> p (a b)"), bank[4][:, :], ACT.Copy).then_inc(s_out, 1)
            while in2_at[0] < N_IN2:
                in2_evac()

            def moba_exp(h):
                if h >= 2:
                    act.wait_ge(moba_T, h - 1)
                b, m = bank[3 + h % 2], mx[:, h % 2, 1]
                act.wait_ge(moba_m, h + 1)
                nc.scalar.activation(soft[:, h % 2, 0:P], b[:, 0:P], ACT.Exp, bias=m[:, 0:1], scale=MD ** -0.5,
                                     accum_out=rz[:, 0, h:h + 1])
                nc.scalar.activation(soft[:, h % 2, P:3 * P], b[:, P:3 * P], ACT.Exp, bias=m[:, 1:2],
                                     scale=MD ** -0.5, accum_out=rz[:, 1, h:h + 1]).then_inc(moba_e, 1)

            moba_exp(0)
            moba_exp(1)
            for h in range(MH):
                if h >= 2:
                    act.wait_ge(moba_y, h - 1)
                act.wait_ge(moba_T, h + 1)
                nc.scalar.activation(softT[:, h % 2], bank[5 + h % 2][:, 0:3 * P], ACT.Copy)\
                  .then_inc(moba_T_out, 1)
                if h + 2 < MH:
                    moba_exp(h + 2)
            act.wait_ge(y_ms, 2)
            nc.scalar.activation(ms2, ms2, ACT.Sqrt, bias=epsc, scale=1.0 / GD).then_inc(y_root, 1)
            for g in range(4):
                act.wait_ge(mixT_done, 4 + g + 1)
                nc.scalar.activation(mix2T[:, 2 * g:2 * g + 2, :].rearrange("p k t -> p (k t)"),
                                     bank[5 + g % 2][:, :], ACT.Copy).then_inc(mixT_out, 1)
            act.wait_ge(x3_ready, 1)
            nc.scalar.activation(sq4, xT, ACT.Square).then_inc(rms_sq, 1)
            act.wait_ge(rms_sum, 3)
            nc.scalar.activation(rstd4, bank[7][:, 0:T], ACT.Sqrt, bias=epsc, scale=1.0 / D)\
              .then_inc(rms_root, 1)
            act.dma_start(final_g, final_g_d).then_inc(final_g_here, 16)
            for g in range(8):
                act.wait_ge(tokens_turned, 4 + g + 1)
                to = h4 if g < 4 else x3
                nc.scalar.activation(to[:, (g // 2) % 2, (g % 2) * 512:(g % 2 + 1) * 512],
                                     bank[g % 4][:, :], ACT.Copy).then_inc(tokens_out, 1)
                if g == 3:
                    for t in range(NT):
                        act.wait_ge(tokens_out, 4 + 2 * t + 2)
                        act.dma_start(h4_d[t * P:(t + 1) * P], h4[:, t]).then_inc(rows_saved, 16)
            act.wait_ge(route_exp, 1)
            nc.scalar.activation(gex, gex, ACT.Exp)
            nc.scalar.activation(pw[:, :, 1:2], pw[:, :, 0:1], ACT.Exp).then_inc(route_expd, 1)
            nc.scalar.activation(zr[:, 0], ones[:, 0:2], ACT.Copy).then_inc(y_left, 2)

            def turned_rows(b, wait_n):
                act.wait_ge(x_turned, wait_n)
                nc.scalar.activation(XT[:, b, 0:4].rearrange("p k t -> p (k t)"), bank[0][:, :],
                                     ACT.Copy).then_inc(xt_left, 1)

            for b in range(2):
                turned_rows(b, b + 1)
            act.wait_ge(slots_ready, 1)
            n_pairs = act.value_load(pairs[0:1, 0:1], min_val=PAIRS, max_val=WINDOWS * PAIRS)
            with act.Fori(0, n_pairs) as i:
                for b in range(2):
                    act.wait_ge(gu_done, 2 * i + (b + 1))
                    nc.scalar.activation(sg[:, b], bank[2 + b][:, 0:FF], ACT.Silu).then_inc(silu_ready, 1)
                for b in range(2):
                    turned_rows(b, 2 * i + (b + 3))
                    act.wait_ge(scattered[b], 16 * i + 16)
                    act.wait_ge(down_used, 2 * i + (b + 1))
                    nc.scalar.activation(Yx[:, b, 0:512], bank[4 + 2 * b][:, :], ACT.Copy).then_inc(y_left, 1)
            for t in range(NT):
                act.wait_ge(x4_ready, t + 1)
                nc.scalar.activation(h4[:, t], x3[:, t], ACT.Square, accum_out=ms4[:, t:t + 1])\
                  .then_inc(act_step, 1)
                steps[0] += 1
                act.wait_ge(act_step, steps[0])
                nc.scalar.activation(ms4[:, t:t + 1], ms4[:, t:t + 1], ACT.Sqrt, bias=epsc, scale=1.0 / D)\
                  .then_inc(rms_root, 1)

        @block.vector
        def _(dve):
            v = nc.vector
            steps = [0]

            def link(ins):
                steps[0] += 1
                ins.then_inc(dve_step, 1)
                dve.wait_ge(dve_step, steps[0])

            dve.wait_ge(const_here, 32)
            x = rows[:, RW["decay"]]
            link(v.tensor_scalar(lt[:, 2, :], x, -1.0, None, ALU.mult))
            link(v.tensor_tensor(lt[:, 0, :], x, lt[:, 2, :], ALU.min))
            v.memset(ss, 0.0).then_inc(gam_e, 1)
            lam = rows[:, RW["lam"]].rearrange("p (a c) -> p a c", a=4)
            link(v.tensor_tensor(lamt[:, 0, :], lam[:, 0, :], lam[:, 1, :], ALU.mult))
            link(v.tensor_tensor(lamt[:, 1, :], lam[:, 2, :], lam[:, 3, :], ALU.mult))
            v.tensor_reduce(lam2[:, 0:2], lamt, AX, ALU.add).then_inc(lam_dots, 1)

            dve.wait_ge(root1, 1)
            link(v.reciprocal(rstd, rstd))
            link(v.tensor_tensor(hT, xT, bc(rstd[:, 0, :], 1, KD), ALU.mult))
            link(v.tensor_tensor(chT, chT, bc(rstd[:, 1, :], 1, KD), ALU.mult))
            def modulation(g):
                dve.wait_ge(mod_turned, g + 1)
                m = slice(g * KD, (g + 1) * KD)
                link(v.tensor_tensor(modv[:, m], bank[MOD_BANK[g]][:, 0:2 * KD].rearrange("p (m c) -> p m c", c=2),
                                     bc(small[:, SM["b_mod"]][:, m], 2, 2), ALU.add))

            modulation(0)
            modulation(1)
            for c in range(2):
                link(v.scalar_tensor_tensor(scale1[:, c, :], modv[:, KD:2 * KD, c], 1.0,
                                            small[:, SM["g1"]], ALU.add, ALU.mult))
            for c, h in enumerate((hT, chT)):
                for k in range(KD):
                    v.tensor_scalar(h[:, k, :], h[:, k, :], scale1[:, c, k:k + 1],
                                    modv[:, k, c:c + 1], ALU.mult, ALU.add).then_inc(h_ready, 1)
            dve.wait_ge(proj_c_out, 5)
            dve.wait_ge(proj_x_out, 10)
            qk = [(proj[:, t, 1536:2560], 16, 16 * t) for t in range(NT)]
            qk += [(cproj[:, t, 768:1280], 8, 32 + 8 * t) for t in range(NT)]
            for ap, n, at in qk:
                flat = tmp[:, 0, 0:n * DD]
                link(v.tensor_tensor(flat, ap, ap, ALU.mult))
                ins = v.tensor_reduce(ss[:, at:at + n], flat.rearrange("p (h c) -> p h c", h=n), AX, ALU.add)
                if at == 40:
                    ins.then_inc(qk_sq, 1)
                else:
                    link(ins)
            dve.wait_ge(qk_root, 1)
            link(v.reciprocal(sr, sr))
            gq, gk = rows[:, RW["qk_g"]][:, 0:DD], rows[:, RW["qk_g"]][:, DD:2 * DD]
            for ap, n, at in qk:
                a3 = ap.rearrange("p (h c) -> p h c", h=n)
                link(v.tensor_tensor(a3, a3, bc(sr[:, at:at + n], 2, DD), ALU.mult))
                if n == 16:
                    link(v.tensor_tensor(a3[:, 0:8], a3[:, 0:8], bc(gq, 1, 8), ALU.mult))
                    link(v.tensor_tensor(a3[:, 8:16], a3[:, 8:16], bc(gk, 1, 8), ALU.mult))
                else:
                    link(v.tensor_tensor(a3, a3, bc(gk, 1, 8), ALU.mult))
            for t in range(NT):
                cos = const[:, CN["cos"]][:, t * 64:(t + 1) * 64]
                sin = const[:, CN["sin"]][:, t * 64:(t + 1) * 64]
                for lo, n in ((0, 8), (1536, 16)):
                    a = proj[:, t, lo:lo + n * 64]
                    t0, t1 = tmp[:, 0, 0:n * 64], tmp[:, 1, 0:n * 64]

                    def parts(ap):
                        return ap.rearrange("p (h r c) -> p h r c", r=2, c=16)
                    link(v.tensor_tensor(t0.rearrange("p (h c) -> p h c", h=n),
                                         a.rearrange("p (h c) -> p h c", h=n), bc(cos, 1, n), ALU.mult))
                    for half in range(2):
                        x4 = a.rearrange("p (h r s c) -> p h r s c", r=2, s=2, c=16)
                        o4 = t1.rearrange("p (h r s c) -> p h r s c", r=2, s=2, c=16)
                        s4 = sin.rearrange("p (r s c) -> p r s c", r=2, s=2)
                        link(v.tensor_tensor(o4[:, :, :, half, :], x4[:, :, :, 1 - half, :],
                                             bc(s4[:, :, half, :], 1, n), ALU.mult))
                    link(v.tensor_tensor(a, t0, t1, ALU.add))
            v.memset(lamt, 0.0).then_inc(roped, 1)
            modulation(2)
            modulation(3)
            dve.wait_ge(gam_e, 2)
            e = lt[:, 1, :]
            link(v.tensor_scalar(lt[:, 2, :], e, 2.0, None, ALU.add))
            link(v.reciprocal(lt[:, 2, :], lt[:, 2, :]))
            link(v.tensor_tensor(lt[:, 3, :], e, lt[:, 2, :], ALU.mult))
            link(v.tensor_tensor(lt[:, 4, :], lt[:, 3, :], lt[:, 3, :], ALU.mult))
            link(v.tensor_scalar(lt[:, 5, :], lt[:, 4, :], 2.0 / 17, 2.0 / 15, ALU.mult, ALU.add))
            for k in (13, 11, 9, 7, 5, 3, 1):
                link(v.tensor_tensor(lt[:, 5, :], lt[:, 5, :], lt[:, 4, :], ALU.mult))
                link(v.tensor_scalar(lt[:, 5, :], lt[:, 5, :], 2.0 / k, None, ALU.add))
            link(v.tensor_tensor(lt[:, 5, :], lt[:, 5, :], lt[:, 3, :], ALU.mult))
            link(v.scalar_tensor_tensor(lg, x, 0.0, lt[:, 5, :], ALU.min, ALU.subtract))
            link(v.tensor_scalar(nlg, lg, -1.0, None, ALU.mult))
            v.tensor_scalar(lgL, lg, float(T), None, ALU.mult).then_inc(gam_ready, 1)
            dve.wait_ge(lam_exp, 1)
            link(v.tensor_tensor(lam2[:, 2:3], lam2[:, 1:2], lam2[:, 0:1], ALU.subtract))
            link(v.tensor_scalar(lam2[:, 3:4], lam2[:, 2:3], -LAM_INIT, None, ALU.add))
            dve.wait_ge(gam_ready, 1)

            for i, dst in enumerate(turned_views(rqT, rkT, dqT, dkT)):
                dve.wait_ge(turned, i + 1)
                v.tensor_copy(dst, bank[5 + i % 2][:, :].rearrange("p (b t) -> p b t", b=2))\
                 .then_inc(turned_out, 1)
            dist = const[:, CN["dist"]].rearrange("p (k t) -> p k t", k=NT)

            def decay_arg(h):
                w = tmp[:, h % 2, 512:1024].rearrange("p (k t) -> p k t", k=NT)
                u = prob[:, h % 2, :].rearrange("p (k t) -> p k t", k=NT)
                link(v.tensor_scalar(w, dist, 0.0, lg[:, h:h + 1], ALU.max, ALU.mult))
                link(v.tensor_scalar(u, dist, 0.0, nlg[:, 4 + h:5 + h], ALU.min, ALU.mult))
                v.tensor_tensor(w, w, u, ALU.add).then_inc(decay_args, 1)

            decay_arg(0)
            for h in range(RH):
                if h + 1 < RH:
                    decay_arg(h + 1)
                dve.wait_ge(decay_ready, h + 1)
                d = DC[:, h % 2]
                link(v.tensor_tensor(d[:, 0:2, :].rearrange("p k t -> p (k t)"),
                                     d[:, 0:2, :].rearrange("p k t -> p (k t)"),
                                     tmp[:, h % 2, 0:512], ALU.add))
                dve.wait_ge(ret_scores, h + 1)
                if h >= 2:
                    dve.wait_ge(ret_y, h - 1)
                for half in range(2):
                    ins = v.scalar_tensor_tensor(
                        SD[:, h % 2, 2 * half:2 * half + 2].rearrange("p k t -> p (k t)"),
                        bank[1 + 2 * (h % 2) + half][:, :], RK ** -0.5,
                        d[:, 2 * half:2 * half + 2].rearrange("p k t -> p (k t)"), ALU.mult, ALU.mult)
                ins.then_inc(ret_masked, 1)
            for j in range(2):
                dve.wait_ge(ret_y, 2 * j + 2)
                v.tensor_copy(Y[:, :, 256 * j:256 * j + 256].rearrange("p t (h e) -> p h t e", h=2),
                              bank[(0, 7)[j]][:, :].rearrange("p (h t e) -> p h t e", h=2, t=NT))\
                 .then_inc(ret_y_out, 1)
            def diff_maxima(i):
                for c in range(2):
                    dve.wait_ge(diff_scores, 2 * i + c + 1)
                    link(v.reduce_max(zm[:, i % 2, 0, c:c + 1], bank[1 + 2 * (i % 2) + c][:, :], AX))
                    v.tensor_scalar(zm[:, i % 2, 1, c:c + 1], zm[:, i % 2, 0, c:c + 1], -DD ** -0.5, None,
                                    ALU.mult).then_inc(diff_max, 1)

            diff_maxima(0)
            diff_maxima(1)
            for i in range(DH * NT):
                pr = probs[i % 2]
                dve.wait_ge(diff_exp, 2 * i + 2)
                link(v.reciprocal(zr[:, 0, :], zz[:, i % 2, :]))
                link(v.tensor_tensor(zr[:, 1, 0:1], zr[:, 0, 1:2], lam2[:, 3:4], ALU.mult))
                link(v.tensor_scalar(pr[:, 0, :], pr[:, 0, :], zr[:, 0, 0:1], None, ALU.mult))
                if i >= 2:
                    dve.wait_ge(diff_aT, i - 1)
                v.scalar_tensor_tensor(tmp[:, i % 2, 0:512], pr[:, 1, :], zr[:, 1, 0:1], pr[:, 0, :],
                                       ALU.mult, ALU.add).then_inc(diff_a, 1)
                if i + 2 < DH * NT:
                    diff_maxima(i + 2)
            for j in range(2):
                dve.wait_ge(diff_y, 4 * j + 4)
                link(v.tensor_copy(
                    Y[:, :, 512 + 256 * j:768 + 256 * j].rearrange("p t (h e) -> p h t e", h=2),
                    bank[(0, 7)[j]][:, :].rearrange("p (h t e) -> p h t e", h=2, t=NT)))
            for t in range(NT):
                dve.wait_ge(diff_aT, DH * NT)
                link(v.tensor_tensor(tmp[:, t, :], Y[:, t, :], Y[:, t, :], ALU.mult))
                ins = v.tensor_reduce(ss[:, 8 * t:8 * t + 8], tmp[:, t, :].rearrange("p (h e) -> p h e", h=8),
                                      AX, ALU.add)
                if t == NT - 1:
                    ins.then_inc(y_ms, 1)
                else:
                    link(ins)
            dve.wait_ge(y_root, 1)
            link(v.reciprocal(sr[:, 0:16], sr[:, 0:16]))
            for t in range(NT):
                y = Y[:, t, :]
                y3 = y.rearrange("p (h e) -> p h e", h=8)
                link(v.tensor_tensor(y3, y3, bc(sr[:, 8 * t:8 * t + 8], 2, RV), ALU.mult))
                link(v.tensor_tensor(y[:, 0:512], y[:, 0:512], proj[:, t, 1024:1536], ALU.mult))
                link(v.tensor_tensor(y[:, 0:512], y[:, 0:512], rows[:, RW["ret_g"]], ALU.mult))
                v.scalar_tensor_tensor(y[:, 512:1024], y[:, 512:1024], 1.0 - LAM_INIT,
                                       rows[:, RW["diff_g"]], ALU.mult, ALU.mult).then_inc(mix_ready, 1)
            modulation(4)
            link(v.scalar_tensor_tensor(scale2, modv[:, 4 * KD:5 * KD, 0], 1.0,
                                        small[:, SM["g2"]], ALU.add, ALU.mult))
            for n in range(N_OUT):
                chunk_done(dve, C_OUT1 + n)
                for m in (2 * n, 2 * n + 1):
                    link(v.scalar_tensor_tensor(xT[:, m, :], bank[1 + n][:, (m % 2) * T:(m % 2 + 1) * T],
                                                modv[:, 2 * KD + m, 0:1], xT[:, m, :], ALU.mult, ALU.add))
            v.memset(zr, 0.0).then_inc(x2_ready, 1)
            dve.wait_ge(rms_root, 1)
            link(v.reciprocal(rstd2, rstd2))
            for k in range(KD):
                ins = v.scalar_tensor_tensor(h2T[:, k, :], xT[:, k, :], scale2[:, k:k + 1], rstd2,
                                             ALU.mult, ALU.mult)
            link(ins)
            for k in range(KD):
                ins = v.tensor_scalar(h2T[:, k, :], h2T[:, k, :], modv[:, 3 * KD + k, 0:1], None, ALU.add)
            ins.then_inc(h2_ready, 1)
            low = -3.0e38

            def best_keys(unit):
                t, h = unit // PH, unit % PH
                dve.wait_ge(keys_out, h + 1)
                src = keyS0[:, h % 2] if t == 0 else keyS1[:, h]
                for first in (True, False):
                    r = slice(0, 8) if first else slice(8, 16)
                    for p in range(2):
                        ins = v.max(topv[:, p, r], src[:, p, :])
                    link(ins)
                    for p in range(2):
                        ins = v.max_index(topi[:, p, r], topv[:, p, r], src[:, p, :])
                    link(ins)
                    if first:
                        for p in range(2):
                            ins = v.match_replace(src[:, p, :], topv[:, p, r], src[:, p, :], low)
                        link(ins)
                link(v.tensor_copy(topf, topi))

            def choose(unit):
                link(v.tensor_tensor(cand.rearrange("p (a b) -> p a b", a=TOPK), bc(topv[:, 0, :], 2, TOPK),
                                     bc(topv[:, 1, :], 1, TOPK), ALU.add))
                best = gates[:, unit * TOPK:(unit + 1) * TOPK]
                for first in (True, False):
                    r = slice(0, 8) if first else slice(8, 16)
                    link(v.max(best[:, r], cand))
                    link(v.max_index(pos[:, r], best[:, r], cand))
                    if first:
                        link(v.match_replace(cand, best[:, r], cand, low))
                link(v.tensor_copy(gsum, best[:, 0:1]))
                v.tensor_scalar(best, best, gsum, None, ALU.subtract).then_inc(top_exp, 1)
                link(v.tensor_scalar(posu[:, 0, :], pos, 4, None, ALU.logical_shift_right))
                link(v.tensor_scalar(posu[:, 1, :], pos, TOPK - 1, None, ALU.bitwise_and))
                link(v.tensor_copy(posf, posu))
                for p in range(2):
                    link(v.tensor_tensor(hot, bc(posf[:, p, :], 2, TOPK), bc(const[:, CN["iota"]], 1, TOPK),
                                         ALU.is_equal))
                    link(v.tensor_tensor(hot, hot, bc(topf[:, p, :], 1, TOPK), ALU.mult))
                    link(v.tensor_reduce(chosen[:, p, :], hot, AX, ALU.add))
                link(v.scalar_tensor_tensor(posf[:, 0, :], chosen[:, 0, :], float(NK), chosen[:, 1, :],
                                            ALU.mult, ALU.add))
                link(v.tensor_copy(expert[:, unit * TOPK:(unit + 1) * TOPK], posf[:, 0, :]))
                dve.wait_ge(top_expd, unit + 1)
                link(v.tensor_reduce(gsum, best, AX, ALU.add))
                link(v.reciprocal(gsum, gsum))
                v.tensor_scalar(best, best, gsum, None, ALU.mult).then_inc(top_ready, 1)

            def add_experts(t):
                for i in range(2):
                    dve.wait_ge(ffnT_done, 2 * t + i + 1)
                    for m in range(4 * i, 4 * i + 4):
                        x_ = xT[:, m, t * P:(t + 1) * P]
                        ins = v.scalar_tensor_tensor(x_, bank[5 + i][:, (m % 4) * P:(m % 4 + 1) * P],
                                                     modv[:, 5 * KD + m, 0:1], x_, ALU.mult, ALU.add)
                return ins

            for unit in range(2):
                best_keys(unit)
                choose(unit)
            dve.wait_ge(top_ready, 2)
            v.memset(zr, 0.0).then_inc(dot_done, 1)
            dve.wait_ge(tokens_out, 4)
            for unit in range(UNITS):
                t = unit // PH
                for half in range(2):
                    for j in range(GS):
                        n = unit * TOPK + half * GS + j
                        dve.wait_ge(gathered[j], 16 * (n // GS + 1))
                        dve.wait_ge(dot_done, n + 1)
                        v.tensor_tensor_reduce(out=junk, in0=G[:, j, 0:D], in1=h2[:, t, :], scale=1.0,
                                               scalar=0.0, op0=ALU.mult, op1=ALU.add,
                                               accum_out=dots[:, j // 4, j % 4:j % 4 + 1])\
                         .then_inc(dot_done, 1)
                    if unit + 2 < UNITS:
                        (best_keys, choose)[half](unit + 2)
                if unit == PH:
                    modulation(5)
                    add_experts(0)
            add_experts(1).then_inc(x2_ready, 1)
            dve.wait_ge(rms_root, 2)
            v.memset(cvin[:, :, 0:CONV - 1], 0.0)
            link(v.reciprocal(rstd3, rstd3))
            for k in range(KD):
                ins = v.scalar_tensor_tensor(h3T[:, k, :], xT[:, k, :], small[:, SM["g3"]][:, k:k + 1], rstd3,
                                             ALU.mult, ALU.mult)
            ins.then_inc(h3_ready, 1)
            dve.wait_ge(ab_done, 1)
            both = bank[1][:, 0:NT * 8].rearrange("p (t c) -> p t c", t=NT)
            flat = lambda a: a.rearrange("p t h -> p (t h)")
            link(v.tensor_tensor(ab[:, 0], both[:, :, 0:4], bc(rows[:, RW["dt"]], 1, NT), ALU.add))
            link(v.tensor_copy(beta.rearrange("p (t h) -> p t h", t=NT), both[:, :, 4:8]))
            link(v.tensor_scalar(spt[:, 2, :], flat(ab[:, 0]), -1.0, None, ALU.mult))
            v.tensor_tensor(spt[:, 0, :], flat(ab[:, 0]), spt[:, 2, :], ALU.min).then_inc(ab_exp, 1)
            dve.wait_ge(ab_expd, 1)
            e = spt[:, 1, :]
            link(v.tensor_scalar(spt[:, 2, :], e, 2.0, None, ALU.add))
            link(v.reciprocal(spt[:, 2, :], spt[:, 2, :]))
            link(v.tensor_tensor(spt[:, 3, :], e, spt[:, 2, :], ALU.mult))
            link(v.tensor_tensor(spt[:, 4, :], spt[:, 3, :], spt[:, 3, :], ALU.mult))
            link(v.tensor_scalar(spt[:, 2, :], spt[:, 4, :], 2.0 / 17, 2.0 / 15, ALU.mult, ALU.add))
            for k in (13, 11, 9, 7, 5, 3, 1):
                link(v.tensor_tensor(spt[:, 2, :], spt[:, 2, :], spt[:, 4, :], ALU.mult))
                link(v.tensor_scalar(spt[:, 2, :], spt[:, 2, :], 2.0 / k, None, ALU.add))
            link(v.tensor_tensor(spt[:, 2, :], spt[:, 2, :], spt[:, 3, :], ALU.mult))
            link(v.scalar_tensor_tensor(spt[:, 3, :], flat(ab[:, 0]), 0.0, spt[:, 2, :], ALU.max, ALU.add))
            link(v.tensor_tensor(g8.rearrange("p (t h) -> p t h", t=NT),
                                 spt[:, 3, :].rearrange("p (t h) -> p t h", t=NT), bc(kd[:, 0:4], 1, NT),
                                 ALU.mult))
            link(v.tensor_scalar(g8, g8, -1.0, None, ALU.mult))
            link(v.tensor_scalar(beta, beta, 1.0, None, ALU.add))
            v.reciprocal(beta, beta).then_inc(g_ready, 1)
            cw = small[:, SM["conv"]].rearrange("p (b i) -> p b i", i=CONV)

            def convolve(i):
                dve.wait_ge(in2_out, i + 1)
                for tap in range(CONV):
                    for b in (2 * i, 2 * i + 1):
                        src = cvin[:, b, tap:tap + T]
                        if tap == 0:
                            ins = v.tensor_scalar(cvT[:, b, :], src, cw[:, b, 0:1], None, ALU.mult)
                        else:
                            ins = v.scalar_tensor_tensor(cvT[:, b, :], src, cw[:, b, tap:tap + 1], cvT[:, b, :],
                                                         ALU.mult, ALU.add)
                    if tap < CONV - 1:
                        link(ins)
                ins.then_inc(conv_ready, 1)

            convolve(0)
            convolve(1)
            dve.wait_ge(g_copied, 1)
            link(v.tensor_tensor(gD, gR, bc(gc, 2, P), ALU.subtract))
            link(v.tensor_scalar(gDT, gD, 0.0, None, ALU.min))
            link(v.tensor_scalar(gD, gD, 0.0, -1.0, ALU.max, ALU.mult))
            v.tensor_tensor(kd, gR[:, :, P - 1], gc, ALU.subtract).then_inc(gx_ready, 1)
            convolve(2)
            convolve(3)
            dve.wait_ge(gx_exp, 1)
            v.tensor_tensor(gDT, gDT, bc(const[:, CN["upper"]], 1, 8), ALU.mult).then_inc(gx_ready, 1)
            v.tensor_tensor(bg, beta, egc, ALU.mult).then_inc(gx_ready, 1)
            convolve(4)
            link(v.tensor_tensor(gD, gD, bc(beta, 2, P), ALU.mult))
            dve.wait_ge(lnorm_root, 1)
            link(v.reciprocal(qk_norm, qk_norm))
            qn = qk_norm.rearrange("p (t b) -> p t b", t=NT)[:, :, 0:4]
            v.tensor_scalar(qn, qn, GD ** -0.5, None, ALU.mult).then_inc(lnorm_root, 1)
            convolve(5)
            for j, i in enumerate((2, 3, 0, 1)):
                dve.wait_ge(norms_spread, j // 2 + 1)
                c = cvT[:, 2 * i:2 * i + 2, :]
                ins = v.tensor_tensor(c, c, bank[3 + i][:, :].rearrange("p (k t) -> p k t", k=2), ALU.mult)
                if j % 2:
                    ins.then_inc(lnorm_done, 1)
            dve.wait_ge(kk_done, 1)
            for i in range(2):
                q4 = slice(4 * i, 4 * i + 4)
                ins = v.tensor_tensor(gA[:, q4, :], bank[1 + i][:, :].rearrange("p (a b) -> p a b", a=4),
                                      gD[:, q4, :], ALU.mult)
            ins.then_inc(a_ready, 1)
            dve.wait_ge(a_ready, 1)
            dve.wait_ge(masks_here, 48)
            link(v.tensor_tensor(gT_, gA, bc(masks[:, 0, 0, :], 1, 8), ALU.mult))
            link(v.tensor_tensor(gT_, bc(ident, 1, 8), gT_, ALU.subtract))
            dve.wait_ge(at_out, 1)
            link(v.tensor_tensor(gTT, gAT, bc(masks[:, 1, 0, :], 1, 8), ALU.mult))
            v.tensor_tensor(gTT, bc(ident, 1, 8), gTT, ALU.subtract).then_inc(t_in, 2)
            for s in range(1, LEVELS):
                for i in range(2):
                    dve.wait_ge(t_done, 2 * (s - 1) + i + 1)
                    q4 = slice(4 * i, 4 * i + 4)
                    dve.wait_ge(t_in, 2 * s + i)
                    link(v.tensor_tensor(gT_[:, q4, :], gT_[:, q4, :],
                                         bank[3 + i][:, :].rearrange("p (a b) -> p a b", a=4), ALU.subtract))
                    v.tensor_tensor(gTT[:, q4, :], gTT[:, q4, :],
                                    bank[5 + i][:, :].rearrange("p (a b) -> p a b", a=4), ALU.subtract)\
                     .then_inc(t_in, 1)
            dve.wait_ge(pt_done, 1)
            for i in range(2):
                q4 = slice(4 * i, 4 * i + 4)
                ins = v.tensor_tensor(gM[:, q4, :], gDT[:, q4, :],
                                      bank[5 + i][:, :].rearrange("p (a b) -> p a b", a=4), ALU.mult)
            ins.then_inc(pt_ready, 1)
            dve.wait_ge(u1_done, 1)
            v.tensor_tensor(gU[:, 4:8, :], gU[:, 4:8, :],
                            bank[3][:, :].rearrange("p (a b) -> p a b", a=4), ALU.subtract).then_inc(pt_ready, 1)
            dve.wait_ge(u1_done, 2)
            for c in range(2):
                link(v.tensor_copy(Y2[:, c, 512:1024], bank[1 + c][:, :]))
                link(v.tensor_tensor(vTM[:, 4 * c:4 * c + 4, :].rearrange("p a b -> p (a b)"),
                                     Y2[:, c, 512:1024], Y2[:, c, 512:1024], ALU.mult))
            link(v.tensor_reduce(ms2, vTM, AX, ALU.add))
            v.memset(zr, 0.0).then_inc(y_ms, 1)
            for h in range(MH):
                b = bank[3 + h % 2]
                if h >= 2:
                    dve.wait_ge(moba_e, h - 1)
                dve.wait_ge(moba_s, h + 1)
                link(v.reduce_max(mx[:, h % 2, 0, 0:1], b[:, 0:P], AX))
                link(v.reduce_max(mx[:, h % 2, 0, 1:2], b[:, P:3 * P], AX))
                v.tensor_scalar(mx[:, h % 2, 1, :], mx[:, h % 2, 0, :], -MD ** -0.5, None, ALU.mult)\
                 .then_inc(moba_m, 1)
            dve.wait_ge(y_root, 2)
            link(v.reciprocal(ms2, ms2))
            for c in range(2):
                y = Y2[:, c, 512:1024]
                y3 = y.rearrange("p (h e) -> p h e", h=GH)
                link(v.tensor_tensor(y3, y3, bc(ms2[:, 4 * c:4 * c + 4], 2, GD), ALU.mult))
                link(v.tensor_tensor(y3, y3, bc(rows[:, RW["gdn_g"]], 1, GH), ALU.mult))
                link(v.tensor_tensor(y, y, gz[:, c, :], ALU.mult))
            dve.wait_ge(moba_e, MH)
            link(v.reciprocal(rz, rz))
            dve.wait_ge(moba_y, MH)
            for t in range(NT):
                ins = v.tensor_tensor(Y2[:, t, 0:512].rearrange("p (h e) -> p h e", h=MH),
                                      bank[1 + t][:, :].rearrange("p (h e) -> p h e", h=MH),
                                      bc(rz[:, t, :], 2, MD), ALU.mult)
            ins.then_inc(mix_ready, 1)
            for n in range(N_OUT):
                chunk_done(dve, C_OUT2 + n)
                x_ = xT[:, 2 * n:2 * n + 2, :]
                ins = v.tensor_tensor(x_, x_, bank[1 + n][:, :].rearrange("p (k t) -> p k t", k=2), ALU.add)
            ins.then_inc(x3_ready, 1)
            dve.wait_ge(rms_root, 3)
            link(v.reciprocal(rstd4, rstd4))
            for k in range(KD):
                ins = v.scalar_tensor_tensor(h4T[:, k, :], xT[:, k, :], small[:, SM["g4"]][:, k:k + 1], rstd4,
                                             ALU.mult, ALU.mult)
            ins.then_inc(h4_ready, 1)
            dve.wait_ge(route_done, 1)
            link(v.tensor_copy(logit, bank[4][:, 0:NT * (NG + NE)].rearrange("p (t e) -> p t e", t=NT)))
            link(v.memset(pad8, low))
            link(v.tensor_copy(pad8[:, :, 0:NG], logit[:, :, 0:NG]))
            for t in range(NT):
                link(v.max(gm8[:, t, :], pad8[:, t, :]))
                link(v.max_index(gi8[:, t, :], gm8[:, t, :], pad8[:, t, :]))
            link(v.tensor_copy(gif, gi8))
            iota = const[:, CN["iota"]]
            link(v.tensor_tensor(ghot, bc(iota[:, 0:NG], 1, NT), bc(gif[:, :, 0], 2, NG), ALU.is_equal))
            for t in range(NT):
                link(v.tensor_tensor(gsel[:, t], logit[:, t, NG:].rearrange("p (g e) -> p e g", g=NG),
                                     bc(ghot[:, t, :], 1, EG), ALU.mult))
            link(v.tensor_reduce(ing, gsel, AX, ALU.add))
            for t in range(NT):
                link(v.max(im8[:, t, :], ing[:, t, :]))
                link(v.max_index(ii8[:, t, :], im8[:, t, :], ing[:, t, :]))
            link(v.tensor_copy(iif, ii8))
            link(v.tensor_tensor(pw[:, :, 0], im8[:, :, 1], im8[:, :, 0], ALU.subtract))
            v.tensor_tensor(gex, logit[:, :, 0:NG], bc(gm8[:, :, 0], 2, NG), ALU.subtract).then_inc(route_exp, 1)
            for r in range(2):
                link(v.tensor_tensor(within[:, r], bc(iota[:, 0:EG], 1, NT), bc(iif[:, :, r], 2, EG),
                                     ALU.is_equal))
            dve.wait_ge(numbers_ready, 1)
            for t in range(NT):
                by_group = lambda a: a.rearrange("p (g e) -> p g e", g=NG)
                link(v.tensor_tensor(by_group(tags[:, t, :, 1]), bc(ghot[:, t, :], 2, EG),
                                     bc(within[:, 1, t, :], 1, NG), ALU.mult))
                link(v.tensor_tensor(by_group(rank_in[:, t]), bc(ghot[:, t, :], 2, EG),
                                     bc(within[:, 0, t, :], 1, NG), ALU.mult))
            link(v.tensor_copy(tags[:, :, :, 0], bc(token_no, 2, NE)))
            v.tensor_tensor(rank_in, rank_in, tags[:, :, :, 1], ALU.add).then_inc(chosen_ready, 1)
            dve.wait_ge(route_done, 2)
            v.tensor_tensor(rank, rank_in, bank[4][:, P:P + NT * NE].rearrange("p (t e) -> p t e", t=NT),
                            ALU.mult).then_inc(rank_ready, 1)
            dve.wait_ge(rank_ready, 1)
            for t in range(NT):
                v.tensor_tensor(hot4[:, t], bc(slot_no[:, 0], 1, NE), bc(rank[:, t], 2, P),
                                ALU.is_equal).then_inc(hot_ready, 1)
            link(v.tensor_reduce(most[:, 0:1], bank[4][:, P + NT * NE:P + (NT + 1) * NE], AX, ALU.max))
            link(v.tensor_scalar(most[:, 1:2], most[:, 0:1], float(P), float(PAIRS), ALU.is_gt, ALU.mult))
            link(v.tensor_scalar(pairs, most[:, 1:2], float(PAIRS), None, ALU.add))
            link(v.memset(to_row, NONE))
            link(v.memset(from_row, NONE))

            def slot_table(w):
                dve.wait_ge(route_done, 3 + w)
                e = slice(w * NE, (w + 1) * NE)
                sv, ab_ = slotv[:, e], absent[:, e]
                link(v.tensor_copy(sv, bank[5 + w][:, 0:2 * NE].rearrange("p (n a) -> p n a", a=2)))
                link(v.tensor_scalar(ab_, sv[:, :, 0], 0.0, float(NONE), ALU.is_equal, ALU.mult))
                link(v.tensor_tensor(ab_, ab_, sv[:, :, 0], ALU.add))
                link(v.tensor_scalar(from_row[:, e], ab_, -1.0, None, ALU.add))
                link(v.tensor_scalar(ab_, ab_, 2.0, -2.0, ALU.mult, ALU.add))
                v.tensor_tensor(to_row[:, e], ab_, sv[:, :, 1], ALU.add).then_inc(slots_ready, 1)

            slot_table(0)
            v.tensor_tensor(hot4[:, 2], bc(slot_no[:, 1], 1, NE), bc(rank[:, 1], 2, P),
                            ALU.is_equal).then_inc(hot_ready, 1)
            dve.wait_ge(route_expd, 1)
            link(v.tensor_reduce(pw[:, :, 3], gex, AX, ALU.add))
            link(v.reciprocal(pw[:, :, 3], pw[:, :, 3]))
            link(v.tensor_scalar(pw[:, :, 2], pw[:, :, 1], 1.0, None, ALU.add))
            link(v.reciprocal(pw[:, :, 2], pw[:, :, 2]))
            link(v.tensor_tensor(pw[:, :, 2], pw[:, :, 2], pw[:, :, 3], ALU.mult))
            link(v.tensor_tensor(pw[:, :, 3], pw[:, :, 2], pw[:, :, 1], ALU.mult))
            slot_table(1)
            v.memset(zz, 0.0).then_inc(y_right, 2)

            def turned_rows(b, wait_n):
                dve.wait_ge(x_turned, wait_n)
                v.tensor_copy(XT[:, b, 4:8].rearrange("p k t -> p (k t)"), bank[1][:, :]).then_inc(xt_right, 1)

            for b in range(2):
                turned_rows(b, b + 1)
            dve.wait_ge(slots_ready, 1)
            n_pairs = dve.value_load(pairs[0:1, 0:1], min_val=PAIRS, max_val=WINDOWS * PAIRS)
            with dve.Fori(0, n_pairs) as i:
                for b in range(2):
                    dve.wait_ge(silu_ready, 2 * i + (b + 1))
                    v.tensor_tensor(hid[:, b], bank[2 + b][:, FF:2 * FF], sg[:, b], ALU.mult).then_inc(hid_ready, 1)
                for b in range(2):
                    dve.wait_ge(hid_turned, 2 * i + (b + 1))
                    v.tensor_copy(hidT[:, b].rearrange("p k t -> p (k t)"), bank[2 + b][:, 0:FF])\
                     .then_inc(hidT_ready, 1)
                    turned_rows(b, 2 * i + (b + 3))
                    dve.wait_ge(scattered[b], 16 * i + 16)
                    dve.wait_ge(down_used, 2 * i + (b + 1))
                    v.tensor_copy(Yx[:, b, 512:1024], bank[5 + 2 * b][:, :]).then_inc(y_right, 1)
            for t in range(NT):
                dve.wait_ge((y_back, y_back1)[t], 16)
                for r in range(2):
                    ins = v.scalar_tensor_tensor(x3[:, t], back[:, t, r], pw[:, t, 2 + r:3 + r], x3[:, t],
                                                 ALU.mult, ALU.add)
                    if r == 0:
                        link(ins)
                ins.then_inc(x4_ready, 1)
            for t in range(NT):
                dve.wait_ge(final_g_here, 16)
                dve.wait_ge(rms_root, 4 + t)
                link(v.reciprocal(ms4[:, t:t + 1], ms4[:, t:t + 1]))
                v.scalar_tensor_tensor(x3[:, t], x3[:, t], ms4[:, t:t + 1], final_g,
                                       ALU.mult, ALU.mult).then_inc(out_ready, 1)

        @block.tensor
        def _(pe):
            mm = nc.tensor.matmul
            pe.wait_ge(inputs_ready, 1)
            mod_products(pe, 0, (1, 2))
            pe.wait_ge(const_here, 32)
            for i, q in enumerate((sq, csq)):
                pe.wait_ge(inputs_ready, i + 2)
                for k in range(KD):
                    ins = mm(bank[7][:, i * T:(i + 1) * T], ones, q[:, k, :], start=k == 0, stop=k == KD - 1)
            ins.then_inc(sums1, 1)
            mod_products(pe, 1, (3, 4))
            mod_turn(pe, 0)
            pe.wait_ge(root1, 1)
            mod_turn(pe, 1)
            n_c = 0
            for n in range(N_IN1):
                chunk_ready(pe, C_IN1 + n)
                w = wchunk(C_IN1 + n)
                if n >= 2:
                    pe.wait_ge(proj_x_out, n - 1)
                groups = [(bank[1 + 2 * (n % 2)], hT)]
                if n in CTX_CHUNKS:
                    n_c += 1
                    if n_c >= 2:
                        pe.wait_ge(proj_c_out, n_c - 1)
                    groups.append((bank[2 + 2 * (n % 2)], chT))
                for out, h in groups:
                    for t in range(NT):
                        for k in range(KD):
                            if n == 0 and t == 0:
                                pe.wait_ge(h_ready, k + 1)
                            if n == 1 and t == 0 and h is chT:
                                pe.wait_ge(h_ready, KD + k + 1)
                            ins = mm(out[:, t * COLS:(t + 1) * COLS], h[:, k, t * P:(t + 1) * P],
                                     w[:, k, :], start=k == 0, stop=k == KD - 1)
                ins.then_inc(chunk_used, 1)
            mod_products(pe, 2, (5, 6))
            pe.wait_ge(proj_x_out, N_IN1 - 1)
            pe.wait_ge(proj_c_out, len(CTX_CHUNKS) - 1)
            mod_products(pe, 3, (1, 2))
            mod_turn(pe, 2)
            mod_turn(pe, 3)
            pe.wait_ge(roped, 1)
            sources = [(proj, 0), (proj, 256), (cproj, 0)]
            sources += [(proj, 1536 + 256 * i) for i in range(4)] + [(cproj, 768 + 256 * i) for i in range(2)]
            for i, (src, at) in enumerate(sources):
                if i >= 2:
                    pe.wait_ge(turned_out, i - 1)
                for b in range(2):
                    for t in range(NT):
                        ins = nc.tensor.transpose(bank[5 + i % 2][:, b * T + t * P:b * T + (t + 1) * P],
                                                  src[:, t, at + b * P:at + (b + 1) * P], ident)
                ins.then_inc(turned, 1)
            pe.wait_ge(turned_out, len(sources))

            def scores(h):
                r = slice(RK * (h % 2), RK * (h % 2) + RK)
                if h >= 2:
                    pe.wait_ge(ret_masked, h - 1)
                for k in range(4):
                    ins = mm(bank[1 + 2 * (h % 2) + k // 2][:, (k % 2) * T:(k % 2 + 1) * T],
                             rkT[r, h // 2, k * P:(k + 1) * P], rqT[r, h // 2, :], start=True, stop=True)
                ins.then_inc(ret_scores, 1)

            def outputs(h):
                pe.wait_ge(ret_masked, h + 1)
                for t in range(NT):
                    for k in range(4):
                        val = cproj[:, k, 256 + h * RV:256 + (h + 1) * RV] if k < 2 else \
                            proj[:, k - 2, 512 + h * RV:512 + (h + 1) * RV]
                        ins = mm(bank[(0, 7)[h // 2]][:, (h % 2) * 256 + t * P:(h % 2) * 256 + (t + 1) * P],
                                 SD[:, h % 2, k, t * P:(t + 1) * P], val, start=k == 0, stop=k == 3)
                ins.then_inc(ret_y, 1)

            scores(0)
            for h in range(RH):
                if h + 1 < RH:
                    scores(h + 1)
                outputs(h)

            def diff_scores_of(i):
                h, t = i // NT, i % NT
                if i >= 2:
                    pe.wait_ge(diff_exp, 2 * i - 2)
                for c in range(2):
                    r = slice(DD * c, DD * (c + 1))
                    mm(bank[1 + 2 * (i % 2) + c][:, :], dqT[r, h, t * P:(t + 1) * P], dkT[r, h, :],
                       start=True, stop=True).then_inc(diff_scores, 1)

            def diff_turn(i):
                pe.wait_ge(diff_a, i + 1)
                if i == 1:
                    pe.wait_ge(mod_out, 2 * 4 + 1)
                if i >= 2:
                    pe.wait_ge(diff_aT_out, i - 1)
                for k in range(4):
                    ins = nc.tensor.transpose(bank[5 + i % 2][:, k * P:(k + 1) * P],
                                              tmp[:, i % 2, k * P:(k + 1) * P], ident)
                ins.then_inc(diff_aT, 1)

            def diff_outputs_of(i):
                h, t = i // NT, i % NT
                pe.wait_ge(diff_aT_out, i + 1)
                if h % 2 == 0 and t == 0:
                    pe.wait_ge(ret_y_out, h // 2 + 1)
                for k in range(4):
                    val = cproj[:, k, 1280 + h * RV:1280 + (h + 1) * RV] if k < 2 else \
                        proj[:, k - 2, 2560 + h * RV:2560 + (h + 1) * RV]
                    ins = mm(bank[(0, 7)[h // 2]][:, (h % 2) * 256 + t * P:(h % 2) * 256 + (t + 1) * P],
                             aT[:, i % 2, k, :], val, start=k == 0, stop=k == 3)
                ins.then_inc(diff_y, 1)

            pe.wait_ge(ret_masked, RH)
            diff_scores_of(0)
            diff_scores_of(1)
            mod_products(pe, 4, (6, 1), (0, 1))
            for i in range(DH * NT):
                if i + 2 < DH * NT:
                    diff_scores_of(i + 2)
                diff_turn(i)
                if i >= 1:
                    diff_outputs_of(i - 1)
            diff_outputs_of(DH * NT - 1)
            pe.wait_ge(diff_exp, 2 * DH * NT)
            mod_products(pe, 4, (6, 1), (2, 3))
            pe.wait_ge(mix_ready, NT)
            mod_turn(pe, 4)
            for g in range(4):
                if g >= 2:
                    pe.wait_ge(mixT_out, g - 1)
                for b in range(2):
                    for t in range(NT):
                        ins = nc.tensor.transpose(bank[5 + g % 2][:, b * T + t * P:b * T + (t + 1) * P],
                                                  Y[:, t, (2 * g + b) * P:(2 * g + b + 1) * P], ident)
                ins.then_inc(mixT_done, 1)
            pe.wait_ge(mixT_out, 4)
            project_fm(pe, C_OUT1, N_OUT, mixT)
            sums_over_features(pe, sq2, 1)
            pe.wait_ge(h2_ready, 1)
            keys = wchunk(C_SK).rearrange("p k c -> p (k c)").rearrange("p (h n) -> p h n", h=2 * PH)

            def query(h, j):
                chunk_ready(pe, C_Q + h + (h > 0))
                w = wchunk(C_Q + h + (h > 0))
                if h >= 1:
                    pe.wait_ge(q_out, h)
                for k in range(KD):
                    ins = mm(bank[5][:, j * T:(j + 1) * T], w[:, k, j * P:(j + 1) * P], h2T[:, k, :],
                             start=k == 0, stop=k == KD - 1)
                if j == 1:
                    ins.then_inc(chunk_used if h == 0 else q_done, 1)

            def key_scores(h):
                chunk_ready(pe, C_SK)
                pe.wait_ge(q_out, h + 1)
                if h >= 1:
                    pe.wait_ge(keys_out, h)
                for t in range(NT):
                    for p in range(2):
                        ins = mm(bank[6][:, (2 * t + p) * NK:(2 * t + p + 1) * NK],
                                 qT[:, h % 2, p, t * P:(t + 1) * P], keys[:, 2 * h + p, :], start=True, stop=True)
                if h < PH - 1:
                    ins.then_inc(keys_done, 1)
                else:
                    ins.then_inc(chunk_used, N_Q)

            def weighted_rows(first):
                for j in range(GS):
                    pe.wait_ge(diag_ready, first + (j + 1))
                    for c in range(2):
                        ins = mm(bank[1 + 2 * tile + c][:, :], diag[:, j, :],
                                 G[:, j, D + c * 512:D + (c + 1) * 512], start=False, stop=False,
                                 skip_group_check=True)
                    ins.then_inc(slot_used, 1)

            tile = 0
            query(0, 0)
            query(0, 1)
            key_scores(0)
            for g in range(4):
                if g >= 2:
                    pe.wait_ge(tokens_out, g - 1)
                t = g // 2
                transposes(pe, bank[(7, 0)[g % 2]], [h2T[:, 4 * (g % 2) + k, t * P:(t + 1) * P] for k in range(4)])\
                    .then_inc(tokens_turned, 1)
            for b in range(1, 5):
                mm(bank[b][:, :], zero, const[:, 0:512], start=True, stop=False, skip_group_check=True)
            for h in (1, 2):
                query(h, 0)
                query(h, 1)
                key_scores(h)
            query(3, 0)
            query(3, 1)
            for unit in range(PH):
                for half in range(2):
                    weighted_rows(unit * TOPK + half * GS)
                    if half == 0 and unit + 3 < PH:
                        key_scores(unit + 3)
                    if unit + 4 < PH:
                        query(unit + 4, half)
                    if unit in (PH - 3, PH - 2):
                        pe.wait_ge(keys_out, PH)
                        mod_products(pe, 5, (5, 6), (2 * (unit - PH + 3) + half,))
            mod_turn(pe, 5)
            for t in range(NT):
                if t > 0:
                    tile = t
                    with pe.Fori(0, SLOTS // GS) as turn:
                        weighted_rows(turn * GS + t * SLOTS)
                pe.wait_ge(ffn_out, t + 1)
                for i in range(2):
                    transposes(pe, bank[5 + i], [ffn[:, (4 * i + k) * P:(4 * i + k + 1) * P] for k in range(4)])\
                        .then_inc(ffnT_done, 1)
            sums_over_features(pe, sq3, 2)
            pe.wait_ge(h3_ready, 1)
            pe.wait_ge(masks_here, 48)
            for t in range(NT):
                for k in range(KD):
                    ins = mm(bank[1][:, t * 8:(t + 1) * 8], h3T[:, k, t * P:(t + 1) * P], gate2[:, k, :],
                             start=k == 0, stop=k == KD - 1)
            ins.then_inc(ab_done, 1)
            in2_half = [0]

            def in2(halves):
                for _ in range(halves):
                    i, j = in2_half[0] // 2, in2_half[0] % 2
                    in2_half[0] += 1
                    out, w = bank[(0, 7)[i % 2]], wchunk(C_IN2 + i)
                    if j == 0:
                        chunk_ready(pe, C_IN2 + i)
                        if i >= 2:
                            pe.wait_ge(in2_out, i - 1)
                    for k in range(KD):
                        if IN2_ORDER[i] in (4, 5, 12, 13):
                            ins = mm(out[:, j * COLS:(j + 1) * COLS], h3T[:, k, j * P:(j + 1) * P], w[:, k, :],
                                     start=k == 0, stop=k == KD - 1)
                        else:
                            ins = mm(out[:, j * T:(j + 1) * T], w[:, k, j * P:(j + 1) * P], h3T[:, k, :],
                                     start=k == 0, stop=k == KD - 1)
                    if j == 1:
                        ins.then_inc(chunk_used, 1)

            def norm_sums(i):
                pe.wait_ge(lnorm_sq, i + 1)
                for b in (2 * i, 2 * i + 1):
                    for t in range(NT):
                        at = t * 8 + b
                        ins = mm(bank[1][:, at:at + 1], nsq[:, b, t * P:(t + 1) * P], ones[:, 0:1],
                                 start=True, stop=True)
                return ins

            in2(4)
            pe.wait_ge(g_ready, 1)
            mm(bank[2][:, 0:8], const[:, CN["upper"]], g8, start=True, stop=True)
            for p in range(8):
                ins = mm(bank[5 + p // 4][:, (p % 4) * P:(p % 4 + 1) * P], bc(g8[:, p], 1, P),
                         const[:, CN["upper"]], start=True, stop=True)
            ins.then_inc(g_done, 1)
            in2(2)
            norm_sums(0)
            in2(2)
            norm_sums(1)
            in2(2)
            norm_sums(2)
            in2(2)
            norm_sums(3).then_inc(lnorm_sum, 1)
            in2(2)
            pe.wait_ge(lnorm_root, 2)
            pe.wait_ge(g_copied, 1)
            for i in (2, 3, 0, 1):
                for b in range(2):
                    for t in range(NT):
                        ins = mm(bank[3 + i][:, b * T + t * P:b * T + (t + 1) * P],
                                 bc(qk_norm[:, t * 8 + 2 * i + b], 1, P), ident, start=True, stop=True)
                if i % 2:
                    ins.then_inc(norms_spread, 1)
            pe.wait_ge(lnorm_done, 1)
            for p in range(8):
                c, h = p // 4, p % 4
                kT = cvT[:, 4 + h, c * P:(c + 1) * P]
                ins = mm(bank[1 + p // 4][:, (p % 4) * P:(p % 4 + 1) * P], kT, kT, start=True, stop=True)
            ins.then_inc(kk_done, 1)
            for c in range(2):
                transposes(pe, bank[5 + c], [cvT[:, 4 + h, c * P:(c + 1) * P] for h in range(4)])\
                    .then_inc(tm_done, 1)
            in2(1)
            pe.wait_ge(a_ready, 1)
            pe.wait_ge(tm_out, 2)
            for i in range(2):
                ins = transposes(pe, bank[5 + i], [gA[:, 4 * i + k, :] for k in range(4)])
            ins.then_inc(at_done, 1)
            in2(1)
            pe.wait_ge(lnorm_done, 2)
            pe.wait_ge(conv_silu, 6)
            for c in range(2):
                transposes(pe, bank[3 + c], [cvT[:, 8 + h, c * P:(c + 1) * P] for h in range(4)])\
                    .then_inc(tm_done, 1)
            pe.wait_ge(at_out, 1)
            pe.wait_ge(tm_out, 4)
            for s in range(1, LEVELS):
                pe.wait_ge(mask_ready, s)
                for i in range(2):
                    pe.wait_ge(t_in, 2 * s + i - 1)
                    for p in range(4 * i, 4 * i + 4):
                        ins = mm(bank[1 + i][:, (p % 4) * P:(p % 4 + 1) * P], (gMT, gM)[s % 2][:, p, :],
                                 gT_[:, p, :], start=True, stop=True)
                    ins.then_inc(w_done, 1)
                for i in range(2):
                    pe.wait_ge(w_out, 2 * (s - 1) + i + 1)
                    for p in range(4 * i, 4 * i + 4):
                        mm(bank[3 + i][:, (p % 4) * P:(p % 4 + 1) * P], gTT[:, p, :], gW[:, p, :],
                           start=True, stop=True)
                        ins = mm(bank[5 + i][:, (p % 4) * P:(p % 4 + 1) * P], gW[:, p, :], gTT[:, p, :],
                                 start=True, stop=True)
                    ins.then_inc(t_done, 1)
                in2(1)
            pe.wait_ge(t_in, 2 * LEVELS)
            pe.wait_ge(prepared, 4)
            for h in range(GH):
                mm(bank[3][:, h * P:(h + 1) * P], gD[:, 4 + h, :], gTT[:, 4 + h, :], start=True, stop=True)
            for p in range(8):
                ins = mm(bank[1 + p // 4][:, (p % 4) * P:(p % 4 + 1) * P], gTT[:, p, :], vTM[:, p, :],
                         start=True, stop=True)
            ins.then_inc(uv_done, 1)
            for p in range(8):
                c, h = p // 4, p % 4
                ins = mm(bank[5 + p // 4][:, (p % 4) * P:(p % 4 + 1) * P], cvT[:, 4 + h, c * P:(c + 1) * P],
                         cvT[:, h, c * P:(c + 1) * P], start=True, stop=True)
            ins.then_inc(pt_done, 1)
            pe.wait_ge(uv_out, 1)
            for h in range(GH):
                ins = mm(bank[4][:, h * P:(h + 1) * P], gD[:, h, :], gU[:, h, :], start=True, stop=True)
            ins.then_inc(s_done, 1)
            in2(1)
            pe.wait_ge(s_out, 1)
            for h in range(GH):
                ins = mm(bank[3][:, h * P:(h + 1) * P], gwT[:, h, :], gS[:, h, :], start=True, stop=True)
            ins.then_inc(u1_done, 1)
            in2(1)
            pe.wait_ge(pt_ready, 2)
            for p in range(8):
                out = bank[1 + p // 4][:, (p % 4) * P:(p % 4 + 1) * P]
                ins = mm(out, gM[:, p, :], gU[:, p, :], start=True, stop=p < 4)
                if p >= 4:
                    ins = mm(out, gR[:, p, :], gS[:, p - 4, :], start=False, stop=True)
            ins.then_inc(u1_done, 1)
            in2(2 * N_IN2 - in2_half[0])

            def moba_scores(h):
                r = slice(MD * (h % 2), MD * (h % 2) + MD)
                b = bank[3 + h % 2]
                if h >= 2:
                    pe.wait_ge(moba_e, h - 1)
                mm(b[:, 0:P], mqT[r, h // 2, 0:P], mkT[r, h // 2, 0:P], start=True, stop=False)
                mm(b[:, 0:P], ident, const[:, CN["causal"]], start=False, stop=True)
                mm(b[:, P:2 * P], mqT[r, h // 2, P:2 * P], mkT[r, h // 2, 0:P], start=True, stop=True)
                mm(b[:, 2 * P:3 * P], mqT[r, h // 2, P:2 * P], mkT[r, h // 2, P:2 * P], start=True, stop=False)
                mm(b[:, 2 * P:3 * P], ident, const[:, CN["causal"]], start=False, stop=True).then_inc(moba_s, 1)

            def moba_outputs(h):
                pe.wait_ge(moba_T_out, h + 1)
                cols = slice(h * MD, (h + 1) * MD)
                mm(bank[1][:, cols], softT[:, h % 2, 0:P], mv[:, 0, cols], start=True, stop=True)
                for k in range(2):
                    ins = mm(bank[2][:, cols], softT[:, h % 2, (1 + k) * P:(2 + k) * P], mv[:, k, cols],
                             start=k == 0, stop=k == 1)
                ins.then_inc(moba_y, 1)

            pe.wait_ge(in2_out, N_IN2)
            moba_scores(0)
            moba_scores(1)
            pe.wait_ge(y_ms, 2)
            for h in range(MH):
                pe.wait_ge(moba_e, h + 1)
                transposes(pe, bank[5 + h % 2], [soft[:, h % 2, k * P:(k + 1) * P] for k in range(3)])\
                    .then_inc(moba_T, 1)
                if h + 2 < MH:
                    moba_scores(h + 2)
                if h >= 1:
                    moba_outputs(h - 1)
            moba_outputs(MH - 1)
            pe.wait_ge(mix_ready, NT + 1)
            for g in range(4):
                if g >= 2:
                    pe.wait_ge(mixT_out, 4 + g - 1)
                transposes(pe, bank[5 + g % 2], [Y2[:, t, (2 * g + b) * P:(2 * g + b + 1) * P]
                                                 for b in range(2) for t in range(NT)]).then_inc(mixT_done, 1)
            pe.wait_ge(mixT_out, 8)
            project_fm(pe, C_OUT2, N_OUT, mix2T)
            sums_over_features(pe, sq4, 3)
            pe.wait_ge(h4_ready, 1)
            for t in range(NT):
                for k in range(KD):
                    ins = mm(bank[4][:, t * (NG + NE):(t + 1) * (NG + NE)], h4T[:, k, t * P:(t + 1) * P],
                             routeW[:, k, :], start=k == 0, stop=k == KD - 1)
            ins.then_inc(route_done, 1)
            for g in range(8):
                if g >= 4:
                    pe.wait_ge(tokens_out, 4 + g - 3)
                src, t = (h4T if g < 4 else xT), (g // 2) % 2
                transposes(pe, bank[g % 4], [src[:, 4 * (g % 2) + k, t * P:(t + 1) * P] for k in range(4)])\
                    .then_inc(tokens_turned, 1)
            pe.wait_ge(chosen_ready, 1)
            upper = const[:, CN["upper"]]
            places = lambda n: bank[4][:, P + n * NE:P + (n + 1) * NE]
            mm(places(0), upper, rank_in[:, 0], start=True, stop=True)
            mm(places(1), upper, rank_in[:, 1], start=True, stop=False)
            mm(places(1), ones, rank_in[:, 0], start=False, stop=True)
            mm(places(2), ones, rank_in[:, 0], start=True, stop=False)
            mm(places(2), ones, rank_in[:, 1], start=False, stop=True).then_inc(route_done, 1)
            slot_tags = lambda w, e: bank[5 + w][:, 2 * e:2 * e + 2]
            pe.wait_ge(hot_ready, NT)
            for e in range(NE):
                for t in range(NT):
                    ins = mm(slot_tags(0, e), hot4[:, t, e], tags[:, t, e], start=t == 0, stop=t == NT - 1)
            ins.then_inc(route_done, 1)
            pe.wait_ge(hot_ready, NT + 1)
            for e in range(NE):
                ins = mm(slot_tags(1, e), hot4[:, 2, e], tags[:, 1, e], start=True, stop=True)
            ins.then_inc(route_done, 1)

            def turn_rows(b, wait_gather, nth):
                pe.wait_ge(gathered[b], wait_gather)
                if nth is not None:
                    pe.wait_ge(xt_left, nth)
                    pe.wait_ge(xt_right, nth)
                for h in range(2):
                    ins = transposes(pe, bank[h], [X[:, b, (4 * h + k) * P:(4 * h + k + 1) * P] for k in range(4)])
                ins.then_inc(x_turned, 1)

            pe.wait_ge(tokens_out, 12)
            turn_rows(0, GATHERED + 16, None)
            turn_rows(1, GATHERED + 16, 1)
            n_pairs = pe.value_load(pairs[0:1, 0:1], min_val=PAIRS, max_val=WINDOWS * PAIRS)
            with pe.Fori(0, n_pairs) as i:
                for b in range(2):
                    pe.wait_ge(gu_here[b], i * 16 + 16)
                    pe.wait_ge(xt_left, 2 * i + (b + 1))
                    pe.wait_ge(xt_right, 2 * i + (b + 1))
                    w = wring[:, 2 * b * CHUNK:(2 * b + 2) * CHUNK].rearrange("p (k c) -> p k c", k=KD)
                    for k in range(KD):
                        ins = mm(bank[2 + b][:, :], XT[:, b, k], w[:, k, :], start=k == 0, stop=k == KD - 1)
                    ins.then_inc(gu_done, 1)
                for b in range(2):
                    pe.wait_ge(hid_ready, 2 * i + (b + 1))
                    transposes(pe, bank[2 + b], [hid[:, b, f * P:(f + 1) * P] for f in range(2)])\
                        .then_inc(hid_turned, 1)
                    turn_rows(b, i * 16 + (GATHERED + 32), 2 * i + (b + 2))
                    pe.wait_ge(down_here[b], i * 16 + 16)
                    pe.wait_ge(hidT_ready, 2 * i + (b + 1))
                    pe.wait_ge(y_left, 2 * i + (b + 1))
                    pe.wait_ge(y_right, 2 * i + (b + 1))
                    w = wring[:, (4 + b) * CHUNK:(5 + b) * CHUNK].rearrange("p (f c) -> p f c", f=2)
                    for h in range(2):
                        for f in range(2):
                            ins = mm(bank[4 + 2 * b + h][:, :], hidT[:, b, f], w[:, f, h * 512:(h + 1) * 512],
                                     start=f == 0, stop=f == 1)
                    ins.then_inc(down_used, 1)


CTX_CHUNKS = (1, 2, 3, 8, 9, 10, 11)


def turned_views(rqT, rkT, dqT, dkT):
    out = [rqT, rkT[:, :, T:2 * T], rkT[:, :, 0:T]]
    out += [dqT[:, 2 * i:2 * i + 2, :] for i in range(2)]
    out += [dkT[:, 2 * i:2 * i + 2, T:2 * T] for i in range(2)]
    out += [dkT[:, 2 * i:2 * i + 2, 0:T] for i in range(2)]
    return out


def constants():
    c = np.zeros((P, CN_N), np.float32)
    p = np.arange(P)
    c[:, CN["ident"]] = np.eye(P)
    c[:, CN["ones"]] = 1.0
    c[:, CN["eps"]] = EPS
    quarter = RK // 4
    freqs = (10000.0 ** (-np.arange(quarter, dtype=np.float32) / quarter)).astype(np.float32)
    t = np.arange(T)
    ar = (t // 64).astype(np.float32)[:, None] * freqs
    ac = (t % 64).astype(np.float32)[:, None] * freqs
    ang = np.concatenate([ar, ar, ac, ac], axis=1).astype(np.float64)
    sign = np.tile(np.repeat([-1.0, 1.0], quarter), 2)
    c[:, CN["cos"]] = np.cos(ang).reshape(NT, P, RK).transpose(1, 0, 2).reshape(P, -1)
    c[:, CN["sin"]] = (np.sin(ang) * sign).reshape(NT, P, RK).transpose(1, 0, 2).reshape(P, -1)
    dist = t[None, None, :] - (np.arange(NT)[None, :, None] * P + p[:, None, None])
    c[:, CN["dist"]] = dist.reshape(P, -1)
    c[:, CN["iota"]] = np.arange(TOPK)
    c[:, CN["upper"]] = p[:, None] <= p[None, :]
    c[:, CN["lower"]] = p[:, None] >= p[None, :]
    c[:, CN["causal"]] = np.where(p[:, None] >= p[None, :], 0.0, -1e30)
    masks = np.zeros((2, LEVELS, P, P), np.float32)
    for s in range(LEVELS):
        w = 1 << s
        low = (p[:, None] // w == p[None, :] // w + 1) & (p[:, None] // (2 * w) == p[None, :] // (2 * w))
        masks[0, s], masks[1, s] = low, low.T
    return c, np.ascontiguousarray(masks.transpose(2, 0, 1, 3)).reshape(P, -1)


def pack(w):
    n = w.shape[1] // COLS
    return w.reshape(KD, P, n, COLS).transpose(2, 1, 0, 3).reshape(n, P, CHUNK)


def fm(a, n):
    return a.reshape(n, P).T


def kernel(**inputs):
    import concourse.bacc as bacc
    from concourse.bass_utils import run_bass_kernel_spmd

    g = {k: np.asarray(a) for k, a in inputs.items()}
    cond = np.stack([g["c"][0], g["c_ctx"]], axis=-1).reshape(KD, P, 2).transpose(1, 0, 2).reshape(P, -1)
    conv = g["conv_w_2"][0].reshape(CONV, 12, P).transpose(2, 1, 0).reshape(P, -1)
    small = np.concatenate([cond, fm(g["b_mod"], 6 * KD), fm(g["norm1_g"], KD), fm(g["norm2_g"], KD),
                            fm(g["attn_norm_2"], KD), fm(g["ffn_norm_2"], KD), fm(g["final_norm_2"], KD),
                            conv], axis=1)
    row = np.concatenate([g[k].reshape(-1) for k in
                          ("ret_norm_g", "diff_norm_g", "diff_qk_norm_g", "diff_lambda", "ret_decay_logit",
                           "gdn_norm_2", "A_log_2", "dt_bias_2")])
    const, masks = constants()
    keys = g["peer_sub_keys"][0].reshape(2 * PH, NK, P).transpose(2, 0, 1).reshape(1, P, CHUNK)
    w2 = g["w_in_2"][0]
    mod = pack(g["w_mod"][0])
    wq = pack(g["peer_w_query"][0])
    m2, m5 = 2 * MOD_GROUP, 5 * MOD_GROUP
    stream = np.concatenate([mod[:m2], pack(g["w_in"][0]), mod[m2:m5], pack(g["w_out"][0]),
                             wq[:1], keys, wq[1:], mod[m5:], pack(w2[:, :3584])[IN2_ORDER],
                             pack(g["w_out_2"][0])])
    fold = lambda w: w.reshape(KD, P, -1).transpose(1, 0, 2)
    gate_up = np.stack([g["w_gate_2"][0].reshape(NE, KD, P, FF), g["w_up_2"][0].reshape(NE, KD, P, FF)], axis=3)
    gate_up = gate_up.transpose(0, 2, 1, 3, 4).reshape(NE, P, 2 * CHUNK)
    down = g["w_down_2"][0].reshape(NE, FF // P, P, D).transpose(0, 2, 1, 3).reshape(NE, P, CHUNK)
    tokens = lambda x: fold(x[0].T)
    arrays = {
        "xT": tokens(g["x"]), "ctxT": tokens(g["ctx"]), "small": small,
        "rows": np.broadcast_to(row, (P, RW_N)), "const": const, "masks": masks, "stream": stream,
        "gate2": fold(w2[:, 3584:]).reshape(P, -1),
        "uv": np.concatenate([g["peer_u"][0], g["peer_v"][0]], axis=1),
        "route": fold(np.concatenate([g["w_group_2"][0], g["w_router_2"][0]], axis=1)).reshape(P, -1),
        "moe": np.concatenate([gate_up, down], axis=2),
        "final_g": np.broadcast_to(g["final_norm_2"], (P, D)),
    }
    arrays = {k: np.ascontiguousarray(a) for k, a in arrays.items()}
    nc = bacc.Bacc("TRN2", target_bir_lowering=False, num_devices=1)
    args = [nc.dram_tensor(f"{k}_in", a.shape, fp32, kind="ExternalInput").ap() for k, a in arrays.items()]
    out = nc.dram_tensor("out_dram", (T, D), fp32, kind="ExternalOutput").ap()
    h4_rows = nc.dram_tensor("h4_rows", (T, D), fp32, kind="Internal").ap()
    expert_rows = nc.dram_tensor("expert_rows", (2 * T, D), fp32, kind="Internal").ap()
    two_blocks(nc, *args, out, h4_rows, expert_rows)
    r = run_bass_kernel_spmd(nc, [{f"{k}_in": a for k, a in arrays.items()}], core_ids=[0])
    return r.results[0]["out_dram"].reshape(1, T, D)
```
